# Optimizing a Trainium2 kernel written in Bass

```python
import math
import jax
import jax.numpy as jnp
from jax import lax
import numpy as np

'''Hybrid autoregressive decoder trunk (DEPTH layers). Each layer computes
  h = RMSNorm(x)
  x = x + W_out( sum_i sigmoid(G_i h) * P_i(branch_i(h)) )
      branch A: short gated conv  B * conv3(C * h_in)
      branch B: gated linear attention (GLA), chunked, low-rank forget gate
      branch C: S5 complex-diagonal state space (groups of 16 channels, 64 states), associative scan, GLU
      branch D: DSA sparse attention (lightning indexer -> top-k key gather), partial rotary
  x = x + CrossAttn(RMSNorm(x), RMSNorm(mem))   (4 heads over 256 memory tokens)
  x = x + HierMoE(RMSNorm(x))                    (top-1 expert group, then top-2 experts inside it)
and a final RMSNorm.
Inputs: x (BATCH, SEQ, D_MODEL) f32, mem (BATCH, 256, D_MODEL) f32, positions (BATCH, SEQ) int32,
plus per-layer parameters stacked on a leading DEPTH axis.
Output: (BATCH, SEQ, D_MODEL).
'''

D_MODEL = 1024
BATCH = 1
SEQ = 256
DEPTH = 2

MEM_LEN = 256
EPS = 1e-6
N_BRANCH = 4
BRANCH_W = 256
CONV_W = 3
GLA_HEADS = 4
GLA_DK = 64
GLA_DV = 64
GLA_RANK = 16
GLA_TAU = 16.0
GLA_CHUNK = 64
S5_GROUP = 16
S5_GROUPS = BRANCH_W // S5_GROUP
S5_STATE = 64
S5_DT_MIN = 1e-3
S5_DT_MAX = 1e-1
DSA_HEADS = 4
DSA_HEAD_DIM = 64
IDX_HEADS = 8
IDX_DIM = 32
DSA_TOPK = 256
Q_BLOCK = 128
ROPE_THETA = 500000.0
ROPE_FRAC = 4
X_HEADS = 4
X_HEAD_DIM = 128
N_GROUPS = 4
EXPERTS_PER_GROUP = 4
N_EXPERTS = N_GROUPS * EXPERTS_PER_GROUP
TOPK_IN_GROUP = 2
D_FF_EXPERT = 512

IN_SPLITS = (
    BRANCH_W, BRANCH_W, BRANCH_W,
    GLA_HEADS * GLA_DK, GLA_HEADS * GLA_DK, GLA_HEADS * GLA_DV,
    GLA_HEADS * GLA_DV, GLA_RANK,
    BRANCH_W,
    DSA_HEADS * DSA_HEAD_DIM, DSA_HEAD_DIM, DSA_HEAD_DIM,
    IDX_HEADS * IDX_DIM, IDX_DIM, IDX_HEADS,
    N_BRANCH * D_MODEL,
)
D_IN = sum(IN_SPLITS)
IN_OFFSETS = tuple(sum(IN_SPLITS[:i + 1]) for i in range(len(IN_SPLITS) - 1))

kernel_name = 'hybrid_gated_conv_gla_s5_dsa_hmoe'

def rmsnorm(x, g):
    xf = x.astype(jnp.float32)
    y = xf * lax.rsqrt(jnp.mean(xf * xf, axis=-1, keepdims=True) + EPS)
    return (y * g.astype(jnp.float32)).astype(x.dtype)

def rope_partial(t, positions):
    dh = t.shape[-1]
    rd = dh // ROPE_FRAC
    half = rd // 2
    inv_freq = ROPE_THETA ** (-jnp.arange(half, dtype=jnp.float32) * (2.0 / rd))
    ang = positions.astype(jnp.float32)[:, :, None] * inv_freq
    cos = jnp.cos(ang)[:, :, None, :]
    sin = jnp.sin(ang)[:, :, None, :]
    t1 = t[..., :half].astype(jnp.float32)
    t2 = t[..., half:rd].astype(jnp.float32)
    rot = jnp.concatenate([t1 * cos - t2 * sin, t2 * cos + t1 * sin], axis=-1).astype(t.dtype)
    return jnp.concatenate([rot, t[..., rd:]], axis=-1)

def short_conv_mixer(h_in, b_gate, c_gate, conv_w, conv_b):
    u = c_gate * h_in
    y = lax.conv_general_dilated(
        u, conv_w[:, None, :], window_strides=(1,), padding=[(CONV_W - 1, 0)],
        dimension_numbers=('NWC', 'WIO', 'NWC'), feature_group_count=u.shape[-1])
    return b_gate * (y + conv_b)

def gla_mixer(q, k, v, r, a_low, a_up, a_b, g_norm):
    B, S, _ = q.shape
    H, dk, dv, C = GLA_HEADS, GLA_DK, GLA_DV, GLA_CHUNK
    N = S // C
    f32 = jnp.float32
    log_a = jax.nn.log_sigmoid((a_low @ a_up).astype(f32) + a_b.astype(f32)) / GLA_TAU
    shp = lambda t, d: t.astype(f32).reshape(B, N, C, H, d)
    qc = shp(q, dk) * (dk ** -0.5)
    kc = shp(k, dk)
    vc = shp(v, dv)
    bcum = jnp.cumsum(shp(log_a, dk), axis=2)
    blast = bcum[:, :, -1:]
    q_dec = qc * jnp.exp(bcum)
    k_inv = kc * jnp.exp(-bcum)
    k_end = kc * jnp.exp(blast - bcum)
    causal = jnp.tril(jnp.ones((C, C), dtype=bool))
    att = jnp.einsum('bnihd,bnjhd->bnhij', q_dec, k_inv)
    att = jnp.where(causal, att, 0.0)
    o_intra = jnp.einsum('bnhij,bnjhe->bnihe', att, vc)

    def step(state, inp):
        qd, ke, vv, dec = inp
        o = jnp.einsum('bihd,bhde->bihe', qd, state)
        state = state * dec[..., None] + jnp.einsum('bjhd,bjhe->bhde', ke, vv)
        return state, o

    xs = (jnp.moveaxis(q_dec, 1, 0), jnp.moveaxis(k_end, 1, 0), jnp.moveaxis(vc, 1, 0),
          jnp.moveaxis(jnp.exp(blast[:, :, 0]), 1, 0))
    state0 = jnp.zeros((B, H, dk, dv), f32)
    _, o_inter = lax.scan(step, state0, xs)
    o = (o_intra + jnp.moveaxis(o_inter, 0, 1)).reshape(B, S, H, dv)
    o = o * lax.rsqrt(jnp.mean(o * o, axis=-1, keepdims=True) + EPS)
    o = o.reshape(B, S, H * dv) * g_norm.astype(f32) * jax.nn.silu(r.astype(f32))
    return o.astype(q.dtype)

def s5_mixer(u, lam_re, lam_im, log_dt, b_re, b_im, c_re, c_im, d_skip, w_glu, b_glu):
    B, S, _ = u.shape
    G, P = S5_GROUPS, S5_STATE
    f32 = jnp.float32
    uf = u.astype(f32).reshape(B, S, G, S5_GROUP)
    lam_re = lam_re.astype(f32)
    lam_im = lam_im.astype(f32)
    dt = jnp.exp(log_dt.astype(f32))[:, None]
    mag = jnp.exp(lam_re * dt)
    lb_re = mag * jnp.cos(lam_im * dt)
    lb_im = mag * jnp.sin(lam_im * dt)
    den = lam_re * lam_re + lam_im * lam_im
    f_re = ((lb_re - 1.0) * lam_re + lb_im * lam_im) / den
    f_im = (lb_im * lam_re - (lb_re - 1.0) * lam_im) / den
    b_re = b_re.astype(f32)
    b_im = b_im.astype(f32)
    bb_re = f_re[..., None] * b_re - f_im[..., None] * b_im
    bb_im = f_re[..., None] * b_im + f_im[..., None] * b_re
    bu_re = jnp.einsum('bsgc,gpc->bsgp', uf, bb_re)
    bu_im = jnp.einsum('bsgc,gpc->bsgp', uf, bb_im)
    a_re = jnp.broadcast_to(lb_re, bu_re.shape)
    a_im = jnp.broadcast_to(lb_im, bu_im.shape)

    def combine(e1, e2):
        a1r, a1i, b1r, b1i = e1
        a2r, a2i, b2r, b2i = e2
        return (a2r * a1r - a2i * a1i, a2r * a1i + a2i * a1r,
                a2r * b1r - a2i * b1i + b2r, a2r * b1i + a2i * b1r + b2i)

    _, _, x_re, x_im = lax.associative_scan(combine, (a_re, a_im, bu_re, bu_im), axis=1)
    y = (jnp.einsum('bsgp,gcp->bsgc', x_re, c_re.astype(f32))
         - jnp.einsum('bsgp,gcp->bsgc', x_im, c_im.astype(f32)))
    y = y.reshape(B, S, G * S5_GROUP) + d_skip.astype(f32) * uf.reshape(B, S, G * S5_GROUP)
    y = jax.nn.gelu(y)
    y = y * jax.nn.sigmoid(y @ w_glu.astype(f32) + b_glu.astype(f32))
    return y.astype(u.dtype)

def dsa_mixer(q, k, v, qi, ki, wi, positions):
    B, S, _ = q.shape
    f32 = jnp.float32
    q = rope_partial(q.reshape(B, S, DSA_HEADS, DSA_HEAD_DIM), positions)
    k = rope_partial(k[:, :, None, :], positions)[:, :, 0]
    qi = rope_partial(qi.reshape(B, S, IDX_HEADS, IDX_DIM), positions)
    ki = rope_partial(ki[:, :, None, :], positions)[:, :, 0]
    wi = wi * ((IDX_HEADS ** -0.5) * (IDX_DIM ** -0.5))
    topk = min(DSA_TOPK, S // 4)
    nb = S // Q_BLOCK
    ki32 = ki.astype(f32)

    def blockify(t):
        return jnp.moveaxis(t.reshape((B, nb, Q_BLOCK) + t.shape[2:]), 1, 0)

    def one_block(args):
        qb, qib, wib, start = args
        t_idx = start + jnp.arange(Q_BLOCK)
        iscore = jnp.einsum('bqhd,bsd->bqhs', qib.astype(f32), ki32)
        iscore = jnp.einsum('bqhs,bqh->bqs', jax.nn.relu(iscore), wib.astype(f32))
        causal = jnp.arange(S)[None, :] <= t_idx[:, None]
        iscore = jnp.where(causal[None], iscore, -jnp.inf)
        _, sel = lax.top_k(iscore, topk)
        valid = sel <= t_idx[None, :, None]
        k_sel = jax.vmap(lambda kk, ii: kk[ii])(k, sel)
        v_sel = jax.vmap(lambda vv, ii: vv[ii])(v, sel)
        logits = jnp.einsum('bqhd,bqkd->bqhk', qb.astype(f32), k_sel.astype(f32)) * (DSA_HEAD_DIM ** -0.5)
        logits = jnp.where(valid[:, :, None, :], logits, -jnp.inf)
        p = jax.nn.softmax(logits, axis=-1)
        o = jnp.einsum('bqhk,bqkd->bqhd', p, v_sel.astype(f32))
        return o.astype(qb.dtype)

    starts = jnp.arange(nb, dtype=jnp.int32) * Q_BLOCK
    out = lax.map(one_block, (blockify(q), blockify(qi), blockify(wi), starts))
    return jnp.moveaxis(out, 0, 1).reshape(B, S, DSA_HEADS * DSA_HEAD_DIM)

def mem_cross_attn(h, memn, w_q, w_kv, w_o):
    B, S, _ = h.shape
    M = memn.shape[1]
    q = (h @ w_q).reshape(B, S, X_HEADS, X_HEAD_DIM)
    k, v = jnp.split(memn @ w_kv, 2, axis=-1)
    k = k.reshape(B, M, X_HEADS, X_HEAD_DIM)
    v = v.reshape(B, M, X_HEADS, X_HEAD_DIM)
    logits = jnp.einsum('bshd,bmhd->bhsm', q, k).astype(jnp.float32) * (X_HEAD_DIM ** -0.5)
    p = jax.nn.softmax(logits, axis=-1).astype(v.dtype)
    o = jnp.einsum('bhsm,bmhd->bshd', p, v).reshape(B, S, X_HEADS * X_HEAD_DIM)
    return o @ w_o

def hier_moe(h, w_rg, b_rg, w_re, b_re, w_gate, w_up, w_down):
    B, S, _ = h.shape
    f32 = jnp.float32
    g_prob = jax.nn.softmax((h @ w_rg).astype(f32) + b_rg.astype(f32), axis=-1)
    p_g, g_sel = lax.top_k(g_prob, 1)
    g_onehot = jax.nn.one_hot(g_sel[..., 0], N_GROUPS, dtype=f32)
    e_logits = ((h @ w_re).astype(f32) + b_re.astype(f32)).reshape(B, S, N_GROUPS, EXPERTS_PER_GROUP)
    e_prob = jax.nn.softmax(jnp.einsum('bsge,bsg->bse', e_logits, g_onehot), axis=-1)
    top_p, top_i = lax.top_k(e_prob, TOPK_IN_GROUP)
    top_p = top_p / jnp.sum(top_p, axis=-1, keepdims=True)
    expert_id = g_sel * EXPERTS_PER_GROUP + top_i
    combine = jnp.einsum('bske,bsk->bse', jax.nn.one_hot(expert_id, N_EXPERTS, dtype=f32),
                         p_g * top_p).astype(h.dtype)
    out = jnp.zeros_like(h)
    for e in range(N_EXPERTS):
        he = jax.nn.silu(h @ w_gate[e]) * (h @ w_up[e])
        out = out + combine[..., e:e + 1] * (he @ w_down[e])
    return out

def setup_inputs(seed: int = 0) -> dict:
    key = jax.random.key(seed)
    ks = iter(jax.random.split(key, 48))
    f32 = jnp.float32
    L, D, W = DEPTH, D_MODEL, BRANCH_W
    G, P = S5_GROUPS, S5_STATE
    nrm = lambda shape, scale: jax.random.normal(next(ks), shape, f32) * scale
    gain = lambda shape: 1.0 + nrm(shape, 0.02)
    x = nrm((BATCH, SEQ, D), 1.0)
    mem = nrm((BATCH, MEM_LEN, D), 1.0)
    positions = (jax.random.randint(next(ks), (BATCH, 1), 0, 1024)
                 + jnp.arange(SEQ)[None, :]).astype(jnp.int32)
    n_idx = jnp.arange(P, dtype=f32)
    return {
        'x': x,
        'mem': mem,
        'positions': positions,
        'norm_mix': gain((L, D)),
        'w_in': nrm((L, D, D_IN), D ** -0.5),
        'conv_w': nrm((L, CONV_W, W), CONV_W ** -0.5),
        'conv_b': nrm((L, W), 0.02),
        'gla_a_up': nrm((L, GLA_RANK, GLA_HEADS * GLA_DK), GLA_RANK ** -0.5),
        'gla_a_b': nrm((L, GLA_HEADS * GLA_DK), 0.1),
        'gla_norm': gain((L, GLA_HEADS * GLA_DV)),
        's5_lambda_re': -0.5 + nrm((L, G, P), 0.01),
        's5_lambda_im': math.pi * n_idx + nrm((L, G, P), 0.01),
        's5_log_dt': jax.random.uniform(next(ks), (L, G), f32, math.log(S5_DT_MIN), math.log(S5_DT_MAX)),
        's5_b_re': nrm((L, G, P, S5_GROUP), (2.0 * S5_GROUP) ** -0.5),
        's5_b_im': nrm((L, G, P, S5_GROUP), (2.0 * S5_GROUP) ** -0.5),
        's5_c_re': nrm((L, G, S5_GROUP, P), (2.0 * P) ** -0.5),
        's5_c_im': nrm((L, G, S5_GROUP, P), (2.0 * P) ** -0.5),
        's5_d': nrm((L, W), 1.0),
        's5_w_glu': nrm((L, W, W), W ** -0.5),
        's5_b_glu': nrm((L, W), 0.02),
        'w_branch': nrm((L, N_BRANCH, W, D), W ** -0.5),
        'w_out': nrm((L, D, D), D ** -0.5),
        'norm_cross': gain((L, D)),
        'w_cq': nrm((L, D, X_HEADS * X_HEAD_DIM), D ** -0.5),
        'w_ckv': nrm((L, D, 2 * X_HEADS * X_HEAD_DIM), D ** -0.5),
        'w_co': nrm((L, X_HEADS * X_HEAD_DIM, D), (X_HEADS * X_HEAD_DIM) ** -0.5),
        'norm_ffn': gain((L, D)),
        'w_route_group': nrm((L, D, N_GROUPS), D ** -0.5),
        'b_route_group': nrm((L, N_GROUPS), 0.01),
        'w_route_expert': nrm((L, D, N_EXPERTS), D ** -0.5),
        'b_route_expert': nrm((L, N_EXPERTS), 0.01),
        'w_e_gate': nrm((L, N_EXPERTS, D, D_FF_EXPERT), D ** -0.5),
        'w_e_up': nrm((L, N_EXPERTS, D, D_FF_EXPERT), D ** -0.5),
        'w_e_down': nrm((L, N_EXPERTS, D_FF_EXPERT, D), D_FF_EXPERT ** -0.5),
        'norm_mem': gain((D,)),
        'norm_final': gain((D,)),
    }

def reference(x, mem, positions, norm_mix, w_in, conv_w, conv_b, gla_a_up, gla_a_b, gla_norm,
              s5_lambda_re, s5_lambda_im, s5_log_dt, s5_b_re, s5_b_im, s5_c_re, s5_c_im, s5_d,
              s5_w_glu, s5_b_glu, w_branch, w_out, norm_cross, w_cq, w_ckv, w_co, norm_ffn,
              w_route_group, b_route_group, w_route_expert, b_route_expert, w_e_gate, w_e_up,
              w_e_down, norm_mem, norm_final):
    memn = rmsnorm(mem, norm_mem)
    for l in range(DEPTH):
        h = rmsnorm(x, norm_mix[l])
        (c_h, c_b, c_c, g_q, g_k, g_v, g_r, g_a, s_u,
         d_q, d_k, d_v, i_q, i_k, i_w, gates) = jnp.split(h @ w_in[l], IN_OFFSETS, axis=-1)
        y_a = short_conv_mixer(c_h, c_b, c_c, conv_w[l], conv_b[l])
        y_b = gla_mixer(g_q, g_k, g_v, g_r, g_a, gla_a_up[l], gla_a_b[l], gla_norm[l])
        y_c = s5_mixer(s_u, s5_lambda_re[l], s5_lambda_im[l], s5_log_dt[l], s5_b_re[l], s5_b_im[l],
                       s5_c_re[l], s5_c_im[l], s5_d[l], s5_w_glu[l], s5_b_glu[l])
        y_d = dsa_mixer(d_q, d_k, d_v, i_q, i_k, i_w, positions)
        gate_parts = jnp.split(gates, N_BRANCH, axis=-1)
        branches = (y_a, y_b, y_c, y_d)
        merged = jnp.zeros_like(x)
        for i in range(N_BRANCH):
            merged = merged + jax.nn.sigmoid(gate_parts[i]) * (branches[i] @ w_branch[l, i])
        x = x + merged @ w_out[l]
        x = x + mem_cross_attn(rmsnorm(x, norm_cross[l]), memn, w_cq[l], w_ckv[l], w_co[l])
        x = x + hier_moe(rmsnorm(x, norm_ffn[l]), w_route_group[l], b_route_group[l],
                         w_route_expert[l], b_route_expert[l], w_e_gate[l], w_e_up[l], w_e_down[l])
    return rmsnorm(x, norm_final)


_drawn_inputs = setup_inputs


def setup_inputs(seed=0):
    import zlib

    import numpy as np

    out = dict(_drawn_inputs(seed))
    spreads = {}
    factors = {'gla_norm': 3.034,
     's5_lambda_re': 200.0,
     's5_c_re': 58.387,
     's5_b_glu': 12.293,
     'norm_cross': 3.289,
     'b_route_expert': 8.0,
     'norm_final': 25.495,
     's5_log_dt': 15.931,
     's5_b_re': 29.024,
     's5_c_im': 63.848,
     'b_route_group': 4.208,
     's5_lambda_im': 8.0,
     's5_b_im': 8.0}
    for name, (base, spread) in spreads.items():
        noise = np.random.default_rng([zlib.crc32(name.encode()), seed]).standard_normal(out[name].shape)
        drawn = base * np.exp(spread * noise) if base else spread * noise
        out[name] = jnp.asarray(drawn.astype(out[name].dtype))
    for name, factor in factors.items():
        out[name] = (out[name] * factor).astype(out[name].dtype)
    return out
```

```python
from contextlib import ExitStack

import numpy as np
import concourse.bass as bass
from concourse import mybir

ALU = mybir.AluOpType
ACT = mybir.ActivationFunctionType
F32 = mybir.dt.float32
I32 = mybir.dt.int32
AX = mybir.AxisListType.X

P = 128
D = 1024
S = 256
TB = S // P
KD = D // P
L = 2
EPS = 1e-6
W = 256
PI = float(np.pi)

C_H, C_B, C_C = 0, 256, 512
G_Q, G_K, G_V, G_R, G_A = 768, 1024, 1280, 1536, 1792
S_U, D_Q, D_K, D_V, I_Q, I_K, I_W, GATES = 1808, 2064, 2320, 2384, 2448, 2704, 2736, 2744

NS = 3
SLOT = KD * 512
N_EXP = 16
TOPK = 64
NEG = -1.0e30
TAKEN = -3.0e38

DENSE = ["m5", "m3", "m1", "m2", "m4", "m0", "g0", "g1", "g2", "g3", "ckv0", "ckv1", "br01",
         "g4", "g5", "g6", "g7", "br23", "wo0", "wo1", "cq", "co"]
MIX_COLS = {"m5": (D_K, GATES), "m3": (S_U, D_K), "m1": (C_C, G_K), "m2": (G_K, G_R),
            "m4": (G_R, S_U), "m0": (C_H, C_C)}
ND = len(DENSE)
NCH = ND + 3 * N_EXP

PER = dict(
    used=NCH,
    sumsq=6, meansq=3, root=3, h_ready=6, tp_mm=16, tp_v=8, tp_a=8, hg_ready=2,
    mix_mm=12, mix_ev=12, rope=1, sa_mm=3, sa_ev=3, la_mm=1, la_ev=1, ix_mm=8, ix_ev=8, ix_acc=8,
    ls_in=1, ls_ab=1, ls_ex=1, gla_cum=1, gla_exp=1, gla_qk=1, ketok_mm=1, ketok_ev=1, att_mm=2, att_ev=2,
    params=1, sp_in=1, sp_out=1, sp2_in=1, sp2_out=1, bt_mm=1, ct_mm=1, bc_ev=2, b2_ready=1,
    u_mm=1, st_ready=1, dl_mm=3, dl_ev=3, mx=2, ex=2, p_ready=1, pt_mm=3, pt_ev=3,
    o_mm=2, o_sq=2, o_ms=1, o_rt=1, o_done=1, sr=1, od_mm=1, od_ev=1, ybt_mm=1, ybt_ev=1,
    e_in=1, e_tab=1, bu_mm=8, bu_ev=8, zin=8, z_out=8, xs=8, yk=8, s5y=1, gelu=1, glu_mm=1, glu_ev=1, yc=1,
    u_conv=1, gate_mm=16, gate_ev=16, ckv_mm=4, ckv_ev=4, mg_mm=16, mg_ev=16, mg_add=16,
    wo_mm=4, wo_ev=4, cq_mm=2, cq_ev=2, cl_mm=4, cmx=1, cex=1, cp=1, cpt_mm=4, cpt_ev=4,
    co_mm=2, co_ev=2, cy_mm=4, cy_ev=4, rt_mm=1, rt_e1=1, rt_x1=1, comb=1,
    gu_mm=64, gu_sg=64, gu_ev=64, dn_mm=64, dn_ev=64, layer_done=1, par_ld=0,
)


def bc(ap, shape):
    return ap.broadcast_to(shape)


def trunk(nc, T, out):
    with ExitStack() as ctx:
        def sb(name, shape, dt=F32):
            return ctx.enter_context(nc.sbuf_tensor(name, shape, dt))

        sems = {}

        def sem(name):
            if name not in sems:
                sems[name] = ctx.enter_context(nc.semaphore(name))
            return sems[name]

        bank = [ctx.enter_context(nc.psum_tensor(f"bank{i}", [P, 512], F32)) for i in range(8)]

        ring = sb("ring", [P, NS, SLOT])
        x = sb("x", [P, TB, D])
        h = sb("h", [P, TB, D])
        hT = sb("hT", [P, KD, S])
        memT = sb("memT", [P, KD, S])
        gs = sb("gs", [P, TB, 2, D])
        kTx = sb("kTx", [P, 4, S])
        vx = sb("vx", [P, TB, 512])
        ident = sb("ident", [P, P])
        gla_mask = sb("gla_mask", [P, P])
        cneg = sb("cneg", [P, P])
        scan_keep = sb("scan_keep", [P, S])
        mask_b = sb("mask_b", [P, 2])
        mask_c = sb("mask_c", [P, 2])
        mc_i = sb("mc_i", [P, 1], I32)
        mc_j = sb("mc_j", [P, 1], I32)
        pos_i = sb("pos_i", [P, TB], I32)
        pos_f = sb("pos_f", [P, TB])
        invf = sb("invf", [P, 8])
        ang = sb("ang", [P, TB, 8])
        rr = sb("rr", [P, 4, 16])
        rope_cs = sb("rope_cs", [P, 2, TB, 8])
        junk = sb("junk", [P, 1])
        st = sb("st", [P, 4, TB])
        g_fm = sb("g_fm", [P, 4, KD])
        conv_w = sb("conv_w", [P, 3, 2])
        conv_b = sb("conv_b", [P, 2])
        a_up = sb("a_up", [16, W])
        a_b = sb("a_b", [P, 2])
        gla_g = sb("gla_g", [P, W])
        lam = sb("lam", [P, 3, 8])
        s5_b = sb("s5_b", [P, 2, 8, 16])
        s5_c = sb("s5_c", [P, 2, 2, 64])
        s5_d = sb("s5_d", [P, 2])
        b_glu = sb("b_glu", [P, 2])
        w_glu = sb("w_glu", [P, 2, W])
        b_rt = sb("b_rt", [P, 20])
        w_rt = sb("w_rt", [P, KD, 20])
        dt_ = sb("dtok", [P, TB, 424])
        dq = sb("dq", [P, TB, W])
        kk = sb("kk", [P, TB, 2, 64])
        ki4 = sb("ki4", [P, TB, 4, 32])
        rp = sb("rp", [P, 4, TB, 32])
        qTd = sb("qTd", [P, 2, S])
        kTd = sb("kTd", [P, 2, S])
        qiT = sb("qiT", [P, 2, S])
        rl = sb("rl", [P, 2, 512])
        state = rl[:].rearrange("p a b -> p (a b)")[:, 0:768].rearrange("p (n h e) -> p n h e", n=3, h=2)
        w16 = sb("w16", [P, TB, 8])
        isc = sb("isc", [P, 3, P])
        top8 = sb("top8", [P, 8])
        dl = sb("dl", [P, 3, 4 * P])
        dstat = sb("dstat", [P, 3, TB, 4])
        pT = sb("pT", [P, 3, 4, P])
        ydT = sb("ydT", [P, 2, S])
        gq = sb("gq", [P, 2, S])
        gk = sb("gk", [P, 2, S])
        gv = sb("gv", [P, TB, W])
        gr = sb("gr", [P, TB, W])
        alow = sb("alow", [16, S])
        za = sb("za", [P, 2, S])
        zb = sb("zb", [P, 2, S])
        eb = sb("eb", [P, 2, S])
        en = sb("en", [P, 2, S])
        ke = sb("ke", [P, 2, S])
        ketok = sb("ketok", [P, TB, W])
        attm = sb("attm", [P, TB, 4, P])
        ost = sb("ost", [P, 2, TB, 4])
        ybT = sb("ybT", [P, 2, S])
        cc = sb("cc", [P, 2, S])
        ch = sb("ch", [P, 2, S])
        cb = sb("cb", [P, 2, S])
        yaT = sb("yaT", [P, 2, S])
        uT = sb("uT", [P, 2, S])
        sp = sb("sp", [P, 20, 8])
        wpow = sb("wpow", [P, 2, 8])
        wtmp = sb("wtmp", [P, 4, 8])
        E = sb("E", [P, 2, 8, S])
        b2 = attm[:].rearrange("p a b c -> p (a b c)")[:, 0:512].rearrange("p (r t g c) -> p r t g c", r=2, t=8, g=2)
        c2 = attm[:].rearrange("p a b c -> p (a b c)")[:, 512:1024].rearrange("p (r h g s) -> p r h g s", r=2, h=2, g=2)
        bT = sb("bT", [P, 2, 2, P])
        cT = sb("cT", [P, 2, 2, P])
        gel = gk
        ycT = en
        hf = h[:].rearrange("p t n -> p (t n)")
        pq = hf[:, 0:1024].rearrange("p (q r s) -> p q r s", q=2, r=2)
        zi = hf[:, 1024:1536].rearrange("p (r s) -> p r s", r=2)
        zo = dl[:].rearrange("p a b -> p (a b)")[:, 0:512].rearrange("p (r s) -> p r s", r=2)
        xb = dl[:].rearrange("p a b -> p (a b)")[:, 512:1536].rearrange("p (q r s) -> p q r s", q=2, r=2)
        Ef = E[:].rearrange("p r t s -> p (r t s)")
        qTx = Ef[:, 0:1024].rearrange("p (h s) -> p h s", h=4)
        oTx = Ef[:, 1024:2048].rearrange("p (h s) -> p h s", h=4)
        px = Ef[:, 2048:4096].rearrange("p (t h m) -> p t h m", t=TB, h=4)
        pTx = gs[:].rearrange("p a b c -> p (a b c)")[:, 0:2048].rearrange("p (b h s) -> p b h s", b=2, h=4)
        cst = sb("cst", [P, 3, TB, 4])
        sg = Ef[:, 0:1024].rearrange("p (t s) -> p t s", t=4)
        heT = Ef[:, 1024:2048].rearrange("p (t s) -> p t s", t=4)
        pf = pT[:].rearrange("p a b c -> p (a b c)")
        rt = pf[:, 0:40].rearrange("p (t n) -> p t n", t=TB)
        rx = pf[:, 40:136].rearrange("p (i t n) -> p i t n", i=12, t=TB)
        rxx = pf[:, 136:168].rearrange("p (t g e) -> p t g e", t=TB, g=4)
        comb = pf[:, 168:200].rearrange("p (t g e) -> p t g e", t=TB, g=4)
        g_out = gs[:].rearrange("p a b c -> p (a b c)")[:, 0:D]
        produced = {}

        class Order:

            def __init__(self, eng, name):
                self.e, self.name, self.n, self.l, self.base = eng, name, 0, None, 0
                self.own = sem(name + "_steps")

            def link(self, ins):
                ins.then_inc(self.own, 1)
                self.n += 1
                self.e.wait_ge(self.own, self.base + self.n)
                if self.name in ("pool", "pe"):
                    self.settle()

            def enter(self, l, stride):
                self.l, self.before, self.stride = l, self.n, stride
                self.base, self.n = l * stride + self.n, 0

            def leave(self):
                assert self.n < self.stride, (self.name, self.n)
                self.e.sem_inc(self.own, self.stride - self.n)
                self.base, self.n, self.l = L * self.stride + self.before, 0, None

            def done(self, ins, name, times=1):
                ins.then_inc(sem(name), 1)
                produced[name] = produced.get(name, 0) + times

            def need(self, name, k):
                per = PER[name]
                l = self.l if self.l is not None else L
                self.e.wait_ge(sem(name), l * per + k)
                if self.name == "pool" or self.name == "sp":
                    self.settle()

            def settle(self):
                self.e.sem_inc(sem("settled"), 1)

        ld = [sem(f"loaded{s}") for s in range(NS)]
        slot_of = [i % NS for i in range(NCH)]
        e_slot = slot_of[ND:ND + 3]
        loads = [slot_of.count(s) for s in range(NS)]
        nth = [slot_of[:i].count(slot_of[i]) + 1 for i in range(NCH)]
        last_in = {}
        before = []
        for i in range(2 * NCH):
            s = slot_of[i % NCH]
            if i >= NCH:
                before.append(last_in[s] - NCH)
            last_in[s] = i

        w_in = T["w_in"]

        def chunk_src(name, l):
            def k_tiles(ap):
                return ap.rearrange("o (p k) n -> p (o k) n", p=P)
            one = bass.ds(l, 1)
            if name in MIX_COLS:
                a, b = MIX_COLS[name]
                return k_tiles(w_in[one, :, a:b]), KD, b - a
            if name[0] == "g":
                a = GATES + int(name[1:]) * 512
                return k_tiles(w_in[one, :, a:a + 512]), KD, 512
            if name.startswith("ckv"):
                a = int(name[3]) * 512
                return k_tiles(T["w_ckv"][one, :, a:a + 512]), KD, 512
            if name.startswith("br"):
                i = int(name[2])
                return T["w_branch"][one, i:i + 2].rearrange("o i (j p) n -> p (o i j) n", p=P), 4, D
            if name.startswith("wo"):
                a = int(name[2]) * 512
                return k_tiles(T["w_out"][one, :, a:a + 512]), KD, 512
            if name == "cq":
                return k_tiles(T["w_cq"][one]), KD, 512
            if name == "co":
                return T["w_co"][one].rearrange("o (h p) n -> p (o h) n", p=P), 4, D

        def slot(s, k, n):
            return ring[:, s, 0:k * n].rearrange("p (k n) -> p k n", n=n)

        block = ctx.enter_context(nc.Block())

        @block.sync
        def _(sp_):
            q = Order(sp_, "sp")
            sp_.dma_start(x[:], T["x"].rearrange("o (t p) n -> p (o t) n", p=P)).then_inc(sem("x_loaded"), 16)
            with sp_.Fori(0, L) as l:
                q.l = l
                for i, name in enumerate(DENSE):
                    q.need("used", before[i] + 1 + NS)
                    src, k, n = chunk_src(name, l)
                    sp_.dma_start(slot(slot_of[i], k, n), src).then_inc(ld[slot_of[i]], 16)
                with sp_.Fori(0, N_EXP) as e:
                    for j, (wt, kk_, nn) in enumerate((("w_e_gate", KD, 512), ("w_e_up", KD, 512), ("w_e_down", 4, D))):
                        sp_.wait_ge(sem("used"), l * NCH + e * 3 + (ND + j - NS + 1 + NS))
                        q.settle()
                        src = T[wt][bass.ds(l, 1), bass.ds(e, 1)].rearrange("o i (p k) n -> p (o i k) n", p=P)
                        sp_.dma_start(slot(e_slot[j], kk_, nn), src).then_inc(ld[e_slot[j]], 16)
            sp_.wait_ge(sem("out_ready"), 2)
            sp_.dma_start(out.rearrange("o (t p) n -> p (o t) n", p=P), h[:]).then_inc(sem("stored"), 16)
            sp_.wait_ge(sem("stored"), 16)

        @block.tensor
        def _(pe):
            q = Order(pe, "pe")
            mm = nc.tensor.matmul
            tr = nc.tensor.transpose

            def chunk(i):
                s = slot_of[i]
                pe.wait_ge(ld[s], q.l * (16 * loads[s]) + 16 * nth[i])
                return s

            def tokens_major(dst, src, w, nk):
                for k in range(nk):
                    ins = mm(dst, src(k), w(k), start=(k == 0), stop=(k == nk - 1))
                return ins

            def transposes(need_h):
                for t in range(TB):
                    need_h(t)
                    if t == 0:
                        continue
                    for j in range(4):
                        for k in (2 * j, 2 * j + 1):
                            for tb in range(TB):
                                ins = tr(bank[4 + j][:, (k % 2) * S + tb * P:(k % 2) * S + tb * P + P],
                                         h[:, tb, k::KD], ident[:])
                        q.done(ins, "tp_mm")

            pe.sem_inc(sem("used"), NS)
            pe.wait_ge(sem("ident_ready"), 1)
            for tb in range(TB):
                pe.wait_ge(sem("m_h_ready"), tb + 1)
            for j in range(4):
                for k in (2 * j, 2 * j + 1):
                    for tb in range(TB):
                        ins = tr(bank[4 + j][:, (k % 2) * S + tb * P:(k % 2) * S + tb * P + P],
                                 h[:, tb, k::KD], ident[:])
                ins.then_inc(sem("m_tp_mm"), 1)
            pe.wait_ge(sem("m_tp_v"), 4)

            with pe.Fori(0, L) as l:
                q.enter(l, 64)
                transposes(lambda t: q.need("h_ready", t + 1))
                q.need("tp_v", 2)
                q.need("tp_a", 2)

                def feature_major(dst, s, n, c0, m=P, src=hT):
                    w = slot(s, KD, n)
                    for k in range(KD):
                        ins = mm(dst, w[:, k, c0:c0 + m], src[:, k, :], start=(k == 0), stop=(k == KD - 1))
                    return ins

                def token_major(dst, s, n, c0, c1, tb, src=hT):
                    w = slot(s, KD, n)
                    for k in range(KD):
                        ins = mm(dst, src[:, k, tb * P:tb * P + P], w[:, k, c0:c1], start=(k == 0), stop=(k == KD - 1))
                    return ins

                s = chunk(0)
                for tb in range(TB):
                    q.done(token_major(bank[tb][:, 0:424], s, 424, 0, 424, tb), "mix_mm")
                pe.sem_inc(sem("used"), 1) if False else None
                mark = []

                def used(ins):
                    pass
                q.need("mix_mm", 2)
                q.done(pe, "used") if False else pe.sem_inc(sem("used"), 1)
                s = chunk(1)
                for j in range(2):
                    ins = feature_major(bank[2][:, j * S:j * S + S], s, 512, j * P)
                q.done(ins, "mix_mm")
                for tb in range(TB):
                    ins = token_major(bank[3][:, tb * W:tb * W + W], s, 512, 256, 512, tb)
                q.done(ins, "mix_mm")
                q.need("mix_mm", 4)
                pe.sem_inc(sem("used"), 1)
                s = chunk(2)
                for b in range(2):
                    for j in range(2):
                        ins = feature_major(bank[4 + b][:, j * S:j * S + S], s, 512, (2 * b + j) * P)
                    q.done(ins, "mix_mm")
                q.need("mix_mm", 6)
                pe.sem_inc(sem("used"), 1)
                s = chunk(3)
                for j in range(2):
                    ins = feature_major(bank[6][:, j * S:j * S + S], s, 512, j * P)
                q.done(ins, "mix_mm")
                for tb in range(TB):
                    ins = token_major(bank[7][:, tb * W:tb * W + W], s, 512, 256, 512, tb)
                q.done(ins, "mix_mm")
                q.need("mix_mm", 8)
                pe.sem_inc(sem("used"), 1)
                s = chunk(4)
                q.need("mix_ev", 1)
                for tb in range(TB):
                    ins = token_major(bank[0][:, tb * W:tb * W + W], s, 272, 0, 256, tb)
                q.done(ins, "mix_mm")
                q.need("mix_ev", 2)
                q.done(feature_major(bank[1][0:16, 0:S], s, 272, 256, m=16), "mix_mm")
                q.need("mix_mm", 10)
                pe.sem_inc(sem("used"), 1)
                s = chunk(5)
                for b in range(2):
                    q.need("mix_ev", 3 + b)
                    for j in range(2):
                        ins = feature_major(bank[2 + b][:, j * S:j * S + S], s, 512, (2 * b + j) * P)
                    q.done(ins, "mix_mm")
                q.need("mix_mm", 12)
                pe.sem_inc(sem("used"), 1)

                def gates(g):
                    s = chunk(DENSE.index(f"g{g}"))
                    for tb in range(TB):
                        b = 2 * (g % 2) + tb
                        if g in (0, 1):
                            q.need("mix_ev", 9 + b)
                        elif g == 4:
                            q.need("mg_ev", 8)
                        elif g != 5:
                            q.need("gate_ev", 2 * (g - 2) + tb + 1)
                        q.done(token_major(bank[b][:], s, 512, 0, 512, tb), "gate_mm")
                    q.need("gate_mm", 2 * g + 2)
                    pe.sem_inc(sem("used"), 1)

                q.need("rope", 1)
                q.need("mix_ev", 7)
                for hp in range(2):
                    for tb in range(TB):
                        ins = tr(bank[4][:, hp * S + tb * P:hp * S + tb * P + P], dq[:, tb, hp * P:hp * P + P], ident[:])
                q.done(ins, "sa_mm")
                for tb in range(TB):
                    tr(bank[5][:, tb * P:tb * P + P], kk[:, tb].rearrange("p a b -> p (a b)"), ident[:])
                for tb in range(TB):
                    ins = tr(bank[5][:, S + tb * P:S + tb * P + P], ki4[:, tb].rearrange("p a b -> p (a b)"), ident[:])
                q.done(ins, "sa_mm")
                for hp in range(2):
                    for tb in range(TB):
                        ins = tr(bank[6][:, hp * S + tb * P:hp * S + tb * P + P],
                                 dt_[:, tb, 128 + hp * P:128 + hp * P + P], ident[:])
                q.done(ins, "sa_mm")
                q.need("mix_ev", 10)
                for j in range(2):
                    ins = mm(bank[7][:, j * S:j * S + S], a_up[:, j * P:j * P + P], alow[:, :], start=True, stop=True)
                q.done(ins, "la_mm")
                gates(0)
                q.need("sa_ev", 3)
                q.need("la_ev", 1)
                for hq in range(8):
                    r = 32 * (hq % 4)
                    ins = mm(bank[4 + hq % 4][:, (hq // 4) * S:(hq // 4) * S + S], qiT[r:r + 32, hq // 4, P:2 * P],
                             kTd[r:r + 32, 1, :], start=True, stop=True)
                    if hq >= 4:
                        q.done(ins, "ix_mm")
                for hq in range(8):
                    r = 32 * (hq % 4)
                    if hq < 4:
                        q.need("ix_ev", 1 + hq)
                    ins = mm(bank[4 + hq % 4][:, (hq // 4) * P:(hq // 4) * P + P], qiT[r:r + 32, hq // 4, 0:P],
                             kTd[r:r + 32, 1, 0:P], start=True, stop=True)
                    if hq >= 4:
                        q.done(ins, "ix_mm")
                gates(1)
                q.need("b2_ready", 1)
                q.need("ix_ev", 8)
                for ri in range(2):
                    for hf_ in range(2):
                        ins = tr(bank[7][:, (ri * 2 + hf_) * P:(ri * 2 + hf_) * P + P],
                                 b2[:, ri, 4 * hf_:4 * hf_ + 4].rearrange("p t g c -> p (t g c)"), ident[:])
                q.done(ins, "bt_mm")
                for ri in range(2):
                    for hf_ in range(2):
                        ins = tr(bank[6][:, (ri * 2 + hf_) * P:(ri * 2 + hf_) * P + P],
                                 c2[:, ri, hf_].rearrange("p g s -> p (g s)"), ident[:])
                q.done(ins, "ct_mm")
                q.need("gla_qk", 1)
                q.need("ix_ev", 8)
                for odd in range(2):
                    r = 64 * odd
                    for tb in range(TB):
                        c = slice(tb * P, tb * P + P)
                        for hd in (odd, odd + 2):
                            ins = mm(bank[4 + tb][:, hd * P:hd * P + P], en[r:r + 64, hd // 2, c],
                                     gq[r:r + 64, hd // 2, c], start=True, stop=True)
                        if odd:
                            q.done(ins, "att_mm")
                    if not odd:
                        q.link(ins)
                gates(2)
                q.need("bc_ev", 2)
                for tb in range(TB):
                    for j in range(2):
                        ins = tr(bank[6][:, tb * W + j * P:tb * W + j * P + P], ke[:, j, tb * P:tb * P + P], ident[:])
                q.done(ins, "ketok_mm")
                q.need("ketok_ev", 1)
                q.need("att_ev", 2)
                for odd in range(2):
                    r = 64 * odd
                    for hd in (odd, odd + 2):
                        ins = mm(bank[5][:, hd * P:hd * P + P], qTd[r:r + 64, hd // 2, 0:P], kTd[r:r + 64, 0, 0:P],
                                 start=True, stop=True)
                    if odd:
                        q.done(ins, "dl_mm")
                    for hd in (odd, odd + 2):
                        ins = mm(bank[6 + hd // 2][:, odd * S:odd * S + S], qTd[r:r + 64, hd // 2, P:2 * P],
                                 kTd[r:r + 64, 0, :], start=True, stop=True)
                        if odd:
                            q.done(ins, "dl_mm")
                    if not odd:
                        q.link(ins)
                for n in (0, 2, 1):
                    if n == 1:
                        q.link(ins)
                    r = 64 * (n % 2)
                    for hd in range(4):
                        ins = mm(bank[4][64 * (hd % 2):64 * (hd % 2) + 64, n * P + (hd // 2) * 64:n * P + (hd // 2) * 64 + 64],
                                 ketok[r:r + 64, n // 2, hd * 64:hd * 64 + 64], gv[r:r + 64, n // 2, hd * 64:hd * 64 + 64],
                                 start=True, stop=True)
                q.done(ins, "u_mm")
                gates(3)
                q.need("st_ready", 1)
                q.need("dl_ev", 1)
                for tb in range(TB):
                    for hd in range(4):
                        c = slice(hd * 64, hd * 64 + 64)
                        mm(bank[4 + tb][:, c], attm[:, tb, hd, :], gv[:, tb, c], start=(hd == 0), stop=False,
                           skip_group_check=True)
                    for half in range(2):
                        n = 2 * tb + half
                        if n == 0:
                            continue
                        for hp in range(2):
                            ins = mm(bank[4 + tb][64 * half:64 * half + 64, hp * P:hp * P + P],
                                     gq[:, hp, n * 64:n * 64 + 64], state[:, n - 1, hp, :],
                                     start=False, stop=(half == 1 and hp == 1), skip_group_check=True)
                    q.done(ins, "o_mm")
                q.need("p_ready", 1)
                q.need("dl_ev", 3)
                for u, b in ((0, 6), (1, 7), (2, 4)):
                    if b == 4:
                        q.need("o_done", 1)
                    for hd in range(4):
                        src = dl[:, 0, hd * P:hd * P + P] if u == 0 else \
                            dl[:, 1:3].rearrange("p a (g s) -> p (a g) s", s=S)[:, hd, (u - 1) * P:u * P]
                        ins = tr(bank[b][:, hd * P:hd * P + P], src, ident[:])
                    q.done(ins, "pt_mm")
                q.need("pt_ev", 3)
                for hd in range(4):
                    r = 64 * (hd % 2)
                    c = (hd // 2) * S
                    mm(bank[5][r:r + 64, c:c + P], dt_[:, 0, 64:128], pT[:, 0, hd, :], start=True, stop=True)
                    mm(bank[5][r:r + 64, c + P:c + S], dt_[:, 0, 64:128], pT[:, 1, hd, :], start=True, stop=False)
                    ins = mm(bank[5][r:r + 64, c + P:c + S], dt_[:, 1, 64:128], pT[:, 2, hd, :], start=False, stop=True)
                q.done(ins, "od_mm")
                for j in range(2):
                    for tb in range(TB):
                        ins = tr(bank[6][:, j * S + tb * P:j * S + tb * P + P], za[:, tb, j * P:j * P + P], ident[:])
                q.done(ins, "ybt_mm")

                def cross_keys():
                    s = chunk(DENSE.index("ckv0"))
                    for b in range(2):
                        q.need("gate_ev", 5 + b)
                        for j in range(2):
                            ins = feature_major(bank[b][:, j * S:j * S + S], s, 512, (2 * b + j) * P, src=memT)
                        q.done(ins, "ckv_mm")
                    q.need("ckv_mm", 2)
                    pe.sem_inc(sem("used"), 1)

                def cross_values():
                    s = chunk(DENSE.index("ckv1"))
                    for tb in range(TB):
                        q.need("gate_ev", 7 + tb)
                        q.done(token_major(bank[2 + tb][:], s, 512, 0, 512, tb, src=memT), "ckv_mm")
                    q.need("ckv_mm", 4)
                    pe.sem_inc(sem("used"), 1)

                def drive(t):
                    b = (4, 7)[t % 2]
                    r = 32 * (t % 4)
                    if t >= 2:
                        q.need("bu_ev", t - 1)
                    for ri in range(2):
                        ins = mm(bank[b][:, ri * S:ri * S + S], bT[r:r + 32, ri, t // 4, :], uT[r:r + 32, t // 4, :],
                                 start=True, stop=True)
                    q.done(ins, "bu_mm")

                def read_out(t):
                    r = 32 * (t % 4)
                    q.need("xs", t + 1)
                    if t == 0:
                        q.need("od_ev", 1)
                    for ri in range(2):
                        ins = mm(bank[5][r:r + 32, (t // 4) * S:(t // 4) * S + S], cT[:, ri, t // 4, r:r + 32],
                                 xb[:, t % 2, ri, :], start=(ri == 0), stop=(ri == 1))
                    q.done(ins, "yk")

                for t in range(8):
                    drive(t)
                    if t >= 1:
                        read_out(t - 1)
                    if t == 2:
                        cross_keys()
                    if t == 4:
                        cross_values()
                read_out(7)
                q.need("gelu", 1)
                q.need("ybt_ev", 1)
                for j in range(2):
                    for k in range(2):
                        ins = mm(bank[6][:, j * S:j * S + S], w_glu[:, k, j * P:j * P + P], gel[:, k, :],
                                 start=(k == 0), stop=(k == 1))
                q.done(ins, "glu_mm")

                def merge(i):
                    src = (yaT, ybT, ycT, ydT)[i]
                    s = slot_of[DENSE.index("br01" if i < 2 else "br23")]
                    w = slot(s, 4, D)
                    for tb in range(TB):
                        for nh in range(2):
                            n = i * 4 + tb * 2 + nh
                            if n < 4:
                                q.need("ckv_ev", n + 1)
                            elif i == 2:
                                q.need("gate_ev", 13 + tb * 2 + nh)
                            else:
                                q.need("mg_ev", n - 3)
                            for j in range(2):
                                ins = mm(bank[n % 4][:], src[:, j, tb * P:tb * P + P],
                                         w[:, (i % 2) * 2 + j, nh * 512:nh * 512 + 512], start=(j == 0), stop=(j == 1))
                            q.done(ins, "mg_mm")
                    if i % 2:
                        q.need("mg_mm", i * 4 + 4)
                        pe.sem_inc(sem("used"), 1)

                chunk(DENSE.index("br01"))
                q.need("u_conv", 1)
                merge(0)
                merge(1)
                for g in range(4, 8):
                    gates(g)
                chunk(DENSE.index("br23"))
                q.need("yc", 1)
                merge(2)
                merge(3)
                q.need("glu_ev", 2) if False else None
                q.need("mg_add", 16)
                transposes(lambda t: None)
                q.need("tp_v", 4)
                q.need("tp_a", 4)
                for nh in range(2):
                    i = DENSE.index(f"wo{nh}")
                    s = chunk(i)
                    for tb in range(TB):
                        if nh == 0:
                            q.need("mg_ev", 13 + tb)
                        else:
                            q.need("mg_ev", 15 + tb)
                        q.done(token_major(bank[2 * nh + tb][:], s, 512, 0, 512, tb), "wo_mm")
                    q.need("wo_mm", 2 * nh + 2)
                    pe.sem_inc(sem("used"), 1)

                transposes(lambda t: q.need("h_ready", 3 + t))
                q.need("tp_v", 6)
                q.need("tp_a", 6)
                s = chunk(DENSE.index("cq"))
                for b in range(2):
                    for j in range(2):
                        ins = feature_major(bank[b][:, j * S:j * S + S], s, 512, (2 * b + j) * P)
                    q.done(ins, "cq_mm")
                q.need("cq_mm", 2)
                pe.sem_inc(sem("used"), 1)
                q.need("cq_ev", 2)
                for tb in range(TB):
                    for hd in range(4):
                        ins = mm(bank[4 + 2 * tb + hd // 2][:, (hd % 2) * S:(hd % 2) * S + S],
                                 qTx[:, hd, tb * P:tb * P + P], kTx[:, hd, :], start=True, stop=True)
                        if hd % 2:
                            q.done(ins, "cl_mm")
                q.need("cp", 1)
                for mb in range(2):
                    for hp in range(2):
                        for hd in (2 * hp, 2 * hp + 1):
                            for tb in range(TB):
                                ins = tr(bank[mb * 2 + hp][:, (hd % 2) * S + tb * P:(hd % 2) * S + tb * P + P],
                                         px[:, tb, hd, mb * P:mb * P + P], ident[:])
                        q.done(ins, "cpt_mm")
                q.need("cpt_ev", 4)
                for hp in range(2):
                    for hd in (2 * hp, 2 * hp + 1):
                        for mb in range(2):
                            ins = mm(bank[4 + hp][:, (hd % 2) * S:(hd % 2) * S + S], vx[:, mb, hd * P:hd * P + P],
                                     pTx[:, mb, hd, :], start=(mb == 0), stop=(mb == 1))
                    q.done(ins, "co_mm")
                q.need("co_ev", 2)
                s = chunk(DENSE.index("co"))
                w = slot(s, 4, D)
                for tb in range(TB):
                    for nh in range(2):
                        for hd in range(4):
                            ins = mm(bank[tb * 2 + nh][:], oTx[:, hd, tb * P:tb * P + P],
                                     w[:, hd, nh * 512:nh * 512 + 512], start=(hd == 0), stop=(hd == 3))
                        q.done(ins, "cy_mm")
                q.need("cy_mm", 4)
                pe.sem_inc(sem("used"), 1)

                transposes(lambda t: q.need("h_ready", 5 + t))
                q.need("tp_v", 8)
                q.need("tp_a", 8)
                for tb in range(TB):
                    for k in range(KD):
                        ins = mm(bank[0][:, tb * 20:tb * 20 + 20], hT[:, k, tb * P:tb * P + P], w_rt[:, k, :],
                                 start=(k == 0), stop=(k == KD - 1))
                q.done(ins, "rt_mm")
                q.need("rt_e1", 1)
                q.settle()
                with pe.Fori(0, N_EXP) as e:
                    for j in range(2):
                        pe.wait_ge(ld[e_slot[j]], l * (16 * loads[e_slot[j]]) + e * 16 + 16 * nth[ND + j])
                        w = slot(e_slot[j], KD, 512)
                        for ft in range(4):
                            if j == 0:
                                pe.wait_ge(sem("gu_ev"), l * 64 + e * 4 + ft + 1)
                            for k in range(KD):
                                ins = mm(bank[ft][:, j * S:j * S + S], w[:, k, ft::4], hT[:, k, :],
                                         start=(k == 0), stop=(k == KD - 1))
                            if j == 1:
                                ins.then_inc(sem("gu_mm"), 1)
                        if j == 0:
                            ins.then_inc(sem("used"), 1)
                    pe.wait_ge(sem("gu_mm"), l * 64 + e * 4 + 4)
                    pe.sem_inc(sem("used"), 1)
                    pe.wait_ge(ld[e_slot[2]], l * (16 * loads[e_slot[2]]) + e * 16 + 16 * nth[ND + 2])
                    w = slot(e_slot[2], 4, D)
                    pe.wait_ge(sem("he_ready"), l * 64 + e * 4 + 4)
                    for tb in range(TB):
                        for nh in range(2):
                            b = tb * 2 + nh
                            pe.wait_ge(sem("dn_ev"), l * 64 + e * 4 + b + 1)
                            for ft in range(4):
                                ins = mm(bank[4 + b][:], heT[:, ft, tb * P:tb * P + P], w[:, ft, nh * 512:nh * 512 + 512],
                                         start=(ft == 0), stop=(ft == 3))
                            ins.then_inc(sem("dn_mm"), 1)
                    pe.wait_ge(sem("dn_mm"), l * 64 + e * 4 + 4)
                    pe.sem_inc(sem("used"), 1)
                q.leave()

        @block.scalar
        def _(act):
            q = Order(act, "act")
            A = nc.scalar.activation

            def copy(dst, src, **kw):
                return A(dst, src, ACT.Copy, **kw)

            act.wait_ge(sem("mem_loaded"), 16)
            for tb in range(TB):
                A(kTx[:].rearrange("p a b -> p (a b)"), h[:, tb, :], ACT.Square,
                  accum_out=st[:, 0, tb:tb + 1]).then_inc(sem("m_sumsq"), 1)
                act.wait_ge(sem("m_sumsq"), tb + 1)
            act.wait_ge(sem("m_meansq"), 1)
            A(st[:, 2, :], st[:, 1, :], ACT.Sqrt).then_inc(sem("m_root"), 1)
            act.wait_ge(sem("ang_ready"), 1)
            A(rope_cs[:, 1].rearrange("p t f -> p (t f)"), rr[:, 0, :], ACT.Sin).then_inc(sem("rope_ready"), 1)
            A(rope_cs[:, 0].rearrange("p t f -> p (t f)"), rr[:, 1, :], ACT.Sin).then_inc(sem("rope_ready"), 1)
            act.wait_ge(sem("x_loaded"), 16)
            act.wait_ge(sem("m_tp_v"), 4)

            def norm_stats(u):
                for tb in range(TB):
                    q.done(A(kTx_junk(u), x[:, tb, :], ACT.Square, accum_out=st[:, 0, tb:tb + 1]), "sumsq")
                    q.need("sumsq", 2 * u + tb + 1)
                q.need("meansq", u + 1)
                q.done(A(st[:, 2, :], st[:, 1, :], ACT.Sqrt), "root")

            def kTx_junk(u):
                return h[:, 1, :]

            def norm_evacuate(u, g):
                for j in (1, 3):
                    q.need("tp_mm", 4 * u + j + 1)
                    for i in range(2):
                        k = 2 * j + i
                        ins = A(hT[:, k, :], bank[4 + j][:, i * S:i * S + S], ACT.Copy, scale=g_fm[:, g, k:k + 1])
                    q.done(ins, "tp_a")

            with act.Fori(0, L) as l:
                q.enter(l, 256)
                norm_stats(0)
                act.wait_ge(sem("par_loaded"), l * N_PAR * 16 + N_PAR * 16)
                q.link(A(sp[:, 0, :], lam[:, 2, :], ACT.Exp))
                q.done(A(junk[:], junk[:], ACT.Copy), "sp_in")
                q.need("sp2_in", 1)
                A(sp[:, 2, :], sp[:, 1, :], ACT.Exp)
                A(sp[:, 8, :], sp[:, 6, :], ACT.Sin)
                q.done(A(sp[:, 9, :], sp[:, 7, :], ACT.Sin), "sp2_out")
                norm_evacuate(0, 0)
                flat = lambda t: t[:].rearrange("p a b -> p (a b)")
                q.need("mix_mm", 1)
                q.done(copy(dt_[:, 0, :], bank[0][:, 0:424]), "mix_ev")
                q.need("mix_mm", 2)
                q.done(copy(dt_[:, 1, :], bank[1][:, 0:424]), "mix_ev")
                for n, (dst, b) in enumerate(((uT, 2), (dq, 3), (cc, 4), (gq, 5), (gk, 6), (gv, 7), (gr, 0))):
                    q.need("mix_mm", n + 3)
                    q.done(copy(flat(dst), bank[b][:]), "mix_ev")
                q.need("mix_mm", 10)
                q.done(copy(alow[:, :], bank[1][0:16, 0:S]), "mix_ev")
                for n, (dst, b) in enumerate(((ch, 2), (cb, 3))):
                    q.need("mix_mm", n + 11)
                    q.done(copy(flat(dst), bank[b][:]), "mix_ev")
                for n, (dst, b) in enumerate(((qTd, 4), (kTd, 5), (qiT, 6))):
                    q.need("sa_mm", n + 1)
                    q.done(copy(flat(dst), bank[b][:]), "sa_ev")

                def gate(g):
                    i = (g // 2) % 2
                    for tb in range(TB):
                        q.need("gate_mm", 2 * g + tb + 1)
                        if g == 4 and tb == 0:
                            q.need("mg_add", 8)
                        q.done(A(gs[:, tb, i, (g % 2) * 512:(g % 2) * 512 + 512], bank[2 * (g % 2) + tb][:], ACT.Sigmoid), "gate_ev")

                q.need("mix_ev", 9)
                q.done(A(flat(gr), flat(gr), ACT.Silu), "sr")
                q.need("ls_in", 1)
                q.link(A(flat(zb), flat(za), ACT.Abs))
                q.link(A(flat(zb), flat(zb), ACT.Exp, scale=-1.0))
                q.done(A(flat(zb), flat(zb), ACT.Ln, bias=1.0), "ls_ex")
                gate(0)
                for n in range(8):
                    q.need("ix_mm", n + 1)
                    if n >= 2:
                        q.need("ix_acc", n - 1)
                    c = slice(0, 2 * S if n < 4 else 2 * P)
                    q.done(A(rl[:, n % 2, c], bank[4 + n % 4][:, c], ACT.Relu), "ix_ev")
                gate(1)
                q.need("gla_cum", 1)
                A(flat(eb), flat(za), ACT.Exp, scale=1.0 / 16)
                A(flat(en), flat(za), ACT.Exp, scale=-1.0 / 16)
                q.done(A(flat(ke), flat(zb), ACT.Exp, scale=1.0 / 16), "gla_exp")
                q.need("bt_mm", 1)
                q.done(copy(bT[:].rearrange("p a b c -> p (a b c)"), bank[7][:]), "bc_ev")
                q.need("ct_mm", 1)
                q.done(copy(cT[:].rearrange("p a b c -> p (a b c)"), bank[6][:]), "bc_ev")
                gate(2)
                q.need("ketok_mm", 1)
                q.done(copy(flat(ketok), bank[6][:]), "ketok_ev")
                gate(3)
                for tb in range(TB):
                    q.need("mx", tb + 1)
                    for hd in range(4):
                        v = dl[:, 0, hd * P:hd * P + P] if tb == 0 else \
                            dl[:, 1:3].rearrange("p a (g s) -> p (a g) s", s=S)[:, hd, :]
                        ins = A(v, v, ACT.Exp, bias=dstat[:, 0, tb, hd:hd + 1], accum_out=dstat[:, 1, tb, hd:hd + 1])
                    q.done(ins, "ex")
                for tb in range(TB):
                    q.need("o_mm", tb + 1)
                    q.done(A(zb[:, tb, :], bank[4 + tb][:, 0:W], ACT.Square), "o_sq")
                q.need("o_ms", 1)
                q.done(A(ost[:, 1].rearrange("p a b -> p (a b)"), ost[:, 0].rearrange("p a b -> p (a b)"), ACT.Sqrt), "o_rt")
                for u, b in ((0, 6), (1, 7), (2, 4)):
                    q.need("pt_mm", u + 1)
                    q.done(copy(pT[:, u].rearrange("p a b -> p (a b)"), bank[b][:]), "pt_ev")
                q.need("od_mm", 1)
                q.done(copy(flat(ydT), bank[5][:]), "od_ev")
                q.need("ybt_mm", 1)
                q.done(copy(flat(ybT), bank[6][:]), "ybt_ev")
                for b in range(2):
                    q.need("ckv_mm", b + 1)
                    q.done(copy(kTx[:, 2 * b:2 * b + 2, :].rearrange("p a b -> p (a b)"), bank[b][:]), "ckv_ev")
                for b in range(2):
                    q.need("ckv_mm", b + 3)
                    q.done(copy(vx[:, b, :], bank[2 + b][:]), "ckv_ev")
                q.need("s5y", 1)
                q.done(A(flat(gel), flat(gel), ACT.Gelu_apprx_tanh), "gelu")
                q.need("glu_mm", 1)
                for j in range(2):
                    ins = A(ycT[:, j, :], bank[6][:, j * S:j * S + S], ACT.Sigmoid, bias=b_glu[:, j:j + 1])
                q.done(ins, "glu_ev")
                for g in range(4, 8):
                    gate(g)
                for j in (1, 3):
                    q.need("tp_mm", 4 + j + 1)
                    q.done(copy(hT[:, 2 * j:2 * j + 2, :].rearrange("p a b -> p (a b)"), bank[4 + j][:]), "tp_a")
                q.need("wo_ev", 4)
                norm_stats(1)
                norm_evacuate(2, 1)
                for b in range(2):
                    q.need("cq_mm", b + 1)
                    q.done(copy(qTx[:, 2 * b:2 * b + 2, :].rearrange("p a b -> p (a b)"), bank[b][:]), "cq_ev")
                q.need("cmx", 1)
                for tb in range(TB):
                    for hd in range(4):
                        ins = A(px[:, tb, hd, :], bank[4 + 2 * tb + hd // 2][:, (hd % 2) * S:(hd % 2) * S + S], ACT.Exp,
                                bias=cst[:, 0, tb, hd:hd + 1], scale=128 ** -0.5, accum_out=cst[:, 1, tb, hd:hd + 1])
                q.done(ins, "cex")
                for n in (1, 3):
                    q.need("cpt_mm", n + 1)
                    q.done(copy(pTx[:, n // 2, 2:4, :].rearrange("p a b -> p (a b)"), bank[n][:]), "cpt_a")
                for hp in range(2):
                    q.need("co_mm", hp + 1)
                    q.done(copy(oTx[:, 2 * hp:2 * hp + 2, :].rearrange("p a b -> p (a b)"), bank[4 + hp][:]), "co_ev")
                q.need("cy_ev", 4)
                norm_stats(2)
                norm_evacuate(3, 2)
                q.need("rt_x1", 1)
                A(rx[:, 2].rearrange("p a b -> p (a b)"), rx[:, 1].rearrange("p a b -> p (a b)"), ACT.Exp)
                q.done(A(rx[:, 7].rearrange("p a b -> p (a b)"), rx[:, 6].rearrange("p a b -> p (a b)"), ACT.Exp), "rt_x2")
                with act.Fori(0, N_EXP) as e:
                    for ft in range(4):
                        act.wait_ge(sem("gu_mm"), l * 64 + e * 4 + ft + 1)
                        act.wait_ge(sem("gu_ev"), l * 64 + e * 4 + ft + 1)
                        A(sg[:, ft, :], bank[ft][:, 0:S], ACT.Silu).then_inc(sem("gu_sg"), 1)
                act.wait_ge(sem("dn_ev"), l * 64 + 64 + 4)
                q.leave()
            for tb in range(TB):
                A(h[:, tb, :], x[:, tb, :], ACT.Square, accum_out=st[:, 0, tb:tb + 1]).then_inc(sem("f_sumsq"), 1)
            act.wait_ge(sem("f_meansq"), 1)
            A(st[:, 2, :], st[:, 1, :], ACT.Sqrt).then_inc(sem("f_root"), 1)

        @block.gpsimd
        def _(pool):
            q = Order(pool, "pool")
            g = nc.gpsimd

            def load(dst, src, name):
                pool.dma_start(dst, src, allow_slow_non_contiguous=True).then_inc(sem(name), 16)

            load(h[:], T["mem"].rearrange("o (t p) n -> p (o t) n", p=P), "mem_loaded")
            load(pos_i[:], T["positions"].rearrange("o (t p) -> p (o t)", p=P), "pos_loaded")
            load(g_fm[:, 3, :], T["norm_mem"].rearrange("(p k) -> p k", p=P), "gm_loaded")
            q.link(g.memset(ident[:], 0.0))
            g.affine_select(out=ident[:], in_=ident[:], compare_op=ALU.not_equal, fill=1.0, base=0,
                            pattern=[[-1, P]], channel_multiplier=1).then_inc(sem("ident_ready"), 1)
            q.link(g.memset(gla_mask[:], 1.0))
            q.link(g.affine_select(out=gla_mask[:], in_=gla_mask[:], compare_op=ALU.is_ge, fill=0.0, base=0,
                                   pattern=[[1, P]], channel_multiplier=-1))
            q.link(g.affine_select(out=gla_mask[:, 64:128], in_=gla_mask[:, 64:128], compare_op=ALU.is_ge, fill=0.0,
                                   base=-64, pattern=[[0, 64]], channel_multiplier=1))
            q.link(g.memset(cneg[:], 0.0))
            q.link(g.affine_select(out=cneg[:], in_=cneg[:], compare_op=ALU.is_ge, fill=NEG, base=0,
                                   pattern=[[-1, P]], channel_multiplier=1))
            q.link(g.memset(scan_keep[:], 1.0))
            q.link(g.memset(scan_keep[:].rearrange("p (c j) -> p c j", j=64)[:, :, 0], 0.0))
            q.link(g.memset(mask_b[0:64, 0:1], 1.0))
            q.link(g.memset(mask_b[64:128, 0:1], 0.0))
            q.link(g.memset(mask_b[0:64, 1:2], 0.0))
            q.link(g.memset(mask_b[64:128, 1:2], 1.0))
            g.memset(junk[:], 0.0)
            g.iota(mc_i[:], pattern=[[0, 1]], base=0, channel_multiplier=1).then_inc(sem("masks_ready"), 1)

            with pool.Fori(0, L) as l:
                q.enter(l, 256)
                pool.wait_ge(sem("layer_done"), l + 1)
                one = bass.ds(l, 1)
                fm = lambda t: t[one].rearrange("o (p k) -> p (o k)", p=P)
                jp = lambda t: t[one].rearrange("o (j p) -> p (o j)", p=P)

                def par(dst, src):
                    load(dst, src, "par_loaded")
                par(g_fm[:, 0, :], fm(T["norm_mix"]))
                for i, n in enumerate(("s5_lambda_re", "s5_lambda_im")):
                    par(lam[:, i, :], T[n][one].rearrange("o (t g) s -> (g s) (o t)", g=2))
                for g2 in range(2):
                    par(lam[64 * g2:64 * g2 + 64, 2, :],
                        T["s5_log_dt"][one].rearrange("o (t g) -> g (o t)", g=2)[g2:g2 + 1].broadcast_to([64, 8]))
                for i, n in enumerate(("s5_b_re", "s5_b_im")):
                    par(s5_b[:, i], T[n][one].rearrange("o (t g) s c -> (g s) (o t) c", g=2))
                for i, n in enumerate(("s5_c_re", "s5_c_im")):
                    par(s5_c[:, i], T[n][one].rearrange("o (a g) c s -> (g c) (o a) s", a=2))
                par(g_fm[:, 1, :], fm(T["norm_cross"]))
                par(g_fm[:, 2, :], fm(T["norm_ffn"]))
                par(conv_w[:], T["conv_w"][one].rearrange("o k (j p) -> p (o k) j", p=P))
                par(conv_b[:], jp(T["conv_b"]))
                par(a_up[:], T["gla_a_up"][one].rearrange("o r n -> r (o n)"))
                par(a_b[:], jp(T["gla_a_b"]))
                par(gla_g[:], T["gla_norm"][one].broadcast_to([P, W]))
                par(s5_d[:], jp(T["s5_d"]))
                par(b_glu[:], jp(T["s5_b_glu"]))
                par(w_glu[:], T["s5_w_glu"][one].rearrange("o (k p) n -> p (o k) n", p=P))
                par(b_rt[:, 0:4], T["b_route_group"][one].broadcast_to([P, 4]))
                par(b_rt[:, 4:20], T["b_route_expert"][one].broadcast_to([P, 16]))
                par(w_rt[:, :, 0:4], T["w_route_group"][one].rearrange("o (p k) n -> p (o k) n", p=P))
                par(w_rt[:, :, 4:20], T["w_route_expert"][one].rearrange("o (p k) n -> p (o k) n", p=P))

                q.need("e_in", 1)
                q.link(g.memset(E[:, 0, :, 0:1], 1.0))
                q.link(g.memset(E[:, 1, :, 0:1], 0.0))
                m = 1
                tA, tB = h[:, 0, :], h[:, 1, :]
                q.need("h_free", 1)
                while m < S:
                    for t0 in range(0, 8, 8):
                        mm_ = m
                        for r in range(2):
                            a = E[:, r, :, 0:mm_]
                            wre = bc(wpow[:, 0, :].unsqueeze(2), [P, 8, mm_])
                            wim = bc(wpow[:, 1, :].unsqueeze(2), [P, 8, mm_])
                            ta = tA[:, 0:8 * mm_].rearrange("p (t s) -> p t s", t=8)
                            tb_ = tB[:, 0:8 * mm_].rearrange("p (t s) -> p t s", t=8)
                            if r == 0:
                                g.tensor_tensor(ta, E[:, 0, :, 0:mm_], wre, ALU.mult)
                                q.link(g.tensor_tensor(tb_, E[:, 1, :, 0:mm_], wim, ALU.mult))
                                q.link(g.tensor_tensor(E[:, 0, :, m:2 * m], ta, tb_, ALU.subtract))
                            else:
                                g.tensor_tensor(ta, E[:, 0, :, 0:mm_], wim, ALU.mult)
                                q.link(g.tensor_tensor(tb_, E[:, 1, :, 0:mm_], wre, ALU.mult))
                                q.link(g.tensor_tensor(E[:, 1, :, m:2 * m], ta, tb_, ALU.add))
                    g.tensor_tensor(wtmp[:, 0, :], wpow[:, 0, :], wpow[:, 0, :], ALU.mult)
                    g.tensor_tensor(wtmp[:, 1, :], wpow[:, 1, :], wpow[:, 1, :], ALU.mult)
                    q.link(g.tensor_tensor(wtmp[:, 2, :], wpow[:, 0, :], wpow[:, 1, :], ALU.mult))
                    g.tensor_tensor(wpow[:, 0, :], wtmp[:, 0, :], wtmp[:, 1, :], ALU.subtract)
                    q.link(g.tensor_tensor(wpow[:, 1, :], wtmp[:, 2, :], wtmp[:, 2, :], ALU.add))
                    m *= 2
                q.done(g.memset(junk[:], 0.0), "e_tab")
                q.need("mix_ev", 12)
                q.link(g.tensor_tensor(ch[:], ch[:], cc[:], ALU.mult))
                for j in range(2):
                    u, y = ch[:, j, :], yaT[:, j, :]
                    t = cc[:, j, :]
                    q.link(g.tensor_scalar(y, u, conv_w[:, 2, j:j + 1], conv_b[:, j:j + 1], ALU.mult, ALU.add))
                    for d in (1, 2):
                        q.link(g.tensor_scalar(t[:, 0:S - d], u[:, 0:S - d], conv_w[:, 2 - d, j:j + 1], None, ALU.mult))
                        q.link(g.tensor_tensor(y[:, d:S], y[:, d:S], t[:, 0:S - d], ALU.add))
                q.done(g.tensor_tensor(yaT[:], yaT[:], cb[:], ALU.mult), "u_conv")
                for t in range(8):
                    q.need("z_out", t + 1)
                    if t >= 2:
                        q.need("yk", t - 1)
                    g.tensor_tensor(gel[:], zo, bc(E[:, 0:1, t, :], [P, 2, S]), ALU.mult)
                    q.link(g.tensor_tensor(ycT[:], zo, bc(E[:, 1:2, t, :], [P, 2, S]), ALU.mult))
                    q.link(g.tensor_tensor(xb[:, t % 2, 0, :], gel[:, 0, :], ycT[:, 1, :], ALU.subtract))
                    q.done(g.tensor_tensor(xb[:, t % 2, 1, :], gel[:, 1, :], ycT[:, 0, :], ALU.add), "xs")
                    q.need("xs", t + 1)
                for n in range(16):
                    i, tb, nh = n // 4, (n // 2) % 2, n % 2
                    q.need("mg_ev", n + 1)
                    src = gs[:, tb, i % 2, nh * 512:nh * 512 + 512]
                    dst_ = h[:, tb, nh * 512:nh * 512 + 512]
                    if i == 0:
                        q.done(g.tensor_copy(dst_, src), "mg_add")
                    else:
                        q.need("mg_add", n - 3)
                        q.done(g.tensor_tensor(dst_, dst_, src, ALU.add), "mg_add")
                q.leave()
            pool.wait_ge(sem("dn_ev"), 4 + 64 * L)
            load(g_out, T["norm_final"].rearrange("(o n) -> o n", o=1).broadcast_to([P, D]), "go_loaded")

        @block.vector
        def _(dve):
            q = Order(dve, "dve")
            v = nc.vector
            flat = lambda t: t[:].rearrange("p a b -> p (a b)")
            flat3 = lambda t: t[:].rearrange("p a b c -> p (a b c)")
            link = q.link

            dve.sem_inc(sem("layer_done"), 1)
            dve.sem_inc(sem("gu_ev"), 4)
            dve.sem_inc(sem("dn_ev"), 4)
            dve.wait_ge(sem("m_sumsq"), 2)
            v.tensor_scalar(st[:, 1, :], st[:, 0, :], 1.0 / D, EPS, ALU.mult, ALU.add).then_inc(sem("m_meansq"), 1)
            inv = (500000.0 ** (-np.arange(8) * 0.125)).astype(np.float32)
            for i in range(8):
                v.memset(invf[:, i:i + 1], float(inv[i]))
            dve.wait_ge(sem("pos_loaded"), 16)
            link(v.tensor_copy(pos_f[:], pos_i[:]))
            link(v.tensor_tensor(ang[:], bc(pos_f[:].unsqueeze(2), [P, TB, 8]),
                                 bc(invf[:].unsqueeze(1), [P, TB, 8]), ALU.mult))

            def reduce_angle(a, r_sin, r_cos, t0, t1):
                magic = 1.5 * 2.0 ** 23
                c1 = 6.28125
                c2 = float(np.float32(2 * np.pi - c1)) if False else 0.0019350051879882812
                c3 = float(2 * np.pi - c1 - c2)
                link(v.tensor_scalar(t0, a, 1.0 / (2 * PI), magic, ALU.mult, ALU.add))
                link(v.tensor_scalar(t0, t0, magic, None, ALU.subtract))
                link(v.scalar_tensor_tensor(out=t1, in0=t0, scalar=-c1, in1=a, op0=ALU.mult, op1=ALU.add))
                link(v.scalar_tensor_tensor(out=t1, in0=t0, scalar=-c2, in1=t1, op0=ALU.mult, op1=ALU.add))
                link(v.scalar_tensor_tensor(out=t1, in0=t0, scalar=-c3, in1=t1, op0=ALU.mult, op1=ALU.add))
                link(v.tensor_scalar(r_sin, t1, 3.1415925, -3.1415925, ALU.min, ALU.max))
                link(v.scalar_tensor_tensor(out=t0, in0=t1, scalar=-1.0, in1=t1, op0=ALU.mult, op1=ALU.max))
                link(v.tensor_scalar(r_cos, t0, -1.0, PI / 2, ALU.mult, ALU.add))

            reduce_angle(ang[:].rearrange("p t f -> p (t f)"), rr[:, 0, :], rr[:, 1, :], rr[:, 2, :], rr[:, 3, :])
            dve.sem_inc(sem("ang_ready"), 1)
            dve.wait_ge(sem("masks_ready"), 1)
            link(v.tensor_scalar(mc_j[:], mc_i[:], 4, 1, ALU.logical_shift_right, ALU.bitwise_and))
            link(v.tensor_copy(mask_c[:, 1:2], mc_j[:]))
            link(v.tensor_scalar(mask_c[:, 0:1], mask_c[:, 1:2], -1.0, 1.0, ALU.mult, ALU.add))
            dve.wait_ge(sem("m_root"), 1)
            link(v.reciprocal(st[:, 3, :], st[:, 2, :]))
            for tb in range(TB):
                v.tensor_scalar(h[:, tb, :], h[:, tb, :], st[:, 3, tb:tb + 1], None, ALU.mult).then_inc(sem("m_h_ready"), 1)
            dve.wait_ge(sem("gm_loaded"), 16)
            for j in range(4):
                dve.wait_ge(sem("m_tp_mm"), j + 1)
                v.tensor_tensor(memT[:, 2 * j:2 * j + 2, :], bank[4 + j][:].rearrange("p (k s) -> p k s", k=2),
                                bc(g_fm[:, 3, 2 * j:2 * j + 2].unsqueeze(2), [P, 2, S]), ALU.mult).then_inc(sem("m_tp_v"), 1)
            dve.wait_ge(sem("rope_ready"), 2)

            def norm_h(u):
                q.need("sumsq", 2 * u + 2)
                q.done(v.tensor_scalar(st[:, 1, :], st[:, 0, :], 1.0 / D, EPS, ALU.mult, ALU.add), "meansq")
                q.need("root", u + 1)
                link(v.reciprocal(st[:, 3, :], st[:, 2, :]))
                for tb in range(TB):
                    q.done(v.tensor_scalar(h[:, tb, :], x[:, tb, :], st[:, 3, tb:tb + 1], None, ALU.mult), "h_ready")

            def norm_evacuate(u, g):
                for j in (0, 2):
                    q.need("tp_mm", 4 * u + j + 1)
                    q.done(v.tensor_tensor(hT[:, 2 * j:2 * j + 2, :], bank[4 + j][:].rearrange("p (k s) -> p k s", k=2),
                                           bc(g_fm[:, g, 2 * j:2 * j + 2].unsqueeze(2), [P, 2, S]), ALU.mult), "tp_v")

            def top_k(w):
                for i in range(TOPK // 8):
                    q.settle()
                    link(v.max(top8[:], w))
                    q.settle()
                    link(v.match_replace(w, top8[:], w, TAKEN))

            def rope(t, half, step, n):
                a, b = t[:, :, :, 0:half], t[:, :, :, half:2 * half]
                cos = bc(rope_cs[:, 0, :, ::step].unsqueeze(2), [P, TB, n, half])
                sin = bc(rope_cs[:, 1, :, ::step].unsqueeze(2), [P, TB, n, half])
                r = [rp[:, i, :, 0:n * half].rearrange("p t (n f) -> p t n f", n=n) for i in range(4)]
                v.tensor_tensor(r[0], a, cos, ALU.mult)
                v.tensor_tensor(r[1], b, sin, ALU.mult)
                v.tensor_tensor(r[2], b, cos, ALU.mult)
                link(v.tensor_tensor(r[3], a, sin, ALU.mult))
                v.tensor_tensor(a, r[0], r[1], ALU.subtract)
                link(v.tensor_tensor(b, r[2], r[3], ALU.add))

            with dve.Fori(0, L) as l:
                q.enter(l, 512)
                norm_h(0)
                q.need("sp_in", 1)
                s_ = lambda i: sp[:, i, :]
                link(v.tensor_tensor(s_(1), lam[:, 0, :], s_(0), ALU.mult))
                link(v.tensor_tensor(s_(3), lam[:, 1, :], s_(0), ALU.mult))
                reduce_angle(s_(3), s_(6), s_(7), s_(4), s_(5))
                q.done(v.memset(s_(19), 0.0), "sp2_in")
                norm_evacuate(0, 0)
                q.need("sp2_out", 1)
                v.tensor_copy(wpow[:, 0, :], s_(9))
                q.done(v.tensor_copy(wpow[:, 1, :], s_(8)), "e_in")
                q.need("tp_mm", 4)
                dve.sem_inc(sem("h_free"), 1)
                link(v.tensor_tensor(s_(10), s_(2), s_(9), ALU.mult))
                link(v.tensor_tensor(s_(11), s_(2), s_(8), ALU.mult))
                link(v.tensor_scalar(s_(10), s_(10), 1.0, None, ALU.subtract))
                link(v.tensor_tensor(s_(12), lam[:, 0, :], lam[:, 0, :], ALU.mult))
                link(v.tensor_tensor(s_(13), lam[:, 1, :], lam[:, 1, :], ALU.mult))
                link(v.tensor_tensor(s_(12), s_(12), s_(13), ALU.add))
                link(v.reciprocal(s_(12), s_(12)))
                link(v.tensor_tensor(s_(13), s_(10), lam[:, 0, :], ALU.mult))
                link(v.tensor_tensor(s_(14), s_(11), lam[:, 1, :], ALU.mult))
                link(v.tensor_tensor(s_(13), s_(13), s_(14), ALU.add))
                link(v.tensor_tensor(s_(13), s_(13), s_(12), ALU.mult))
                link(v.tensor_tensor(s_(14), s_(11), lam[:, 0, :], ALU.mult))
                link(v.tensor_tensor(s_(15), s_(10), lam[:, 1, :], ALU.mult))
                link(v.tensor_tensor(s_(14), s_(14), s_(15), ALU.subtract))
                link(v.tensor_tensor(s_(14), s_(14), s_(12), ALU.mult))
                fr = bc(s_(13).unsqueeze(2), [P, 8, 16])
                fi = bc(s_(14).unsqueeze(2), [P, 8, 16])
                t4 = [rl[:, 0, i * 128:i * 128 + 128].rearrange("p (t c) -> p t c", t=8) for i in range(4)]
                v.tensor_tensor(t4[0], s5_b[:, 0], fr, ALU.mult)
                v.tensor_tensor(t4[1], s5_b[:, 1], fi, ALU.mult)
                v.tensor_tensor(t4[2], s5_b[:, 1], fr, ALU.mult)
                link(v.tensor_tensor(t4[3], s5_b[:, 0], fi, ALU.mult))
                link(v.tensor_tensor(t4[0], t4[0], t4[1], ALU.subtract))
                link(v.tensor_tensor(t4[2], t4[2], t4[3], ALU.add))
                for ri in range(2):
                    for g2 in range(2):
                        v.tensor_scalar(b2[:, ri, :, g2, :], t4[2 * ri], mask_b[:, g2:g2 + 1], None, ALU.mult)
                        v.tensor_scalar(c2[:, ri, :, g2, :], s5_c[:, ri], mask_c[:, g2:g2 + 1], 1.0 - 2.0 * ri,
                                        ALU.mult, ALU.mult)
                q.done(v.memset(s_(19), 0.0), "b2_ready")
                q.need("mix_ev", 4)
                rope(dq[:].rearrange("p t (n d) -> p t n d", n=4), 8, 1, 4)
                rope(dt_[:, :, 0:64].unsqueeze(2), 8, 1, 1)
                rope(dt_[:, :, 128:384].rearrange("p t (n d) -> p t n d", n=8), 4, 2, 8)
                rope(dt_[:, :, 384:416].unsqueeze(2), 4, 2, 1)
                v.tensor_copy(kk[:], bc(dt_[:, :, 0:64].unsqueeze(2), [P, TB, 2, 64]))
                v.tensor_scalar(w16[:], dt_[:, :, 416:424], 0.0625, None, ALU.mult)
                q.done(v.tensor_copy(ki4[:], bc(dt_[:, :, 384:416].unsqueeze(2), [P, TB, 4, 32])), "rope")
                q.need("la_mm", 1)
                for j in range(2):
                    ins = v.tensor_scalar(za[:, j, :], bank[7][:, j * S:j * S + S], a_b[:, j:j + 1], None, ALU.add)
                q.link(ins)
                q.done(v.memset(s_(19), 0.0), "la_ev")
                dve.sem_inc(sem("ls_in"), 1)
                q.need("ls_ex", 1)
                link(v.scalar_tensor_tensor(out=zb[:], in0=za[:], scalar=0.0, in1=zb[:], op0=ALU.min, op1=ALU.subtract))
                for j in range(2):
                    ins = v.tensor_tensor_scan(out=za[:, j, :], data0=scan_keep[:], data1=zb[:, j, :], initial=0.0,
                                               op0=ALU.mult, op1=ALU.add)
                link(ins)
                zc = za[:].rearrange("p a (c j) -> p (a c) j", j=64)
                q.done(v.tensor_tensor(zb[:].rearrange("p a (c j) -> p (a c) j", j=64),
                                       bc(zc[:, :, 63:64], [P, 8, 64]), zc, ALU.subtract), "gla_cum")
                for n in range(8):
                    q.need("ix_ev", n + 1)
                    blk = 1 if n < 4 else 0
                    wide = S if n < 4 else P
                    acc = isc[:, 1:3, :].rearrange("p a s -> p (a s)") if n < 4 else isc[:, 0, :]
                    for i in range(2):
                        hd = n % 4 + 4 * i
                        src = rl[:, n % 2, i * wide:i * wide + wide]
                        if hd == 0:
                            link(v.tensor_scalar(acc, src, w16[:, blk, 0:1], None, ALU.mult))
                        else:
                            ins = v.scalar_tensor_tensor(out=acc, in0=src, scalar=w16[:, blk, hd:hd + 1], in1=acc,
                                                         op0=ALU.mult, op1=ALU.add)
                            if i == 0:
                                link(ins)
                    q.done(ins, "ix_acc")
                    q.need("ix_acc", n + 1)
                q.need("gla_exp", 1)
                q.need("mix_ev", 8)
                link(v.scalar_tensor_tensor(out=gq[:], in0=gq[:], scalar=0.125, in1=eb[:], op0=ALU.mult, op1=ALU.mult))
                link(v.tensor_tensor(en[:], en[:], gk[:], ALU.mult))
                q.done(v.tensor_tensor(ke[:], ke[:], gk[:], ALU.mult), "gla_qk")
                for blk in range(2):
                    d_ = isc[:, 2 * blk, :]
                    link(v.tensor_tensor(d_, d_, cneg[:], ALU.add))
                    w_ = isc[:, 0, :] if blk == 0 else isc[:, 1:3, :].rearrange("p a s -> p (a s)")
                    top_k(w_)
                    link(v.tensor_scalar(w_, w_, TAKEN, NEG, ALU.not_equal, ALU.mult))
                    link(v.tensor_tensor(d_, d_, cneg[:], ALU.add))
                for tb in range(TB):
                    q.need("att_mm", tb + 1)
                    if tb == 0:
                        q.need("bc_ev", 2)
                    q.done(v.tensor_tensor(attm[:, tb], bank[4 + tb][:].rearrange("p (h s) -> p h s", h=4),
                                           bc(gla_mask[:].unsqueeze(1), [P, 4, P]), ALU.mult), "att_ev")
                for u in range(3):
                    q.need("dl_mm", u + 1)
                    n, wide = (4, P) if u == 0 else (2, S)
                    bias = isc[:, 0, :] if u == 0 else isc[:, 1:3, :].rearrange("p a s -> p (a s)")
                    q.done(v.scalar_tensor_tensor(out=dl[:, u].rearrange("p (h s) -> p h s", h=n),
                                                  in0=bank[5 + u][:].rearrange("p (h s) -> p h s", h=n), scalar=0.125,
                                                  in1=bc(bias.unsqueeze(1), [P, n, wide]), op0=ALU.mult, op1=ALU.add),
                           "dl_ev")
                q.need("dl_ev", 3)
                q.done(v.tensor_reduce(dstat[:, 0, 0, :], dl[:, 0].rearrange("p (h s) -> p h s", h=4), AX, ALU.max,
                                       negate=True), "mx")
                q.done(v.tensor_reduce(dstat[:, 0, 1, :], dl[:, 1:3].rearrange("p a (g s) -> p (a g) s", s=S), AX, ALU.max,
                                       negate=True), "mx")
                q.need("u_mm", 1)
                link(v.memset(rl[:], 0.0))
                for n in range(3):
                    for i in range(2):
                        r = slice(64 * i, 64 * i + 64)
                        if n == 0:
                            v.tensor_copy(state[r, 0, :, r], bank[4][r, 0:P].rearrange("p (h e) -> p h e", h=2))
                            continue
                        for hp in range(2):
                            ins = v.scalar_tensor_tensor(out=state[r, n, hp, r], in0=state[r, n - 1, hp, r],
                                                         scalar=eb[r, hp, 64 * n + 63:64 * n + 64],
                                                         in1=bank[4][r, n * P + hp * 64:n * P + hp * 64 + 64],
                                                         op0=ALU.mult, op1=ALU.add)
                    if n:
                        link(ins)
                    else:
                        link(v.memset(s_(19), 0.0))
                q.done(v.memset(s_(19), 0.0), "st_ready")
                q.need("ex", 2)
                link(v.reciprocal(dstat[:, 2].rearrange("p a b -> p (a b)"), dstat[:, 1].rearrange("p a b -> p (a b)")))
                vv = dl[:, 0].rearrange("p (h s) -> p h s", h=4)
                link(v.tensor_tensor(vv, vv, bc(dstat[:, 2, 0, :].unsqueeze(2), [P, 4, P]), ALU.mult))
                vv = dl[:, 1:3].rearrange("p a (g s) -> p (a g) s", s=S)
                q.done(v.tensor_tensor(vv, vv, bc(dstat[:, 2, 1, :].unsqueeze(2), [P, 4, S]), ALU.mult), "p_ready")
                q.need("o_sq", 2)
                link(v.tensor_reduce(ost[:, 0].rearrange("p a b -> p (a b)"),
                                     zb[:].rearrange("p t (h d) -> p (t h) d", h=4), AX, ALU.add))
                q.link(v.tensor_scalar(ost[:, 0], ost[:, 0], 1.0 / 64, EPS, ALU.mult, ALU.add))
                q.done(v.memset(s_(19), 0.0), "o_ms")
                q.need("sr", 1)
                link(v.tensor_tensor(gr[:], gr[:], bc(gla_g[:].unsqueeze(1), [P, TB, W]), ALU.mult))
                q.need("o_rt", 1)
                link(v.reciprocal(ost[:, 0].rearrange("p a b -> p (a b)"), ost[:, 1].rearrange("p a b -> p (a b)")))
                for tb in range(TB):
                    ins = v.tensor_tensor(za[:, tb, :].rearrange("p (h d) -> p h d", h=4),
                                          bank[4 + tb][:, 0:W].rearrange("p (h d) -> p h d", h=4),
                                          bc(ost[:, 0, tb, :].unsqueeze(2), [P, 4, 64]), ALU.mult)
                link(ins)
                q.done(v.tensor_tensor(za[:], za[:], gr[:], ALU.mult), "o_done")
                q.need("e_tab", 1)
                q.need("pt_mm", 3)
                for t in range(8):
                    q.need("bu_mm", t + 1)
                    bu = bank[(4, 7)[t % 2]][:].rearrange("p (r s) -> p r s", r=2)
                    v.tensor_tensor(pq[:, 0], bu, bc(E[:, 0:1, t, :], [P, 2, S]), ALU.mult)
                    link(v.tensor_tensor(pq[:, 1], bu, bc(E[:, 1:2, t, :], [P, 2, S]), ALU.mult))
                    dve.sem_inc(sem("bu_ev"), 1)
                    v.tensor_tensor(zi[:, 0, :], pq[:, 0, 0, :], pq[:, 1, 1, :], ALU.add)
                    link(v.tensor_tensor(zi[:, 1, :], pq[:, 0, 1, :], pq[:, 1, 0, :], ALU.subtract))
                    if t >= 1:
                        q.need("xs", t)
                    for ri in range(2):
                        ins = v.tensor_tensor_scan(out=zo[:, ri, :], data0=bc(sp[:, 2, t:t + 1], [P, S]), data1=zi[:, ri, :],
                                                   initial=0.0, op0=ALU.mult, op1=ALU.add)
                    q.done(ins, "z_out")
                q.need("yk", 8)
                for j in range(2):
                    ins = v.scalar_tensor_tensor(out=gel[:, j, :], in0=uT[:, j, :], scalar=s5_d[:, j:j + 1],
                                                 in1=bank[5][:, j * S:j * S + S], op0=ALU.mult, op1=ALU.add)
                q.done(ins, "s5y")
                q.need("glu_ev", 1)
                q.done(v.tensor_tensor(ycT[:], ycT[:], gel[:], ALU.mult), "yc")
                for n in range(16):
                    i, tb, nh = n // 4, (n // 2) % 2, n % 2
                    q.need("mg_mm", n + 1)
                    q.need("gate_ev", 4 * i + 4)
                    gsv = gs[:, tb, i % 2, nh * 512:nh * 512 + 512]
                    q.done(v.tensor_tensor(gsv, bank[n % 4][:], gsv, ALU.mult), "mg_ev")
                for j in (0, 2):
                    q.need("tp_mm", 4 + j + 1)
                    q.done(v.tensor_copy(hT[:, 2 * j:2 * j + 2, :].rearrange("p a b -> p (a b)"), bank[4 + j][:]), "tp_v")
                for n in range(4):
                    nh, tb = n // 2, n % 2
                    q.need("wo_mm", n + 1)
                    xv = x[:, tb, nh * 512:nh * 512 + 512]
                    q.done(v.tensor_tensor(xv, xv, bank[n][:], ALU.add), "wo_ev")
                norm_h(1)
                norm_evacuate(2, 1)
                for n in range(4):
                    q.need("cl_mm", n + 1)
                    link(v.tensor_reduce(cst[:, 2, n // 2, 2 * (n % 2):2 * (n % 2) + 2],
                                         bank[4 + n][:].rearrange("p (h s) -> p h s", h=2), AX, ALU.max))
                q.done(v.tensor_scalar(cst[:, 0], cst[:, 2], -(128 ** -0.5), None, ALU.mult), "cmx")
                q.need("cex", 1)
                link(v.reciprocal(cst[:, 2].rearrange("p a b -> p (a b)"), cst[:, 1].rearrange("p a b -> p (a b)")))
                for tb in range(TB):
                    ins = v.tensor_tensor(px[:, tb], px[:, tb], bc(cst[:, 2, tb, :].unsqueeze(2), [P, 4, S]), ALU.mult)
                q.done(ins, "cp")
                for n in (0, 2):
                    q.need("cpt_mm", n + 1)
                    ins = v.tensor_copy(pTx[:, n // 2, 0:2, :].rearrange("p a b -> p (a b)"), bank[n][:])
                    if n == 0:
                        ins.then_inc(sem("cpt_v"), 1)
                    else:
                        ins.then_inc(sem("cpt_v"), 1)
                q.need("cpt_v", 2)
                q.need("cpt_a", 2)
                dve.sem_inc(sem("cpt_ev"), 4)
                for n in range(4):
                    tb, nh = n // 2, n % 2
                    q.need("cy_mm", n + 1)
                    xv = x[:, tb, nh * 512:nh * 512 + 512]
                    q.done(v.tensor_tensor(xv, xv, bank[n][:], ALU.add), "cy_ev")
                norm_h(2)
                norm_evacuate(3, 2)
                q.need("rt_mm", 1)
                r_ = lambda i: rx[:, i]
                link(v.tensor_tensor(rt[:], bank[0][:, 0:40].rearrange("p (t n) -> p t n", t=2),
                                     bc(b_rt[:].unsqueeze(1), [P, TB, 20]), ALU.add))
                dve.sem_inc(sem("rt_e1"), 1)

                def first_max(vals, mx, eq, run, hot):
                    link(v.tensor_reduce(mx[:, :, 0], vals, AX, ALU.max))
                    link(v.tensor_tensor(eq, vals, bc(mx[:, :, 0:1], [P, TB, 4]), ALU.is_equal))
                    for tb in range(TB):
                        link(v.tensor_tensor_scan(out=run[:, tb, :], data0=ones4[:], data1=eq[:, tb, :], initial=0.0,
                                                  op0=ALU.mult, op1=ALU.add))
                    link(v.scalar_tensor_tensor(out=hot, in0=run, scalar=1.0, in1=eq, op0=ALU.is_equal, op1=ALU.mult))

                ones4 = scan_keep[:, 1:5]
                first_max(rt[:, :, 0:4], r_(0), r_(3), r_(4), r_(5))
                link(v.tensor_tensor(r_(1), rt[:, :, 0:4], bc(r_(0)[:, :, 0:1], [P, TB, 4]), ALU.subtract))
                for tb in range(TB):
                    link(v.tensor_tensor(rxx[:, tb], rt[:, tb, 4:20].rearrange("p (g e) -> p g e", g=4),
                                         bc(r_(5)[:, tb, :].unsqueeze(2), [P, 4, 4]), ALU.mult))
                link(v.tensor_tensor(rxx[:, :, 0:2, :], rxx[:, :, 0:2, :], rxx[:, :, 2:4, :], ALU.add))
                link(v.tensor_tensor(r_(8), rxx[:, :, 0, :], rxx[:, :, 1, :], ALU.add))
                first_max(r_(8), r_(0), r_(3), r_(4), r_(9))
                link(v.tensor_tensor(r_(6), r_(8), bc(r_(0)[:, :, 0:1], [P, TB, 4]), ALU.subtract))
                dve.sem_inc(sem("rt_x1"), 1)
                link(v.scalar_tensor_tensor(out=r_(8), in0=r_(9), scalar=NEG, in1=r_(8), op0=ALU.mult, op1=ALU.add))
                first_max(r_(8), r_(0), r_(3), r_(4), r_(10))
                q.need("rt_x2", 1)
                link(v.tensor_tensor(r_(9), r_(9), r_(10), ALU.add))
                link(v.tensor_tensor(r_(7), r_(7), r_(9), ALU.mult))
                link(v.tensor_reduce(r_(0)[:, :, 0], r_(7), AX, ALU.add))
                link(v.tensor_reduce(r_(0)[:, :, 1], r_(2), AX, ALU.add))
                link(v.tensor_tensor(r_(0)[:, :, 2], r_(0)[:, :, 0], r_(0)[:, :, 1], ALU.mult))
                link(v.reciprocal(r_(0)[:, :, 3], r_(0)[:, :, 2]))
                link(v.tensor_tensor(r_(7), r_(7), bc(r_(0)[:, :, 3:4], [P, TB, 4]), ALU.mult))
                for tb in range(TB):
                    link(v.tensor_tensor(comb[:, tb], bc(r_(5)[:, tb, :].unsqueeze(2), [P, 4, 4]),
                                         bc(r_(7)[:, tb, :].unsqueeze(1), [P, 4, 4]), ALU.mult))
                q.settle()
                combf = comb[:].rearrange("p t g e -> p t (g e)")
                with dve.Fori(0, N_EXP) as e:
                    for ft in range(4):
                        dve.wait_ge(sem("gu_sg"), l * 64 + e * 4 + ft + 1)
                        v.tensor_tensor(heT[:, ft, :], sg[:, ft, :], bank[ft][:, S:2 * S],
                                        ALU.mult).then_inc(sem("he_ready"), 1)
                    dve.wait_ge(sem("he_ready"), l * 64 + e * 4 + 4)
                    dve.sem_inc(sem("gu_ev"), 4)
                    for b in range(4):
                        tb, nh = b // 2, b % 2
                        dve.wait_ge(sem("dn_mm"), l * 64 + e * 4 + b + 1)
                        xv = x[:, tb, nh * 512:nh * 512 + 512]
                        v.scalar_tensor_tensor(out=xv, in0=bank[4 + b][:], scalar=combf[:, tb, bass.ds(e, 1)], in1=xv,
                                               op0=ALU.mult, op1=ALU.add).then_inc(sem("dn_ev"), 1)
                    dve.wait_ge(sem("dn_ev"), l * 64 + e * 4 + 8)
                dve.sem_inc(sem("layer_done"), 1)
                q.leave()
            dve.wait_ge(sem("f_sumsq"), 2)
            v.tensor_scalar(st[:, 1, :], st[:, 0, :], 1.0 / D, EPS, ALU.mult, ALU.add).then_inc(sem("f_meansq"), 1)
            dve.wait_ge(sem("f_root"), 1)
            link(v.reciprocal(st[:, 3, :], st[:, 2, :]))
            dve.wait_ge(sem("go_loaded"), 16)
            for tb in range(TB):
                v.scalar_tensor_tensor(out=h[:, tb, :], in0=x[:, tb, :], scalar=st[:, 3, tb:tb + 1], in1=g_out,
                                       op0=ALU.mult, op1=ALU.mult).then_inc(sem("out_ready"), 1)

        for name, n in produced.items():
            if name in PER and PER[name] != n and name not in ("used",):
                print("semaphore", name, "produced", n, "said", PER[name])


N_PAR = 23
for _n, _k in dict(h_free=1, rt_x2=1, cpt_v=2, cpt_a=2, settled=0).items():
    PER[_n] = _k

_INS = ['x', 'mem', 'positions', 'norm_mix', 'w_in', 'conv_w', 'conv_b', 'gla_a_up', 'gla_a_b', 'gla_norm',
        's5_lambda_re', 's5_lambda_im', 's5_log_dt', 's5_b_re', 's5_b_im', 's5_c_re', 's5_c_im', 's5_d',
        's5_w_glu', 's5_b_glu', 'w_branch', 'w_out', 'norm_cross', 'w_cq', 'w_ckv', 'w_co', 'norm_ffn',
        'w_route_group', 'b_route_group', 'w_route_expert', 'b_route_expert', 'w_e_gate', 'w_e_up',
        'w_e_down', 'norm_mem', 'norm_final']


def kernel(**inputs):
    import concourse.bacc as _bacc
    from concourse.bass_utils import run_bass_kernel_spmd as _run

    nc = _bacc.Bacc("TRN2", target_bir_lowering=False, num_devices=1)
    arrays, T = {}, {}
    for name in _INS:
        a = np.ascontiguousarray(inputs[name])
        arrays["in_" + name] = a
        T[name] = nc.dram_tensor("in_" + name, a.shape, mybir.dt.from_np(a.dtype), kind="ExternalInput").ap()
    out = nc.dram_tensor("out", (1, S, D), F32, kind="ExternalOutput").ap()
    trunk(nc, T, out)
    r = _run(nc, [arrays], core_ids=[0])
    return r.results[0]["out"]
```

```python
from contextlib import ExitStack

import numpy as np
import concourse.bass as bass
from concourse import mybir

ALU = mybir.AluOpType
ACT = mybir.ActivationFunctionType
F32 = mybir.dt.float32
F32R = mybir.dt.float32r
I32 = mybir.dt.int32
AX = mybir.AxisListType.X

P = 128
D = 1024
S = 256
TB = S // P
KD = D // P
L = 2
EPS = 1e-6
W = 256
PI = float(np.pi)

C_H, C_B, C_C = 0, 256, 512
G_Q, G_K, G_V, G_R, G_A = 768, 1024, 1280, 1536, 1792
S_U, D_Q, D_K, D_V, I_Q, I_K, I_W, GATES = 1808, 2064, 2320, 2384, 2448, 2704, 2736, 2744

NS = 3
SLOT = KD * 512
N_EXP = 16
TOPK = 64
NEG = -1.0e30
TAKEN = -3.0e38

DENSE = ["m5", "m3", "m1", "m2", "m4", "m0", "g0", "g1", "g2", "g3", "ckv0", "ckv1", "br01",
         "g4", "g5", "g6", "g7", "br23", "wo0", "wo1", "cq", "co"]
MIX_COLS = {"m5": (D_K, GATES), "m3": (S_U, D_K), "m1": (C_C, G_K), "m2": (G_K, G_R),
            "m4": (G_R, S_U), "m0": (C_H, C_C)}
ND = len(DENSE)
NCH = ND + 3 * N_EXP

PER = dict(
    used=ND,
    sumsq=6, meansq=3, root=3, h_ready=6, tp_mm=16, tp_v=8, tp_a=8, hg_ready=2,
    mix_mm=12, mix_ev=12, rope=1, sa_mm=3, sa_ev=3, la_mm=1, la_ev=1, ix_mm=8, ix_ev=8, ix_acc=8,
    ls_in=1, ls_ab=1, ls_ex=1, gla_cum=1, gla_exp=1, gla_qk=1, ketok_mm=1, ketok_ev=1, att_mm=2, att_ev=2,
    params=1, sp_in=1, sp_out=1, sp2_in=1, sp2_out=1, bt_mm=1, ct_mm=1, bc_ev=2, b2_ready=1,
    u_mm=1, st_ready=1, dl_mm=3, dl_ev=3, mx=2, ex=2, p_ready=1, pt_mm=3, pt_ev=3,
    o_mm=2, o_sq=2, o_ms=1, o_rt=1, o_done=1, sr=1, od_mm=1, od_ev=1, ybt_mm=1, ybt_ev=1,
    e_in=1, e_tab=1, bu_mm=8, bu_ev=8, zin=8, z_out=8, xs=8, yk=8, s5y=1, gelu=1, glu_mm=1, glu_ev=1, yc=1,
    u_conv=1, gate_mm=16, gate_ev=16, ckv_mm=4, ckv_ev=4, mg_mm=16, mg_ev=16, mg_add=16,
    wo_mm=4, wo_ev=4, cq_mm=2, cq_ev=2, cl_mm=4, cmx=1, cex=1, cp=1, cpt_mm=4, cpt_ev=4,
    co_mm=2, co_ev=2, cy_mm=4, cy_ev=4, rt_mm=1, rt_e1=1, rt_x1=1, comb=1,
    hs=1, flag=1, ffn_done=1,
)
PER_TURN = dict(split=3, w_hi=12, w_lo=12, w_used=12, pick=1, pickT_mm=1, pickT=1, ga_mm=2, ga_hi=2, ga_lo=2,
                act_gate=1, hid=1, hidT_mm=1, hidT_hi=1, hidT_lo=1, y_mm=2, y_hi=2, y_lo=2,
                sc_mm=4, x_acc=4)
PASSES = 2
RP = 6
PIECE = SLOT // 4


def bc(ap, shape):
    return ap.broadcast_to(shape)


def trunk(nc, T, out):
    with ExitStack() as ctx:
        def sb(name, shape, dt=F32):
            return ctx.enter_context(nc.sbuf_tensor(name, shape, dt))

        sems = {}

        def sem(name):
            if name not in sems:
                sems[name] = ctx.enter_context(nc.semaphore(name))
            return sems[name]

        bank = [ctx.enter_context(nc.psum_tensor(f"bank{i}", [P, 512], F32)) for i in range(8)]

        ring = sb("ring", [P, NS, SLOT])
        x = sb("x", [P, TB, D])
        h = sb("h", [P, TB, D])
        hT = sb("hT", [P, KD, S])
        memT = sb("memT", [P, KD, S])
        ident = sb("ident", [P, P])
        gla_mask = sb("gla_mask", [P, P])
        cneg = sb("cneg", [P, P])
        scan_keep = sb("scan_keep", [P, S])
        tri = sb("tri", [P, P])
        ones = sb("ones", [P, P])
        slot_no = sb("slot_no", [P, P])
        flag = sb("flag", [P, 1], I32)
        mask_b = sb("mask_b", [P, 2])
        mask_c = sb("mask_c", [P, 2])
        mc_i = sb("mc_i", [P, 1], I32)
        mc_j = sb("mc_j", [P, 1], I32)
        pos_i = sb("pos_i", [P, TB], I32)
        pos_f = sb("pos_f", [P, TB])
        invf = sb("invf", [P, 8])
        ang = sb("ang", [P, TB, 8])
        rr = sb("rr", [P, 4, 16])
        rope_cs = sb("rope_cs", [P, 2, TB, 8])
        junk = sb("junk", [P, 1])
        st = sb("st", [P, 4, TB])
        g_fm = sb("g_fm", [P, 4, KD])
        conv_w = sb("conv_w", [P, 3, 2])
        conv_b = sb("conv_b", [P, 2])
        a_up = sb("a_up", [16, W])
        a_b = sb("a_b", [P, 2])
        gla_g = sb("gla_g", [P, W])
        lam = sb("lam", [P, 3, 8])
        s5_b = sb("s5_b", [P, 2, 8, 16])
        s5_c = sb("s5_c", [P, 2, 2, 64])
        s5_d = sb("s5_d", [P, 2])
        b_glu = sb("b_glu", [P, 2])
        w_glu = sb("w_glu", [P, 2, W])
        b_rt = sb("b_rt", [P, 20])
        w_rt = sb("w_rt", [P, KD, 20])
        outer, branch_ctx = ctx, ExitStack()

        def sb(name, shape, dt=F32):
            return branch_ctx.enter_context(nc.sbuf_tensor(name, shape, dt))

        gs = sb("gs", [P, TB, 2, D])
        kTx = sb("kTx", [P, 4, S])
        vx = sb("vx", [P, TB, 512])
        dt_ = sb("dtok", [P, TB, 424])
        dq = sb("dq", [P, TB, W])
        kk = sb("kk", [P, TB, 2, 64])
        ki4 = sb("ki4", [P, TB, 4, 32])
        rp = sb("rp", [P, 4, TB, 32])
        qTd = sb("qTd", [P, 2, S])
        kTd = sb("kTd", [P, 2, S])
        qiT = sb("qiT", [P, 2, S])
        rl = sb("rl", [P, 2, 512])
        state = rl[:].rearrange("p a b -> p (a b)")[:, 0:768].rearrange("p (n h e) -> p n h e", n=3, h=2)
        w16 = sb("w16", [P, TB, 8])
        isc = sb("isc", [P, 3, P])
        top8 = sb("top8", [P, 8])
        dl = sb("dl", [P, 3, 4 * P])
        dstat = sb("dstat", [P, 3, TB, 4])
        pT = sb("pT", [P, 3, 4, P])
        ydT = sb("ydT", [P, 2, S])
        gq = sb("gq", [P, 2, S])
        gk = sb("gk", [P, 2, S])
        gv = sb("gv", [P, TB, W])
        gr = sb("gr", [P, TB, W])
        alow = sb("alow", [16, S])
        za = sb("za", [P, 2, S])
        zb = sb("zb", [P, 2, S])
        eb = sb("eb", [P, 2, S])
        en = sb("en", [P, 2, S])
        ke = sb("ke", [P, 2, S])
        ketok = sb("ketok", [P, TB, W])
        attm = sb("attm", [P, TB, 4, P])
        ost = sb("ost", [P, 2, TB, 4])
        ybT = sb("ybT", [P, 2, S])
        cc = sb("cc", [P, 2, S])
        ch = sb("ch", [P, 2, S])
        cb = sb("cb", [P, 2, S])
        yaT = sb("yaT", [P, 2, S])
        uT = sb("uT", [P, 2, S])
        sp = sb("sp", [P, 20, 8])
        wpow = sb("wpow", [P, 2, 8])
        wtmp = sb("wtmp", [P, 4, 8])
        E = sb("E", [P, 2, 8, S])
        b2 = attm[:].rearrange("p a b c -> p (a b c)")[:, 0:512].rearrange("p (r t g c) -> p r t g c", r=2, t=8, g=2)
        c2 = attm[:].rearrange("p a b c -> p (a b c)")[:, 512:1024].rearrange("p (r h g s) -> p r h g s", r=2, h=2, g=2)
        bT = sb("bT", [P, 2, 2, P])
        cT = sb("cT", [P, 2, 2, P])
        gel = gk
        ycT = en
        hf = h[:].rearrange("p t n -> p (t n)")
        pq = hf[:, 0:1024].rearrange("p (q r s) -> p q r s", q=2, r=2)
        zi = hf[:, 1024:1536].rearrange("p (r s) -> p r s", r=2)
        zo = dl[:].rearrange("p a b -> p (a b)")[:, 0:512].rearrange("p (r s) -> p r s", r=2)
        xb = dl[:].rearrange("p a b -> p (a b)")[:, 512:1536].rearrange("p (q r s) -> p q r s", q=2, r=2)
        Ef = E[:].rearrange("p r t s -> p (r t s)")
        qTx = Ef[:, 0:1024].rearrange("p (h s) -> p h s", h=4)
        oTx = Ef[:, 1024:2048].rearrange("p (h s) -> p h s", h=4)
        px = Ef[:, 2048:4096].rearrange("p (t h m) -> p t h m", t=TB, h=4)
        pTx = gs[:].rearrange("p a b c -> p (a b c)")[:, 0:2048].rearrange("p (b h s) -> p b h s", b=2, h=4)
        cst = sb("cst", [P, 3, TB, 4])

        branch_ctx.close()

        def sb(name, shape, dt=F32):
            return outer.enter_context(nc.sbuf_tensor(name, shape, dt))

        g_bc = sb("g_bc", [P, D])
        hs_hi = sb("hs_hi", [P, TB, D], F32R)
        hs_lo = sb("hs_lo", [P, TB, D], F32R)
        ga_hi = sb("ga_hi", [P, KD, P], F32R)
        ga_lo = sb("ga_lo", [P, KD, P], F32R)
        pick = sb("pick", [P, TB, P], F32R)
        pickT = sb("pickT", [P, S], F32R)
        act_g = sb("act_g", [P, 512])
        hid = sb("hid", [P, 512])
        hidT_hi = sb("hidT_hi", [P, 4, P], F32R)
        hidT_lo = sb("hidT_lo", [P, 4, P], F32R)
        y_hi = sb("y_hi", [P, D], F32R)
        y_lo = sb("y_lo", [P, D], F32R)
        w_hi = sb("w_hi", [P, RP, PIECE], F32R)
        w_lo = sb("w_lo", [P, RP, PIECE], F32R)
        rt = sb("rt", [P, TB, 20])
        rx = sb("rx", [P, 12, TB, 4])
        rxx = sb("rxx", [P, TB, 4, 4])
        comb = sb("comb", [P, TB, 4, 4])
        sel = sb("sel", [P, TB, 4, 4])
        place = sb("place", [P, TB, PASSES, N_EXP])
        most = sb("most", [P, 2])
        g_out = g_bc[:]
        produced = {}

        class Order:

            def __init__(self, eng, name):
                self.e, self.name, self.n, self.l, self.base = eng, name, 0, None, 0
                self.own = sem(name + "_steps")

            def link(self, ins):
                ins.then_inc(self.own, 1)
                self.n += 1
                self.e.wait_ge(self.own, self.base + self.n)
                if self.name in ("pool", "pe"):
                    self.settle()

            def enter(self, l, stride):
                self.l, self.before, self.stride = l, self.n, stride
                self.base, self.n = l * stride + self.n, 0

            def leave(self):
                assert self.n < self.stride, (self.name, self.n)
                self.e.sem_inc(self.own, self.stride - self.n)
                self.base, self.n, self.l = L * self.stride + self.before, 0, None

            def done(self, ins, name, times=1):
                ins.then_inc(sem(name), 1)
                produced[name] = produced.get(name, 0) + times

            def need(self, name, k):
                per = PER[name]
                l = self.l if self.l is not None else L
                self.e.wait_ge(sem(name), l * per + k)
                if self.name == "pool" or self.name == "sp":
                    self.settle()

            def need_turn(self, name, p, e, k):
                per = PER_TURN[name]
                self.e.wait_ge(sem(name), (self.l * PASSES + p) * (N_EXP * per) + e * per + k)

            def turns(self, p, one):
                one(p, 0, first=True)
                self.settle()
                with self.e.Fori(1, N_EXP - 1) as e:
                    one(p, e)
                one(p, N_EXP - 1, last=True)

            def passes(self, one_pass, signals):
                one_pass(0)
                self.e.wait_ge(sem("flag"), self.l + 1)
                self.settle()
                more = self.e.value_load(flag[0:1, 0:1], min_val=0, max_val=1)
                with self.e.If(more):
                    one_pass(1)
                with self.e.Else():
                    for name, n in signals:
                        if name in PER_TURN:
                            credit = {"split": NS, "w_used": RP}.get(name, 0)
                            self.e.wait_ge(sem(name), (self.l * PASSES + 1) * n + credit)
                        else:
                            self.e.wait_ge(sem("split"), (self.l * PASSES + 1) * (3 * N_EXP) + NS)
                        self.e.sem_inc(sem(name), n)

            def settle(self):
                self.e.sem_inc(sem("settled"), 1)

        SC_BANKS = (7, 0, 1, 4)
        ld = [sem(f"loaded{s}") for s in range(NS)]
        slot_of = [i % NS for i in range(NCH)]
        e_slot = slot_of[ND:ND + 3]
        dense_loads = [slot_of[:ND].count(s) for s in range(NS)]
        loads = [n + PASSES * N_EXP for n in dense_loads]
        nth = [slot_of[:i].count(slot_of[i]) + 1 for i in range(ND)]
        w_in = T["w_in"]

        def chunk_src(name, l):
            def k_tiles(ap):
                return ap.rearrange("o (p k) n -> p (o k) n", p=P)
            one = bass.ds(l, 1)
            if name in MIX_COLS:
                a, b = MIX_COLS[name]
                return k_tiles(w_in[one, :, a:b]), KD, b - a
            if name[0] == "g":
                a = GATES + int(name[1:]) * 512
                return k_tiles(w_in[one, :, a:a + 512]), KD, 512
            if name.startswith("ckv"):
                a = int(name[3]) * 512
                return k_tiles(T["w_ckv"][one, :, a:a + 512]), KD, 512
            if name.startswith("br"):
                i = int(name[2])
                return T["w_branch"][one, i:i + 2].rearrange("o i (j p) n -> p (o i j) n", p=P), 4, D
            if name.startswith("wo"):
                a = int(name[2]) * 512
                return k_tiles(T["w_out"][one, :, a:a + 512]), KD, 512
            if name == "cq":
                return k_tiles(T["w_cq"][one]), KD, 512
            if name == "co":
                return T["w_co"][one].rearrange("o (h p) n -> p (o h) n", p=P), 4, D

        def slot(s, k, n):
            return ring[:, s, 0:k * n].rearrange("p (k n) -> p k n", n=n)

        block = ctx.enter_context(nc.Block())

        @block.sync
        def _(sp_):
            q = Order(sp_, "sp")
            sp_.dma_start(x[:], T["x"].rearrange("o (t p) n -> p (o t) n", p=P)).then_inc(sem("x_loaded"), 16)
            with sp_.Fori(0, L) as l:
                q.l = l
                for i, name in enumerate(DENSE):
                    if i < NS:
                        sp_.wait_ge(sem("split"), l * (PASSES * N_EXP * 3) + NS)
                        q.settle()
                    else:
                        q.need("used", i - NS + 1)
                    src, k, n = chunk_src(name, l)
                    sp_.dma_start(slot(slot_of[i], k, n), src).then_inc(ld[slot_of[i]], 16)

                def experts(p):
                    with sp_.Fori(0, N_EXP) as e:
                        for j, (wt, k, n) in enumerate((("w_e_gate", KD, 512), ("w_e_up", KD, 512), ("w_e_down", 4, D))):
                            if p == 0:
                                q.need("used", ND + j - NS + 1)
                            q.need_turn("split", p, e, j + 1)
                            q.settle()
                            src = T[wt][bass.ds(l, 1), bass.ds(e, 1)].rearrange("o i (p k) n -> p (o i k) n", p=P)
                            sp_.dma_start(slot(e_slot[j], k, n), src).then_inc(ld[e_slot[j]], 16)

                q.passes(experts, [(f"loaded{s}", 16 * N_EXP) for s in range(NS)])
            sp_.wait_ge(sem("out_ready"), 2)
            sp_.dma_start(out.rearrange("o (t p) n -> p (o t) n", p=P), h[:]).then_inc(sem("stored"), 16)
            sp_.wait_ge(sem("stored"), 16)

        @block.tensor
        def _(pe):
            q = Order(pe, "pe")
            mm = nc.tensor.matmul
            tr = nc.tensor.transpose

            def chunk(i):
                s = slot_of[i]
                pe.wait_ge(ld[s], q.l * (16 * loads[s]) + 16 * nth[i])
                return s

            def tokens_major(dst, src, w, nk):
                for k in range(nk):
                    ins = mm(dst, src(k), w(k), start=(k == 0), stop=(k == nk - 1))
                return ins

            def transposes(need_h):
                for t in range(TB):
                    need_h(t)
                    if t == 0:
                        continue
                    for j in range(4):
                        for k in (2 * j, 2 * j + 1):
                            for tb in range(TB):
                                ins = tr(bank[4 + j][:, (k % 2) * S + tb * P:(k % 2) * S + tb * P + P],
                                         h[:, tb, k::KD], ident[:])
                        q.done(ins, "tp_mm")

            pe.wait_ge(sem("ident_ready"), 1)
            for tb in range(TB):
                pe.wait_ge(sem("m_h_ready"), tb + 1)
            for j in range(4):
                for k in (2 * j, 2 * j + 1):
                    for tb in range(TB):
                        ins = tr(bank[4 + j][:, (k % 2) * S + tb * P:(k % 2) * S + tb * P + P],
                                 h[:, tb, k::KD], ident[:])
                ins.then_inc(sem("m_tp_mm"), 1)
            pe.wait_ge(sem("m_tp_v"), 4)

            with pe.Fori(0, L) as l:
                q.enter(l, 64)
                transposes(lambda t: q.need("h_ready", t + 1))
                q.need("tp_v", 2)
                q.need("tp_a", 2)

                def feature_major(dst, s, n, c0, m=P, src=hT):
                    w = slot(s, KD, n)
                    for k in range(KD):
                        ins = mm(dst, w[:, k, c0:c0 + m], src[:, k, :], start=(k == 0), stop=(k == KD - 1))
                    return ins

                def token_major(dst, s, n, c0, c1, tb, src=hT):
                    w = slot(s, KD, n)
                    for k in range(KD):
                        ins = mm(dst, src[:, k, tb * P:tb * P + P], w[:, k, c0:c1], start=(k == 0), stop=(k == KD - 1))
                    return ins

                s = chunk(0)
                for tb in range(TB):
                    q.done(token_major(bank[tb][:, 0:424], s, 424, 0, 424, tb), "mix_mm")
                pe.sem_inc(sem("used"), 1) if False else None
                mark = []

                def used(ins):
                    pass
                q.need("mix_mm", 2)
                q.done(pe, "used") if False else pe.sem_inc(sem("used"), 1)
                s = chunk(1)
                for j in range(2):
                    ins = feature_major(bank[2][:, j * S:j * S + S], s, 512, j * P)
                q.done(ins, "mix_mm")
                for tb in range(TB):
                    ins = token_major(bank[3][:, tb * W:tb * W + W], s, 512, 256, 512, tb)
                q.done(ins, "mix_mm")
                q.need("mix_mm", 4)
                pe.sem_inc(sem("used"), 1)
                s = chunk(2)
                for b in range(2):
                    for j in range(2):
                        ins = feature_major(bank[4 + b][:, j * S:j * S + S], s, 512, (2 * b + j) * P)
                    q.done(ins, "mix_mm")
                q.need("mix_mm", 6)
                pe.sem_inc(sem("used"), 1)
                s = chunk(3)
                for j in range(2):
                    ins = feature_major(bank[6][:, j * S:j * S + S], s, 512, j * P)
                q.done(ins, "mix_mm")
                for tb in range(TB):
                    ins = token_major(bank[7][:, tb * W:tb * W + W], s, 512, 256, 512, tb)
                q.done(ins, "mix_mm")
                q.need("mix_mm", 8)
                pe.sem_inc(sem("used"), 1)
                s = chunk(4)
                q.need("mix_ev", 1)
                for tb in range(TB):
                    ins = token_major(bank[0][:, tb * W:tb * W + W], s, 272, 0, 256, tb)
                q.done(ins, "mix_mm")
                q.need("mix_ev", 2)
                q.done(feature_major(bank[1][0:16, 0:S], s, 272, 256, m=16), "mix_mm")
                q.need("mix_mm", 10)
                pe.sem_inc(sem("used"), 1)
                s = chunk(5)
                for b in range(2):
                    q.need("mix_ev", 3 + b)
                    for j in range(2):
                        ins = feature_major(bank[2 + b][:, j * S:j * S + S], s, 512, (2 * b + j) * P)
                    q.done(ins, "mix_mm")
                q.need("mix_mm", 12)
                pe.sem_inc(sem("used"), 1)

                def gates(g):
                    s = chunk(DENSE.index(f"g{g}"))
                    for tb in range(TB):
                        b = 2 * (g % 2) + tb
                        if g in (0, 1):
                            q.need("mix_ev", 9 + b)
                        elif g == 4:
                            q.need("mg_ev", 8)
                        elif g != 5:
                            q.need("gate_ev", 2 * (g - 2) + tb + 1)
                        q.done(token_major(bank[b][:], s, 512, 0, 512, tb), "gate_mm")
                    q.need("gate_mm", 2 * g + 2)
                    pe.sem_inc(sem("used"), 1)

                q.need("rope", 1)
                q.need("mix_ev", 7)
                for hp in range(2):
                    for tb in range(TB):
                        ins = tr(bank[4][:, hp * S + tb * P:hp * S + tb * P + P], dq[:, tb, hp * P:hp * P + P], ident[:])
                q.done(ins, "sa_mm")
                for tb in range(TB):
                    tr(bank[5][:, tb * P:tb * P + P], kk[:, tb].rearrange("p a b -> p (a b)"), ident[:])
                for tb in range(TB):
                    ins = tr(bank[5][:, S + tb * P:S + tb * P + P], ki4[:, tb].rearrange("p a b -> p (a b)"), ident[:])
                q.done(ins, "sa_mm")
                for hp in range(2):
                    for tb in range(TB):
                        ins = tr(bank[6][:, hp * S + tb * P:hp * S + tb * P + P],
                                 dt_[:, tb, 128 + hp * P:128 + hp * P + P], ident[:])
                q.done(ins, "sa_mm")
                q.need("mix_ev", 10)
                for j in range(2):
                    ins = mm(bank[7][:, j * S:j * S + S], a_up[:, j * P:j * P + P], alow[:, :], start=True, stop=True)
                q.done(ins, "la_mm")
                gates(0)
                q.need("sa_ev", 3)
                q.need("la_ev", 1)
                for hq in range(8):
                    r = 32 * (hq % 4)
                    ins = mm(bank[4 + hq % 4][:, (hq // 4) * S:(hq // 4) * S + S], qiT[r:r + 32, hq // 4, P:2 * P],
                             kTd[r:r + 32, 1, :], start=True, stop=True)
                    if hq >= 4:
                        q.done(ins, "ix_mm")
                for hq in range(8):
                    r = 32 * (hq % 4)
                    if hq < 4:
                        q.need("ix_ev", 1 + hq)
                    ins = mm(bank[4 + hq % 4][:, (hq // 4) * P:(hq // 4) * P + P], qiT[r:r + 32, hq // 4, 0:P],
                             kTd[r:r + 32, 1, 0:P], start=True, stop=True)
                    if hq >= 4:
                        q.done(ins, "ix_mm")
                gates(1)
                q.need("b2_ready", 1)
                q.need("ix_ev", 8)
                for ri in range(2):
                    for hf_ in range(2):
                        ins = tr(bank[7][:, (ri * 2 + hf_) * P:(ri * 2 + hf_) * P + P],
                                 b2[:, ri, 4 * hf_:4 * hf_ + 4].rearrange("p t g c -> p (t g c)"), ident[:])
                q.done(ins, "bt_mm")
                for ri in range(2):
                    for hf_ in range(2):
                        ins = tr(bank[6][:, (ri * 2 + hf_) * P:(ri * 2 + hf_) * P + P],
                                 c2[:, ri, hf_].rearrange("p g s -> p (g s)"), ident[:])
                q.done(ins, "ct_mm")
                q.need("gla_qk", 1)
                q.need("ix_ev", 8)
                for odd in range(2):
                    r = 64 * odd
                    for tb in range(TB):
                        c = slice(tb * P, tb * P + P)
                        for hd in (odd, odd + 2):
                            ins = mm(bank[4 + tb][:, hd * P:hd * P + P], en[r:r + 64, hd // 2, c],
                                     gq[r:r + 64, hd // 2, c], start=True, stop=True)
                        if odd:
                            q.done(ins, "att_mm")
                    if not odd:
                        q.link(ins)
                gates(2)
                q.need("bc_ev", 2)
                for tb in range(TB):
                    for j in range(2):
                        ins = tr(bank[6][:, tb * W + j * P:tb * W + j * P + P], ke[:, j, tb * P:tb * P + P], ident[:])
                q.done(ins, "ketok_mm")
                q.need("ketok_ev", 1)
                q.need("att_ev", 2)
                for odd in range(2):
                    r = 64 * odd
                    for hd in (odd, odd + 2):
                        ins = mm(bank[5][:, hd * P:hd * P + P], qTd[r:r + 64, hd // 2, 0:P], kTd[r:r + 64, 0, 0:P],
                                 start=True, stop=True)
                    if odd:
                        q.done(ins, "dl_mm")
                    for hd in (odd, odd + 2):
                        ins = mm(bank[6 + hd // 2][:, odd * S:odd * S + S], qTd[r:r + 64, hd // 2, P:2 * P],
                                 kTd[r:r + 64, 0, :], start=True, stop=True)
                        if odd:
                            q.done(ins, "dl_mm")
                    if not odd:
                        q.link(ins)
                for n in (0, 2, 1):
                    if n == 1:
                        q.link(ins)
                    r = 64 * (n % 2)
                    for hd in range(4):
                        ins = mm(bank[4][64 * (hd % 2):64 * (hd % 2) + 64, n * P + (hd // 2) * 64:n * P + (hd // 2) * 64 + 64],
                                 ketok[r:r + 64, n // 2, hd * 64:hd * 64 + 64], gv[r:r + 64, n // 2, hd * 64:hd * 64 + 64],
                                 start=True, stop=True)
                q.done(ins, "u_mm")
                gates(3)
                q.need("st_ready", 1)
                q.need("dl_ev", 1)
                for tb in range(TB):
                    for hd in range(4):
                        c = slice(hd * 64, hd * 64 + 64)
                        mm(bank[4 + tb][:, c], attm[:, tb, hd, :], gv[:, tb, c], start=(hd == 0), stop=False,
                           skip_group_check=True)
                    for half in range(2):
                        n = 2 * tb + half
                        if n == 0:
                            continue
                        for hp in range(2):
                            ins = mm(bank[4 + tb][64 * half:64 * half + 64, hp * P:hp * P + P],
                                     gq[:, hp, n * 64:n * 64 + 64], state[:, n - 1, hp, :],
                                     start=False, stop=(half == 1 and hp == 1), skip_group_check=True)
                    q.done(ins, "o_mm")
                q.need("p_ready", 1)
                q.need("dl_ev", 3)
                for u, b in ((0, 6), (1, 7), (2, 4)):
                    if b == 4:
                        q.need("o_done", 1)
                    for hd in range(4):
                        src = dl[:, 0, hd * P:hd * P + P] if u == 0 else \
                            dl[:, 1:3].rearrange("p a (g s) -> p (a g) s", s=S)[:, hd, (u - 1) * P:u * P]
                        ins = tr(bank[b][:, hd * P:hd * P + P], src, ident[:])
                    q.done(ins, "pt_mm")
                q.need("pt_ev", 3)
                for hd in range(4):
                    r = 64 * (hd % 2)
                    c = (hd // 2) * S
                    mm(bank[5][r:r + 64, c:c + P], dt_[:, 0, 64:128], pT[:, 0, hd, :], start=True, stop=True)
                    mm(bank[5][r:r + 64, c + P:c + S], dt_[:, 0, 64:128], pT[:, 1, hd, :], start=True, stop=False)
                    ins = mm(bank[5][r:r + 64, c + P:c + S], dt_[:, 1, 64:128], pT[:, 2, hd, :], start=False, stop=True)
                q.done(ins, "od_mm")
                for j in range(2):
                    for tb in range(TB):
                        ins = tr(bank[6][:, j * S + tb * P:j * S + tb * P + P], za[:, tb, j * P:j * P + P], ident[:])
                q.done(ins, "ybt_mm")

                def cross_keys():
                    s = chunk(DENSE.index("ckv0"))
                    for b in range(2):
                        q.need("gate_ev", 5 + b)
                        for j in range(2):
                            ins = feature_major(bank[b][:, j * S:j * S + S], s, 512, (2 * b + j) * P, src=memT)
                        q.done(ins, "ckv_mm")
                    q.need("ckv_mm", 2)
                    pe.sem_inc(sem("used"), 1)

                def cross_values():
                    s = chunk(DENSE.index("ckv1"))
                    for tb in range(TB):
                        q.need("gate_ev", 7 + tb)
                        q.done(token_major(bank[2 + tb][:], s, 512, 0, 512, tb, src=memT), "ckv_mm")
                    q.need("ckv_mm", 4)
                    pe.sem_inc(sem("used"), 1)

                def drive(t):
                    b = (4, 7)[t % 2]
                    r = 32 * (t % 4)
                    if t >= 2:
                        q.need("bu_ev", t - 1)
                    for ri in range(2):
                        ins = mm(bank[b][:, ri * S:ri * S + S], bT[r:r + 32, ri, t // 4, :], uT[r:r + 32, t // 4, :],
                                 start=True, stop=True)
                    q.done(ins, "bu_mm")

                def read_out(t):
                    r = 32 * (t % 4)
                    q.need("xs", t + 1)
                    if t == 0:
                        q.need("od_ev", 1)
                    for ri in range(2):
                        ins = mm(bank[5][r:r + 32, (t // 4) * S:(t // 4) * S + S], cT[:, ri, t // 4, r:r + 32],
                                 xb[:, t % 2, ri, :], start=(ri == 0), stop=(ri == 1))
                    q.done(ins, "yk")

                for t in range(8):
                    drive(t)
                    if t >= 1:
                        read_out(t - 1)
                    if t == 2:
                        cross_keys()
                    if t == 4:
                        cross_values()
                read_out(7)
                q.need("gelu", 1)
                q.need("ybt_ev", 1)
                for j in range(2):
                    for k in range(2):
                        ins = mm(bank[6][:, j * S:j * S + S], w_glu[:, k, j * P:j * P + P], gel[:, k, :],
                                 start=(k == 0), stop=(k == 1))
                q.done(ins, "glu_mm")

                def merge(i):
                    src = (yaT, ybT, ycT, ydT)[i]
                    s = slot_of[DENSE.index("br01" if i < 2 else "br23")]
                    w = slot(s, 4, D)
                    for tb in range(TB):
                        for nh in range(2):
                            n = i * 4 + tb * 2 + nh
                            if n < 4:
                                q.need("ckv_ev", n + 1)
                            elif i == 2:
                                q.need("gate_ev", 13 + tb * 2 + nh)
                            else:
                                q.need("mg_ev", n - 3)
                            for j in range(2):
                                ins = mm(bank[n % 4][:], src[:, j, tb * P:tb * P + P],
                                         w[:, (i % 2) * 2 + j, nh * 512:nh * 512 + 512], start=(j == 0), stop=(j == 1))
                            q.done(ins, "mg_mm")
                    if i % 2:
                        q.need("mg_mm", i * 4 + 4)
                        pe.sem_inc(sem("used"), 1)

                chunk(DENSE.index("br01"))
                q.need("u_conv", 1)
                merge(0)
                merge(1)
                for g in range(4, 8):
                    gates(g)
                chunk(DENSE.index("br23"))
                q.need("yc", 1)
                merge(2)
                merge(3)
                q.need("glu_ev", 2) if False else None
                q.need("mg_add", 16)
                transposes(lambda t: None)
                q.need("tp_v", 4)
                q.need("tp_a", 4)
                for nh in range(2):
                    i = DENSE.index(f"wo{nh}")
                    s = chunk(i)
                    for tb in range(TB):
                        if nh == 0:
                            q.need("mg_ev", 13 + tb)
                        else:
                            q.need("mg_ev", 15 + tb)
                        q.done(token_major(bank[2 * nh + tb][:], s, 512, 0, 512, tb), "wo_mm")
                    q.need("wo_mm", 2 * nh + 2)
                    pe.sem_inc(sem("used"), 1)

                transposes(lambda t: q.need("h_ready", 3 + t))
                q.need("tp_v", 6)
                q.need("tp_a", 6)
                s = chunk(DENSE.index("cq"))
                for b in range(2):
                    for j in range(2):
                        ins = feature_major(bank[b][:, j * S:j * S + S], s, 512, (2 * b + j) * P)
                    q.done(ins, "cq_mm")
                q.need("cq_mm", 2)
                pe.sem_inc(sem("used"), 1)
                q.need("cq_ev", 2)
                for tb in range(TB):
                    for hd in range(4):
                        ins = mm(bank[4 + 2 * tb + hd // 2][:, (hd % 2) * S:(hd % 2) * S + S],
                                 qTx[:, hd, tb * P:tb * P + P], kTx[:, hd, :], start=True, stop=True)
                        if hd % 2:
                            q.done(ins, "cl_mm")
                q.need("cp", 1)
                for mb in range(2):
                    for hp in range(2):
                        for hd in (2 * hp, 2 * hp + 1):
                            for tb in range(TB):
                                ins = tr(bank[mb * 2 + hp][:, (hd % 2) * S + tb * P:(hd % 2) * S + tb * P + P],
                                         px[:, tb, hd, mb * P:mb * P + P], ident[:])
                        q.done(ins, "cpt_mm")
                q.need("cpt_ev", 4)
                for hp in range(2):
                    for hd in (2 * hp, 2 * hp + 1):
                        for mb in range(2):
                            ins = mm(bank[4 + hp][:, (hd % 2) * S:(hd % 2) * S + S], vx[:, mb, hd * P:hd * P + P],
                                     pTx[:, mb, hd, :], start=(mb == 0), stop=(mb == 1))
                    q.done(ins, "co_mm")
                q.need("co_ev", 2)
                s = chunk(DENSE.index("co"))
                w = slot(s, 4, D)
                for tb in range(TB):
                    for nh in range(2):
                        for hd in range(4):
                            ins = mm(bank[tb * 2 + nh][:], oTx[:, hd, tb * P:tb * P + P],
                                     w[:, hd, nh * 512:nh * 512 + 512], start=(hd == 0), stop=(hd == 3))
                        q.done(ins, "cy_mm")
                q.need("cy_mm", 4)
                pe.sem_inc(sem("used"), 1)

                transposes(lambda t: q.need("h_ready", 5 + t))
                q.need("tp_v", 8)
                q.need("tp_a", 8)
                for tb in range(TB):
                    for k in range(KD):
                        ins = mm(bank[0][:, tb * 20:tb * 20 + 20], hT[:, k, tb * P:tb * P + P], w_rt[:, k, :],
                                 start=(k == 0), stop=(k == KD - 1))
                q.done(ins, "rt_mm")
                q.need("rt_e1", 1)
                q.settle()
                q.need("hs", 1)
                sel_ = lambda tb: sel[:, tb].rearrange("p g e -> p (g e)")
                mm(bank[0][:, 0:16], tri[:], sel_(0), start=True, stop=True)
                mm(bank[0][:, 16:32], tri[:], sel_(1), start=True, stop=False)
                mm(bank[0][:, 16:32], ones[:], sel_(0), start=False, stop=True)
                mm(bank[0][:, 32:48], ones[:], sel_(0), start=True, stop=False)
                q.done(mm(bank[0][:, 32:48], ones[:], sel_(1), start=False, stop=True), "rank_mm")

                def split_products(dst, a_hi, a_lo, b_hi, b_lo, first, last):
                    mm(dst, a_hi, b_hi, start=first, stop=False)
                    mm(dst, a_hi, b_lo, start=False, stop=False)
                    return mm(dst, a_lo, b_hi, start=False, stop=last)

                def gather(p, e, banks_free):
                    q.need_turn("pick", p, e, 1)
                    if banks_free:
                        q.need_turn("x_acc", p, e - 1, 0)
                    for b in range(2):
                        for k in range(4 * b, 4 * b + 4):
                            for tb in range(TB):
                                mm(bank[b][:, (k % 4) * P:(k % 4) * P + P], hs_hi[:, tb, k::KD], pick[:, tb, :],
                                   start=(tb == 0), stop=False)
                                ins = mm(bank[b][:, (k % 4) * P:(k % 4) * P + P], hs_lo[:, tb, k::KD], pick[:, tb, :],
                                         start=False, stop=(tb == 1))
                        ins.then_inc(sem("ga_mm"), 1)

                def turn(p, e, first=False, last=False):
                    for j in range(2):
                        if j == 0:
                            q.need_turn("ga_lo", p, e, 2)
                        for i in range(4):
                            n = 4 * j + i
                            q.need_turn("w_lo", p, e, n + 1)
                            for k in (2 * i, 2 * i + 1):
                                c = slice((k % 2) * 512, (k % 2) * 512 + 512)
                                ins = split_products(bank[2 + j][:], ga_hi[:, k, :], ga_lo[:, k, :], w_hi[:, n % RP, c],
                                                     w_lo[:, n % RP, c], k == 0, k == KD - 1)
                            ins.then_inc(sem("w_used"), 1)
                        if j == 0:
                            for tb in range(TB):
                                ins = tr(bank[5][:, tb * P:tb * P + P], pick[:, tb, :].bitcast(F32), ident[:])
                            ins.then_inc(sem("pickT_mm"), 1)
                    if not last:
                        gather(p, e + 1, not first)
                    elif not first:
                        q.need_turn("x_acc", p, e, 0)
                    q.need_turn("hid", p, e, 1)
                    for t in range(4):
                        ins = tr(bank[4][:, t * P:t * P + P], hid[:, t::4], ident[:])
                    ins.then_inc(sem("hidT_mm"), 1)
                    q.need_turn("hidT_lo", p, e, 1)
                    q.need_turn("pickT", p, e, 1)
                    for t in range(4):
                        n = 8 + t
                        q.need_turn("w_lo", p, e, n + 1)
                        for nh in range(2):
                            c = slice(nh * 512, nh * 512 + 512)
                            ins = split_products(bank[5 + nh][:], hidT_hi[:, t, :], hidT_lo[:, t, :], w_hi[:, n % RP, c],
                                                 w_lo[:, n % RP, c], t == 0, t == 3)
                            if t == 3 and nh == 0:
                                ins.then_inc(sem("y_mm"), 1)
                        if t < 3:
                            ins.then_inc(sem("w_used"), 1)
                    ins.then_inc(sem("y_mm"), 1)
                    pe.wait_ge(sem("y_mm"), (l * PASSES + p) * (2 * N_EXP) + e * 2 + 2)
                    pe.sem_inc(sem("w_used"), 1)
                    for nh in range(2):
                        c = slice(nh * 512, nh * 512 + 512)
                        q.need_turn("y_lo", p, e, nh + 1)
                        if nh == 0 and not last:
                            q.need_turn("ga_lo", p, e + 1, 2)
                        for tb in range(TB):
                            b = SC_BANKS[nh * 2 + tb]
                            mm(bank[b][:], pickT[:, tb * P:tb * P + P], y_hi[:, c], start=True, stop=False)
                            mm(bank[b][:], pickT[:, tb * P:tb * P + P], y_lo[:, c], start=False,
                               stop=True).then_inc(sem("sc_mm"), 1)

                def one_pass(p):
                    if p == 1:
                        pe.wait_ge(sem("x_acc"), (l * PASSES + 1) * (4 * N_EXP))
                    gather(p, 0, False)
                    q.turns(p, turn)

                q.passes(one_pass, [(n, N_EXP * PER_TURN[n]) for n in
                                    ("ga_mm", "pickT_mm", "hidT_mm", "y_mm", "w_used", "sc_mm")])
                q.leave()

        @block.scalar
        def _(act):
            q = Order(act, "act")
            A = nc.scalar.activation

            def copy(dst, src, **kw):
                return A(dst, src, ACT.Copy, **kw)

            act.wait_ge(sem("mem_loaded"), 16)
            for tb in range(TB):
                A(kTx[:].rearrange("p a b -> p (a b)"), h[:, tb, :], ACT.Square,
                  accum_out=st[:, 0, tb:tb + 1]).then_inc(sem("m_sumsq"), 1)
                act.wait_ge(sem("m_sumsq"), tb + 1)
            act.wait_ge(sem("m_meansq"), 1)
            A(st[:, 2, :], st[:, 1, :], ACT.Sqrt).then_inc(sem("m_root"), 1)
            act.wait_ge(sem("ang_ready"), 1)
            A(rope_cs[:, 1].rearrange("p t f -> p (t f)"), rr[:, 0, :], ACT.Sin).then_inc(sem("rope_ready"), 1)
            A(rope_cs[:, 0].rearrange("p t f -> p (t f)"), rr[:, 1, :], ACT.Sin).then_inc(sem("rope_ready"), 1)
            act.wait_ge(sem("x_loaded"), 16)
            act.wait_ge(sem("m_tp_v"), 4)

            def norm_stats(u):
                for tb in range(TB):
                    q.done(A(kTx_junk(u), x[:, tb, :], ACT.Square, accum_out=st[:, 0, tb:tb + 1]), "sumsq")
                    q.need("sumsq", 2 * u + tb + 1)
                q.need("meansq", u + 1)
                q.done(A(st[:, 2, :], st[:, 1, :], ACT.Sqrt), "root")

            def kTx_junk(u):
                return h[:, 1, :]

            def norm_evacuate(u, g):
                for j in (1, 3):
                    q.need("tp_mm", 4 * u + j + 1)
                    for i in range(2):
                        k = 2 * j + i
                        ins = A(hT[:, k, :], bank[4 + j][:, i * S:i * S + S], ACT.Copy, scale=g_fm[:, g, k:k + 1])
                    q.done(ins, "tp_a")

            with act.Fori(0, L) as l:
                q.enter(l, 256)
                norm_stats(0)
                act.wait_ge(sem("par_loaded"), l * N_PAR * 16 + N_PAR * 16)
                q.link(A(sp[:, 0, :], lam[:, 2, :], ACT.Exp))
                q.done(A(junk[:], junk[:], ACT.Copy), "sp_in")
                q.need("sp2_in", 1)
                A(sp[:, 2, :], sp[:, 1, :], ACT.Exp)
                A(sp[:, 8, :], sp[:, 6, :], ACT.Sin)
                q.done(A(sp[:, 9, :], sp[:, 7, :], ACT.Sin), "sp2_out")
                norm_evacuate(0, 0)
                flat = lambda t: t[:].rearrange("p a b -> p (a b)")
                q.need("mix_mm", 1)
                q.done(copy(dt_[:, 0, :], bank[0][:, 0:424]), "mix_ev")
                q.need("mix_mm", 2)
                q.done(copy(dt_[:, 1, :], bank[1][:, 0:424]), "mix_ev")
                for n, (dst, b) in enumerate(((uT, 2), (dq, 3), (cc, 4), (gq, 5), (gk, 6), (gv, 7), (gr, 0))):
                    q.need("mix_mm", n + 3)
                    q.done(copy(flat(dst), bank[b][:]), "mix_ev")
                q.need("mix_mm", 10)
                q.done(copy(alow[:, :], bank[1][0:16, 0:S]), "mix_ev")
                for n, (dst, b) in enumerate(((ch, 2), (cb, 3))):
                    q.need("mix_mm", n + 11)
                    q.done(copy(flat(dst), bank[b][:]), "mix_ev")
                for n, (dst, b) in enumerate(((qTd, 4), (kTd, 5), (qiT, 6))):
                    q.need("sa_mm", n + 1)
                    q.done(copy(flat(dst), bank[b][:]), "sa_ev")

                def gate(g):
                    i = (g // 2) % 2
                    for tb in range(TB):
                        q.need("gate_mm", 2 * g + tb + 1)
                        if g == 4 and tb == 0:
                            q.need("mg_add", 8)
                        q.done(A(gs[:, tb, i, (g % 2) * 512:(g % 2) * 512 + 512], bank[2 * (g % 2) + tb][:], ACT.Sigmoid), "gate_ev")

                q.need("mix_ev", 9)
                q.done(A(flat(gr), flat(gr), ACT.Silu), "sr")
                q.need("ls_in", 1)
                q.link(A(flat(zb), flat(za), ACT.Abs))
                q.link(A(flat(zb), flat(zb), ACT.Exp, scale=-1.0))
                q.done(A(flat(zb), flat(zb), ACT.Ln, bias=1.0), "ls_ex")
                gate(0)
                for n in range(8):
                    q.need("ix_mm", n + 1)
                    if n >= 2:
                        q.need("ix_acc", n - 1)
                    c = slice(0, 2 * S if n < 4 else 2 * P)
                    q.done(A(rl[:, n % 2, c], bank[4 + n % 4][:, c], ACT.Relu), "ix_ev")
                gate(1)
                q.need("gla_cum", 1)
                A(flat(eb), flat(za), ACT.Exp, scale=1.0 / 16)
                A(flat(en), flat(za), ACT.Exp, scale=-1.0 / 16)
                q.done(A(flat(ke), flat(zb), ACT.Exp, scale=1.0 / 16), "gla_exp")
                q.need("bt_mm", 1)
                q.done(copy(bT[:].rearrange("p a b c -> p (a b c)"), bank[7][:]), "bc_ev")
                q.need("ct_mm", 1)
                q.done(copy(cT[:].rearrange("p a b c -> p (a b c)"), bank[6][:]), "bc_ev")
                gate(2)
                q.need("ketok_mm", 1)
                q.done(copy(flat(ketok), bank[6][:]), "ketok_ev")
                gate(3)
                for tb in range(TB):
                    q.need("mx", tb + 1)
                    for hd in range(4):
                        v = dl[:, 0, hd * P:hd * P + P] if tb == 0 else \
                            dl[:, 1:3].rearrange("p a (g s) -> p (a g) s", s=S)[:, hd, :]
                        ins = A(v, v, ACT.Exp, bias=dstat[:, 0, tb, hd:hd + 1], accum_out=dstat[:, 1, tb, hd:hd + 1])
                    q.done(ins, "ex")
                for tb in range(TB):
                    q.need("o_mm", tb + 1)
                    q.done(A(zb[:, tb, :], bank[4 + tb][:, 0:W], ACT.Square), "o_sq")
                q.need("o_ms", 1)
                q.done(A(ost[:, 1].rearrange("p a b -> p (a b)"), ost[:, 0].rearrange("p a b -> p (a b)"), ACT.Sqrt), "o_rt")
                for u, b in ((0, 6), (1, 7), (2, 4)):
                    q.need("pt_mm", u + 1)
                    q.done(copy(pT[:, u].rearrange("p a b -> p (a b)"), bank[b][:]), "pt_ev")
                q.need("od_mm", 1)
                q.done(copy(flat(ydT), bank[5][:]), "od_ev")
                q.need("ybt_mm", 1)
                q.done(copy(flat(ybT), bank[6][:]), "ybt_ev")
                for b in range(2):
                    q.need("ckv_mm", b + 1)
                    q.done(copy(kTx[:, 2 * b:2 * b + 2, :].rearrange("p a b -> p (a b)"), bank[b][:]), "ckv_ev")
                for b in range(2):
                    q.need("ckv_mm", b + 3)
                    q.done(copy(vx[:, b, :], bank[2 + b][:]), "ckv_ev")
                q.need("s5y", 1)
                q.done(A(flat(gel), flat(gel), ACT.Gelu_apprx_tanh), "gelu")
                q.need("glu_mm", 1)
                for j in range(2):
                    ins = A(ycT[:, j, :], bank[6][:, j * S:j * S + S], ACT.Sigmoid, bias=b_glu[:, j:j + 1])
                q.done(ins, "glu_ev")
                for g in range(4, 8):
                    gate(g)
                for j in (1, 3):
                    q.need("tp_mm", 4 + j + 1)
                    q.done(copy(hT[:, 2 * j:2 * j + 2, :].rearrange("p a b -> p (a b)"), bank[4 + j][:]), "tp_a")
                q.need("wo_ev", 4)
                norm_stats(1)
                norm_evacuate(2, 1)
                for b in range(2):
                    q.need("cq_mm", b + 1)
                    q.done(copy(qTx[:, 2 * b:2 * b + 2, :].rearrange("p a b -> p (a b)"), bank[b][:]), "cq_ev")
                q.need("cmx", 1)
                for tb in range(TB):
                    for hd in range(4):
                        ins = A(px[:, tb, hd, :], bank[4 + 2 * tb + hd // 2][:, (hd % 2) * S:(hd % 2) * S + S], ACT.Exp,
                                bias=cst[:, 0, tb, hd:hd + 1], scale=128 ** -0.5, accum_out=cst[:, 1, tb, hd:hd + 1])
                q.done(ins, "cex")
                for n in (1, 3):
                    q.need("cpt_mm", n + 1)
                    q.done(copy(pTx[:, n // 2, 2:4, :].rearrange("p a b -> p (a b)"), bank[n][:]), "cpt_a")
                for hp in range(2):
                    q.need("co_mm", hp + 1)
                    q.done(copy(oTx[:, 2 * hp:2 * hp + 2, :].rearrange("p a b -> p (a b)"), bank[4 + hp][:]), "co_ev")
                q.need("cy_ev", 4)
                norm_stats(2)
                norm_evacuate(3, 2)
                q.need("rt_x1", 1)
                A(rx[:, 2].rearrange("p a b -> p (a b)"), rx[:, 1].rearrange("p a b -> p (a b)"), ACT.Exp)
                q.done(A(rx[:, 7].rearrange("p a b -> p (a b)"), rx[:, 6].rearrange("p a b -> p (a b)"), ACT.Exp), "rt_x2")
                q.need("hs_f", 2)
                for tb in range(TB):
                    q.done(copy(hs_hi[:, tb, :], h[:, tb, :]), "hs_h")

                def pieces(p, e, js):
                    for j in js:
                        s_ = e_slot[j]
                        act.wait_ge(ld[s_], l * (16 * loads[s_]) + 16 * (dense_loads[s_] + p * N_EXP + 1) + e * 16)
                        for i in range(4):
                            n = 4 * j + i
                            q.need_turn("w_used", p, e, n + 1)
                            copy(w_hi[:, n % RP, :], ring[:, s_, i * PIECE:i * PIECE + PIECE]).then_inc(sem("w_hi"), 1)

                def gathered(p, e):
                    for b in range(2):
                        q.need_turn("ga_mm", p, e, b + 1)
                        copy(ga_hi[:, 4 * b:4 * b + 4, :].rearrange("p a b -> p (a b)"),
                             bank[b][:]).then_inc(sem("ga_hi"), 1)

                def turn(p, e, first=False, last=False):
                    pieces(p, e, (1,))
                    q.need_turn("pickT_mm", p, e, 1)
                    copy(pickT[:, :], bank[5][:, 0:S]).then_inc(sem("pickT"), 1)
                    pieces(p, e, (2,))
                    act.wait_ge(sem("w_used"), (l * PASSES + p) * (12 * N_EXP) + e * 12 + 8 + RP)
                    A(act_g[:, :], bank[2][:], ACT.Silu).then_inc(sem("act_gate"), 1)
                    if not last:
                        gathered(p, e + 1)
                    q.need_turn("hidT_mm", p, e, 1)
                    copy(hidT_hi[:].rearrange("p a b -> p (a b)"), bank[4][:]).then_inc(sem("hidT_hi"), 1)
                    if not last:
                        pieces(p, e + 1, (0,))
                    for nh in range(2):
                        q.need_turn("y_mm", p, e, nh + 1)
                        copy(y_hi[:, nh * 512:nh * 512 + 512], bank[5 + nh][:]).then_inc(sem("y_hi"), 1)

                def one_pass(p):
                    gathered(p, 0)
                    pieces(p, 0, (0,))
                    q.turns(p, turn)

                q.passes(one_pass, [(n, N_EXP * PER_TURN[n]) for n in
                                    ("w_hi", "ga_hi", "pickT", "act_gate", "hidT_hi", "y_hi")])
                act.wait_ge(sem("x_acc"), l * (PASSES * N_EXP * 4) + PASSES * N_EXP * 4)
                q.leave()
            for tb in range(TB):
                A(h[:, tb, :], x[:, tb, :], ACT.Square, accum_out=st[:, 0, tb:tb + 1]).then_inc(sem("f_sumsq"), 1)
            act.wait_ge(sem("f_meansq"), 1)
            A(st[:, 2, :], st[:, 1, :], ACT.Sqrt).then_inc(sem("f_root"), 1)

        @block.gpsimd
        def _(pool):
            q = Order(pool, "pool")
            g = nc.gpsimd

            def load(dst, src, name):
                pool.dma_start(dst, src, allow_slow_non_contiguous=True).then_inc(sem(name), 16)

            load(h[:], T["mem"].rearrange("o (t p) n -> p (o t) n", p=P), "mem_loaded")
            load(pos_i[:], T["positions"].rearrange("o (t p) -> p (o t)", p=P), "pos_loaded")
            load(g_fm[:, 3, :], T["norm_mem"].rearrange("(p k) -> p k", p=P), "gm_loaded")
            q.link(g.memset(ident[:], 0.0))
            g.affine_select(out=ident[:], in_=ident[:], compare_op=ALU.not_equal, fill=1.0, base=0,
                            pattern=[[-1, P]], channel_multiplier=1).then_inc(sem("ident_ready"), 1)
            q.link(g.memset(gla_mask[:], 1.0))
            q.link(g.memset(ones[:], 1.0))
            q.link(g.affine_select(out=tri[:], in_=ones[:], compare_op=ALU.is_ge, fill=0.0, base=0,
                                   pattern=[[1, P]], channel_multiplier=-1))
            q.link(g.iota(slot_no[:], pattern=[[1, P]], base=0, channel_multiplier=0,
                          allow_small_or_imprecise_dtypes=True))
            q.link(g.affine_select(out=gla_mask[:], in_=gla_mask[:], compare_op=ALU.is_ge, fill=0.0, base=0,
                                   pattern=[[1, P]], channel_multiplier=-1))
            q.link(g.affine_select(out=gla_mask[:, 64:128], in_=gla_mask[:, 64:128], compare_op=ALU.is_ge, fill=0.0,
                                   base=-64, pattern=[[0, 64]], channel_multiplier=1))
            q.link(g.memset(cneg[:], 0.0))
            q.link(g.affine_select(out=cneg[:], in_=cneg[:], compare_op=ALU.is_ge, fill=NEG, base=0,
                                   pattern=[[-1, P]], channel_multiplier=1))
            q.link(g.memset(scan_keep[:], 1.0))
            q.link(g.memset(scan_keep[:].rearrange("p (c j) -> p c j", j=64)[:, :, 0], 0.0))
            q.link(g.memset(mask_b[0:64, 0:1], 1.0))
            q.link(g.memset(mask_b[64:128, 0:1], 0.0))
            q.link(g.memset(mask_b[0:64, 1:2], 0.0))
            q.link(g.memset(mask_b[64:128, 1:2], 1.0))
            g.memset(junk[:], 0.0)
            g.iota(mc_i[:], pattern=[[0, 1]], base=0, channel_multiplier=1).then_inc(sem("masks_ready"), 1)

            with pool.Fori(0, L) as l:
                q.enter(l, 256)
                q.need("ffn_done", 1)
                one = bass.ds(l, 1)
                fm = lambda t: t[one].rearrange("o (p k) -> p (o k)", p=P)
                jp = lambda t: t[one].rearrange("o (j p) -> p (o j)", p=P)

                def par(dst, src):
                    load(dst, src, "par_loaded")
                par(g_fm[:, 0, :], fm(T["norm_mix"]))
                for i, n in enumerate(("s5_lambda_re", "s5_lambda_im")):
                    par(lam[:, i, :], T[n][one].rearrange("o (t g) s -> (g s) (o t)", g=2))
                for g2 in range(2):
                    par(lam[64 * g2:64 * g2 + 64, 2, :],
                        T["s5_log_dt"][one].rearrange("o (t g) -> g (o t)", g=2)[g2:g2 + 1].broadcast_to([64, 8]))
                for i, n in enumerate(("s5_b_re", "s5_b_im")):
                    par(s5_b[:, i], T[n][one].rearrange("o (t g) s c -> (g s) (o t) c", g=2))
                for i, n in enumerate(("s5_c_re", "s5_c_im")):
                    par(s5_c[:, i], T[n][one].rearrange("o (a g) c s -> (g c) (o a) s", a=2))
                par(g_fm[:, 1, :], fm(T["norm_cross"]))
                par(g_fm[:, 2, :], fm(T["norm_ffn"]))
                par(conv_w[:], T["conv_w"][one].rearrange("o k (j p) -> p (o k) j", p=P))
                par(conv_b[:], jp(T["conv_b"]))
                par(a_up[:], T["gla_a_up"][one].rearrange("o r n -> r (o n)"))
                par(a_b[:], jp(T["gla_a_b"]))
                par(gla_g[:], T["gla_norm"][one].broadcast_to([P, W]))
                par(s5_d[:], jp(T["s5_d"]))
                par(b_glu[:], jp(T["s5_b_glu"]))
                par(w_glu[:], T["s5_w_glu"][one].rearrange("o (k p) n -> p (o k) n", p=P))
                par(b_rt[:, 0:4], T["b_route_group"][one].broadcast_to([P, 4]))
                par(b_rt[:, 4:20], T["b_route_expert"][one].broadcast_to([P, 16]))
                par(w_rt[:, :, 0:4], T["w_route_group"][one].rearrange("o (p k) n -> p (o k) n", p=P))
                par(w_rt[:, :, 4:20], T["w_route_expert"][one].rearrange("o (p k) n -> p (o k) n", p=P))

                q.need("e_in", 1)
                q.link(g.memset(E[:, 0, :, 0:1], 1.0))
                q.link(g.memset(E[:, 1, :, 0:1], 0.0))
                m = 1
                tA, tB = h[:, 0, :], h[:, 1, :]
                q.need("h_free", 1)
                while m < S:
                    for t0 in range(0, 8, 8):
                        mm_ = m
                        for r in range(2):
                            a = E[:, r, :, 0:mm_]
                            wre = bc(wpow[:, 0, :].unsqueeze(2), [P, 8, mm_])
                            wim = bc(wpow[:, 1, :].unsqueeze(2), [P, 8, mm_])
                            ta = tA[:, 0:8 * mm_].rearrange("p (t s) -> p t s", t=8)
                            tb_ = tB[:, 0:8 * mm_].rearrange("p (t s) -> p t s", t=8)
                            if r == 0:
                                g.tensor_tensor(ta, E[:, 0, :, 0:mm_], wre, ALU.mult)
                                q.link(g.tensor_tensor(tb_, E[:, 1, :, 0:mm_], wim, ALU.mult))
                                q.link(g.tensor_tensor(E[:, 0, :, m:2 * m], ta, tb_, ALU.subtract))
                            else:
                                g.tensor_tensor(ta, E[:, 0, :, 0:mm_], wim, ALU.mult)
                                q.link(g.tensor_tensor(tb_, E[:, 1, :, 0:mm_], wre, ALU.mult))
                                q.link(g.tensor_tensor(E[:, 1, :, m:2 * m], ta, tb_, ALU.add))
                    g.tensor_tensor(wtmp[:, 0, :], wpow[:, 0, :], wpow[:, 0, :], ALU.mult)
                    g.tensor_tensor(wtmp[:, 1, :], wpow[:, 1, :], wpow[:, 1, :], ALU.mult)
                    q.link(g.tensor_tensor(wtmp[:, 2, :], wpow[:, 0, :], wpow[:, 1, :], ALU.mult))
                    g.tensor_tensor(wpow[:, 0, :], wtmp[:, 0, :], wtmp[:, 1, :], ALU.subtract)
                    q.link(g.tensor_tensor(wpow[:, 1, :], wtmp[:, 2, :], wtmp[:, 2, :], ALU.add))
                    m *= 2
                q.done(g.memset(junk[:], 0.0), "e_tab")
                q.need("mix_ev", 12)
                q.link(g.tensor_tensor(ch[:], ch[:], cc[:], ALU.mult))
                for j in range(2):
                    u, y = ch[:, j, :], yaT[:, j, :]
                    t = cc[:, j, :]
                    q.link(g.tensor_scalar(y, u, conv_w[:, 2, j:j + 1], conv_b[:, j:j + 1], ALU.mult, ALU.add))
                    for d in (1, 2):
                        q.link(g.tensor_scalar(t[:, 0:S - d], u[:, 0:S - d], conv_w[:, 2 - d, j:j + 1], None, ALU.mult))
                        q.link(g.tensor_tensor(y[:, d:S], y[:, d:S], t[:, 0:S - d], ALU.add))
                q.done(g.tensor_tensor(yaT[:], yaT[:], cb[:], ALU.mult), "u_conv")
                for t in range(8):
                    q.need("z_out", t + 1)
                    if t >= 2:
                        q.need("yk", t - 1)
                    g.tensor_tensor(gel[:], zo, bc(E[:, 0:1, t, :], [P, 2, S]), ALU.mult)
                    q.link(g.tensor_tensor(ycT[:], zo, bc(E[:, 1:2, t, :], [P, 2, S]), ALU.mult))
                    q.link(g.tensor_tensor(xb[:, t % 2, 0, :], gel[:, 0, :], ycT[:, 1, :], ALU.subtract))
                    q.done(g.tensor_tensor(xb[:, t % 2, 1, :], gel[:, 1, :], ycT[:, 0, :], ALU.add), "xs")
                    q.need("xs", t + 1)
                for n in range(16):
                    i, tb, nh = n // 4, (n // 2) % 2, n % 2
                    q.need("mg_ev", n + 1)
                    src = gs[:, tb, i % 2, nh * 512:nh * 512 + 512]
                    dst_ = h[:, tb, nh * 512:nh * 512 + 512]
                    if i == 0:
                        q.done(g.tensor_copy(dst_, src), "mg_add")
                    else:
                        q.need("mg_add", n - 3)
                        q.done(g.tensor_tensor(dst_, dst_, src, ALU.add), "mg_add")
                q.need("cy_ev", 4)
                load(g_bc[:], T["norm_ffn"][one].broadcast_to([P, D]), "g_loaded")
                q.leave()
            pool.wait_ge(sem("ffn_done"), L + 1)
            load(g_out, T["norm_final"].rearrange("(o n) -> o n", o=1).broadcast_to([P, D]), "go_loaded")

        @block.vector
        def _(dve):
            q = Order(dve, "dve")
            v = nc.vector
            flat = lambda t: t[:].rearrange("p a b -> p (a b)")
            flat3 = lambda t: t[:].rearrange("p a b c -> p (a b c)")
            link = q.link

            dve.sem_inc(sem("ffn_done"), 1)
            dve.sem_inc(sem("split"), NS)
            dve.sem_inc(sem("w_used"), RP)
            dve.wait_ge(sem("m_sumsq"), 2)
            v.tensor_scalar(st[:, 1, :], st[:, 0, :], 1.0 / D, EPS, ALU.mult, ALU.add).then_inc(sem("m_meansq"), 1)
            inv = (500000.0 ** (-np.arange(8) * 0.125)).astype(np.float32)
            for i in range(8):
                v.memset(invf[:, i:i + 1], float(inv[i]))
            dve.wait_ge(sem("pos_loaded"), 16)
            link(v.tensor_copy(pos_f[:], pos_i[:]))
            link(v.tensor_tensor(ang[:], bc(pos_f[:].unsqueeze(2), [P, TB, 8]),
                                 bc(invf[:].unsqueeze(1), [P, TB, 8]), ALU.mult))

            def reduce_angle(a, r_sin, r_cos, t0, t1):
                magic = 1.5 * 2.0 ** 23
                c1 = 6.28125
                c2 = float(np.float32(2 * np.pi - c1)) if False else 0.0019350051879882812
                c3 = float(2 * np.pi - c1 - c2)
                link(v.tensor_scalar(t0, a, 1.0 / (2 * PI), magic, ALU.mult, ALU.add))
                link(v.tensor_scalar(t0, t0, magic, None, ALU.subtract))
                link(v.scalar_tensor_tensor(out=t1, in0=t0, scalar=-c1, in1=a, op0=ALU.mult, op1=ALU.add))
                link(v.scalar_tensor_tensor(out=t1, in0=t0, scalar=-c2, in1=t1, op0=ALU.mult, op1=ALU.add))
                link(v.scalar_tensor_tensor(out=t1, in0=t0, scalar=-c3, in1=t1, op0=ALU.mult, op1=ALU.add))
                link(v.tensor_scalar(r_sin, t1, 3.1415925, -3.1415925, ALU.min, ALU.max))
                link(v.scalar_tensor_tensor(out=t0, in0=t1, scalar=-1.0, in1=t1, op0=ALU.mult, op1=ALU.max))
                link(v.tensor_scalar(r_cos, t0, -1.0, PI / 2, ALU.mult, ALU.add))

            reduce_angle(ang[:].rearrange("p t f -> p (t f)"), rr[:, 0, :], rr[:, 1, :], rr[:, 2, :], rr[:, 3, :])
            dve.sem_inc(sem("ang_ready"), 1)
            dve.wait_ge(sem("masks_ready"), 1)
            link(v.tensor_scalar(mc_j[:], mc_i[:], 4, 1, ALU.logical_shift_right, ALU.bitwise_and))
            link(v.tensor_copy(mask_c[:, 1:2], mc_j[:]))
            link(v.tensor_scalar(mask_c[:, 0:1], mask_c[:, 1:2], -1.0, 1.0, ALU.mult, ALU.add))
            dve.wait_ge(sem("m_root"), 1)
            link(v.reciprocal(st[:, 3, :], st[:, 2, :]))
            for tb in range(TB):
                v.tensor_scalar(h[:, tb, :], h[:, tb, :], st[:, 3, tb:tb + 1], None, ALU.mult).then_inc(sem("m_h_ready"), 1)
            dve.wait_ge(sem("gm_loaded"), 16)
            for j in range(4):
                dve.wait_ge(sem("m_tp_mm"), j + 1)
                v.tensor_tensor(memT[:, 2 * j:2 * j + 2, :], bank[4 + j][:].rearrange("p (k s) -> p k s", k=2),
                                bc(g_fm[:, 3, 2 * j:2 * j + 2].unsqueeze(2), [P, 2, S]), ALU.mult).then_inc(sem("m_tp_v"), 1)
            dve.wait_ge(sem("rope_ready"), 2)

            def norm_h(u):
                q.need("sumsq", 2 * u + 2)
                q.done(v.tensor_scalar(st[:, 1, :], st[:, 0, :], 1.0 / D, EPS, ALU.mult, ALU.add), "meansq")
                q.need("root", u + 1)
                link(v.reciprocal(st[:, 3, :], st[:, 2, :]))
                for tb in range(TB):
                    q.done(v.tensor_scalar(h[:, tb, :], x[:, tb, :], st[:, 3, tb:tb + 1], None, ALU.mult), "h_ready")

            def norm_evacuate(u, g):
                for j in (0, 2):
                    q.need("tp_mm", 4 * u + j + 1)
                    q.done(v.tensor_tensor(hT[:, 2 * j:2 * j + 2, :], bank[4 + j][:].rearrange("p (k s) -> p k s", k=2),
                                           bc(g_fm[:, g, 2 * j:2 * j + 2].unsqueeze(2), [P, 2, S]), ALU.mult), "tp_v")

            def top_k(w):
                for i in range(TOPK // 8):
                    q.settle()
                    link(v.max(top8[:], w))
                    q.settle()
                    link(v.match_replace(w, top8[:], w, TAKEN))

            def rope(t, half, step, n):
                a, b = t[:, :, :, 0:half], t[:, :, :, half:2 * half]
                cos = bc(rope_cs[:, 0, :, ::step].unsqueeze(2), [P, TB, n, half])
                sin = bc(rope_cs[:, 1, :, ::step].unsqueeze(2), [P, TB, n, half])
                r = [rp[:, i, :, 0:n * half].rearrange("p t (n f) -> p t n f", n=n) for i in range(4)]
                v.tensor_tensor(r[0], a, cos, ALU.mult)
                v.tensor_tensor(r[1], b, sin, ALU.mult)
                v.tensor_tensor(r[2], b, cos, ALU.mult)
                link(v.tensor_tensor(r[3], a, sin, ALU.mult))
                v.tensor_tensor(a, r[0], r[1], ALU.subtract)
                link(v.tensor_tensor(b, r[2], r[3], ALU.add))

            with dve.Fori(0, L) as l:
                q.enter(l, 512)
                norm_h(0)
                q.need("sp_in", 1)
                s_ = lambda i: sp[:, i, :]
                link(v.tensor_tensor(s_(1), lam[:, 0, :], s_(0), ALU.mult))
                link(v.tensor_tensor(s_(3), lam[:, 1, :], s_(0), ALU.mult))
                reduce_angle(s_(3), s_(6), s_(7), s_(4), s_(5))
                q.done(v.memset(s_(19), 0.0), "sp2_in")
                norm_evacuate(0, 0)
                q.need("sp2_out", 1)
                v.tensor_copy(wpow[:, 0, :], s_(9))
                q.done(v.tensor_copy(wpow[:, 1, :], s_(8)), "e_in")
                q.need("tp_mm", 4)
                dve.sem_inc(sem("h_free"), 1)
                link(v.tensor_tensor(s_(10), s_(2), s_(9), ALU.mult))
                link(v.tensor_tensor(s_(11), s_(2), s_(8), ALU.mult))
                link(v.tensor_scalar(s_(10), s_(10), 1.0, None, ALU.subtract))
                link(v.tensor_tensor(s_(12), lam[:, 0, :], lam[:, 0, :], ALU.mult))
                link(v.tensor_tensor(s_(13), lam[:, 1, :], lam[:, 1, :], ALU.mult))
                link(v.tensor_tensor(s_(12), s_(12), s_(13), ALU.add))
                link(v.reciprocal(s_(12), s_(12)))
                link(v.tensor_tensor(s_(13), s_(10), lam[:, 0, :], ALU.mult))
                link(v.tensor_tensor(s_(14), s_(11), lam[:, 1, :], ALU.mult))
                link(v.tensor_tensor(s_(13), s_(13), s_(14), ALU.add))
                link(v.tensor_tensor(s_(13), s_(13), s_(12), ALU.mult))
                link(v.tensor_tensor(s_(14), s_(11), lam[:, 0, :], ALU.mult))
                link(v.tensor_tensor(s_(15), s_(10), lam[:, 1, :], ALU.mult))
                link(v.tensor_tensor(s_(14), s_(14), s_(15), ALU.subtract))
                link(v.tensor_tensor(s_(14), s_(14), s_(12), ALU.mult))
                fr = bc(s_(13).unsqueeze(2), [P, 8, 16])
                fi = bc(s_(14).unsqueeze(2), [P, 8, 16])
                t4 = [rl[:, 0, i * 128:i * 128 + 128].rearrange("p (t c) -> p t c", t=8) for i in range(4)]
                v.tensor_tensor(t4[0], s5_b[:, 0], fr, ALU.mult)
                v.tensor_tensor(t4[1], s5_b[:, 1], fi, ALU.mult)
                v.tensor_tensor(t4[2], s5_b[:, 1], fr, ALU.mult)
                link(v.tensor_tensor(t4[3], s5_b[:, 0], fi, ALU.mult))
                link(v.tensor_tensor(t4[0], t4[0], t4[1], ALU.subtract))
                link(v.tensor_tensor(t4[2], t4[2], t4[3], ALU.add))
                for ri in range(2):
                    for g2 in range(2):
                        v.tensor_scalar(b2[:, ri, :, g2, :], t4[2 * ri], mask_b[:, g2:g2 + 1], None, ALU.mult)
                        v.tensor_scalar(c2[:, ri, :, g2, :], s5_c[:, ri], mask_c[:, g2:g2 + 1], 1.0 - 2.0 * ri,
                                        ALU.mult, ALU.mult)
                q.done(v.memset(s_(19), 0.0), "b2_ready")
                q.need("mix_ev", 4)
                rope(dq[:].rearrange("p t (n d) -> p t n d", n=4), 8, 1, 4)
                rope(dt_[:, :, 0:64].unsqueeze(2), 8, 1, 1)
                rope(dt_[:, :, 128:384].rearrange("p t (n d) -> p t n d", n=8), 4, 2, 8)
                rope(dt_[:, :, 384:416].unsqueeze(2), 4, 2, 1)
                v.tensor_copy(kk[:], bc(dt_[:, :, 0:64].unsqueeze(2), [P, TB, 2, 64]))
                v.tensor_scalar(w16[:], dt_[:, :, 416:424], 0.0625, None, ALU.mult)
                q.done(v.tensor_copy(ki4[:], bc(dt_[:, :, 384:416].unsqueeze(2), [P, TB, 4, 32])), "rope")
                q.need("la_mm", 1)
                for j in range(2):
                    ins = v.tensor_scalar(za[:, j, :], bank[7][:, j * S:j * S + S], a_b[:, j:j + 1], None, ALU.add)
                q.link(ins)
                q.done(v.memset(s_(19), 0.0), "la_ev")
                dve.sem_inc(sem("ls_in"), 1)
                q.need("ls_ex", 1)
                link(v.scalar_tensor_tensor(out=zb[:], in0=za[:], scalar=0.0, in1=zb[:], op0=ALU.min, op1=ALU.subtract))
                for j in range(2):
                    ins = v.tensor_tensor_scan(out=za[:, j, :], data0=scan_keep[:], data1=zb[:, j, :], initial=0.0,
                                               op0=ALU.mult, op1=ALU.add)
                link(ins)
                zc = za[:].rearrange("p a (c j) -> p (a c) j", j=64)
                q.done(v.tensor_tensor(zb[:].rearrange("p a (c j) -> p (a c) j", j=64),
                                       bc(zc[:, :, 63:64], [P, 8, 64]), zc, ALU.subtract), "gla_cum")
                for n in range(8):
                    q.need("ix_ev", n + 1)
                    blk = 1 if n < 4 else 0
                    wide = S if n < 4 else P
                    acc = isc[:, 1:3, :].rearrange("p a s -> p (a s)") if n < 4 else isc[:, 0, :]
                    for i in range(2):
                        hd = n % 4 + 4 * i
                        src = rl[:, n % 2, i * wide:i * wide + wide]
                        if hd == 0:
                            link(v.tensor_scalar(acc, src, w16[:, blk, 0:1], None, ALU.mult))
                        else:
                            ins = v.scalar_tensor_tensor(out=acc, in0=src, scalar=w16[:, blk, hd:hd + 1], in1=acc,
                                                         op0=ALU.mult, op1=ALU.add)
                            if i == 0:
                                link(ins)
                    q.done(ins, "ix_acc")
                    q.need("ix_acc", n + 1)
                q.need("gla_exp", 1)
                q.need("mix_ev", 8)
                link(v.scalar_tensor_tensor(out=gq[:], in0=gq[:], scalar=0.125, in1=eb[:], op0=ALU.mult, op1=ALU.mult))
                link(v.tensor_tensor(en[:], en[:], gk[:], ALU.mult))
                q.done(v.tensor_tensor(ke[:], ke[:], gk[:], ALU.mult), "gla_qk")
                for blk in range(2):
                    d_ = isc[:, 2 * blk, :]
                    link(v.tensor_tensor(d_, d_, cneg[:], ALU.add))
                    w_ = isc[:, 0, :] if blk == 0 else isc[:, 1:3, :].rearrange("p a s -> p (a s)")
                    top_k(w_)
                    link(v.tensor_scalar(w_, w_, TAKEN, NEG, ALU.not_equal, ALU.mult))
                    link(v.tensor_tensor(d_, d_, cneg[:], ALU.add))
                for tb in range(TB):
                    q.need("att_mm", tb + 1)
                    if tb == 0:
                        q.need("bc_ev", 2)
                    q.done(v.tensor_tensor(attm[:, tb], bank[4 + tb][:].rearrange("p (h s) -> p h s", h=4),
                                           bc(gla_mask[:].unsqueeze(1), [P, 4, P]), ALU.mult), "att_ev")
                for u in range(3):
                    q.need("dl_mm", u + 1)
                    n, wide = (4, P) if u == 0 else (2, S)
                    bias = isc[:, 0, :] if u == 0 else isc[:, 1:3, :].rearrange("p a s -> p (a s)")
                    q.done(v.scalar_tensor_tensor(out=dl[:, u].rearrange("p (h s) -> p h s", h=n),
                                                  in0=bank[5 + u][:].rearrange("p (h s) -> p h s", h=n), scalar=0.125,
                                                  in1=bc(bias.unsqueeze(1), [P, n, wide]), op0=ALU.mult, op1=ALU.add),
                           "dl_ev")
                q.need("dl_ev", 3)
                q.done(v.tensor_reduce(dstat[:, 0, 0, :], dl[:, 0].rearrange("p (h s) -> p h s", h=4), AX, ALU.max,
                                       negate=True), "mx")
                q.done(v.tensor_reduce(dstat[:, 0, 1, :], dl[:, 1:3].rearrange("p a (g s) -> p (a g) s", s=S), AX, ALU.max,
                                       negate=True), "mx")
                q.need("u_mm", 1)
                link(v.memset(rl[:], 0.0))
                for n in range(3):
                    for i in range(2):
                        r = slice(64 * i, 64 * i + 64)
                        if n == 0:
                            v.tensor_copy(state[r, 0, :, r], bank[4][r, 0:P].rearrange("p (h e) -> p h e", h=2))
                            continue
                        for hp in range(2):
                            ins = v.scalar_tensor_tensor(out=state[r, n, hp, r], in0=state[r, n - 1, hp, r],
                                                         scalar=eb[r, hp, 64 * n + 63:64 * n + 64],
                                                         in1=bank[4][r, n * P + hp * 64:n * P + hp * 64 + 64],
                                                         op0=ALU.mult, op1=ALU.add)
                    if n:
                        link(ins)
                    else:
                        link(v.memset(s_(19), 0.0))
                q.done(v.memset(s_(19), 0.0), "st_ready")
                q.need("ex", 2)
                link(v.reciprocal(dstat[:, 2].rearrange("p a b -> p (a b)"), dstat[:, 1].rearrange("p a b -> p (a b)")))
                vv = dl[:, 0].rearrange("p (h s) -> p h s", h=4)
                link(v.tensor_tensor(vv, vv, bc(dstat[:, 2, 0, :].unsqueeze(2), [P, 4, P]), ALU.mult))
                vv = dl[:, 1:3].rearrange("p a (g s) -> p (a g) s", s=S)
                q.done(v.tensor_tensor(vv, vv, bc(dstat[:, 2, 1, :].unsqueeze(2), [P, 4, S]), ALU.mult), "p_ready")
                q.need("o_sq", 2)
                link(v.tensor_reduce(ost[:, 0].rearrange("p a b -> p (a b)"),
                                     zb[:].rearrange("p t (h d) -> p (t h) d", h=4), AX, ALU.add))
                q.link(v.tensor_scalar(ost[:, 0], ost[:, 0], 1.0 / 64, EPS, ALU.mult, ALU.add))
                q.done(v.memset(s_(19), 0.0), "o_ms")
                q.need("sr", 1)
                link(v.tensor_tensor(gr[:], gr[:], bc(gla_g[:].unsqueeze(1), [P, TB, W]), ALU.mult))
                q.need("o_rt", 1)
                link(v.reciprocal(ost[:, 0].rearrange("p a b -> p (a b)"), ost[:, 1].rearrange("p a b -> p (a b)")))
                for tb in range(TB):
                    ins = v.tensor_tensor(za[:, tb, :].rearrange("p (h d) -> p h d", h=4),
                                          bank[4 + tb][:, 0:W].rearrange("p (h d) -> p h d", h=4),
                                          bc(ost[:, 0, tb, :].unsqueeze(2), [P, 4, 64]), ALU.mult)
                link(ins)
                q.done(v.tensor_tensor(za[:], za[:], gr[:], ALU.mult), "o_done")
                q.need("e_tab", 1)
                q.need("pt_mm", 3)
                for t in range(8):
                    q.need("bu_mm", t + 1)
                    bu = bank[(4, 7)[t % 2]][:].rearrange("p (r s) -> p r s", r=2)
                    v.tensor_tensor(pq[:, 0], bu, bc(E[:, 0:1, t, :], [P, 2, S]), ALU.mult)
                    link(v.tensor_tensor(pq[:, 1], bu, bc(E[:, 1:2, t, :], [P, 2, S]), ALU.mult))
                    dve.sem_inc(sem("bu_ev"), 1)
                    v.tensor_tensor(zi[:, 0, :], pq[:, 0, 0, :], pq[:, 1, 1, :], ALU.add)
                    link(v.tensor_tensor(zi[:, 1, :], pq[:, 0, 1, :], pq[:, 1, 0, :], ALU.subtract))
                    if t >= 1:
                        q.need("xs", t)
                    for ri in range(2):
                        ins = v.tensor_tensor_scan(out=zo[:, ri, :], data0=bc(sp[:, 2, t:t + 1], [P, S]), data1=zi[:, ri, :],
                                                   initial=0.0, op0=ALU.mult, op1=ALU.add)
                    q.done(ins, "z_out")
                q.need("yk", 8)
                for j in range(2):
                    ins = v.scalar_tensor_tensor(out=gel[:, j, :], in0=uT[:, j, :], scalar=s5_d[:, j:j + 1],
                                                 in1=bank[5][:, j * S:j * S + S], op0=ALU.mult, op1=ALU.add)
                q.done(ins, "s5y")
                q.need("glu_ev", 1)
                q.done(v.tensor_tensor(ycT[:], ycT[:], gel[:], ALU.mult), "yc")
                for n in range(16):
                    i, tb, nh = n // 4, (n // 2) % 2, n % 2
                    q.need("mg_mm", n + 1)
                    q.need("gate_ev", 4 * i + 4)
                    gsv = gs[:, tb, i % 2, nh * 512:nh * 512 + 512]
                    q.done(v.tensor_tensor(gsv, bank[n % 4][:], gsv, ALU.mult), "mg_ev")
                for j in (0, 2):
                    q.need("tp_mm", 4 + j + 1)
                    q.done(v.tensor_copy(hT[:, 2 * j:2 * j + 2, :].rearrange("p a b -> p (a b)"), bank[4 + j][:]), "tp_v")
                for n in range(4):
                    nh, tb = n // 2, n % 2
                    q.need("wo_mm", n + 1)
                    xv = x[:, tb, nh * 512:nh * 512 + 512]
                    q.done(v.tensor_tensor(xv, xv, bank[n][:], ALU.add), "wo_ev")
                norm_h(1)
                norm_evacuate(2, 1)
                for n in range(4):
                    q.need("cl_mm", n + 1)
                    link(v.tensor_reduce(cst[:, 2, n // 2, 2 * (n % 2):2 * (n % 2) + 2],
                                         bank[4 + n][:].rearrange("p (h s) -> p h s", h=2), AX, ALU.max))
                q.done(v.tensor_scalar(cst[:, 0], cst[:, 2], -(128 ** -0.5), None, ALU.mult), "cmx")
                q.need("cex", 1)
                link(v.reciprocal(cst[:, 2].rearrange("p a b -> p (a b)"), cst[:, 1].rearrange("p a b -> p (a b)")))
                for tb in range(TB):
                    ins = v.tensor_tensor(px[:, tb], px[:, tb], bc(cst[:, 2, tb, :].unsqueeze(2), [P, 4, S]), ALU.mult)
                q.done(ins, "cp")
                for n in (0, 2):
                    q.need("cpt_mm", n + 1)
                    ins = v.tensor_copy(pTx[:, n // 2, 0:2, :].rearrange("p a b -> p (a b)"), bank[n][:])
                    if n == 0:
                        ins.then_inc(sem("cpt_v"), 1)
                    else:
                        ins.then_inc(sem("cpt_v"), 1)
                q.need("cpt_v", 2)
                q.need("cpt_a", 2)
                dve.sem_inc(sem("cpt_ev"), 4)
                for n in range(4):
                    tb, nh = n // 2, n % 2
                    q.need("cy_mm", n + 1)
                    xv = x[:, tb, nh * 512:nh * 512 + 512]
                    q.done(v.tensor_tensor(xv, xv, bank[n][:], ALU.add), "cy_ev")
                norm_h(2)
                norm_evacuate(3, 2)
                q.need("rt_mm", 1)
                r_ = lambda i: rx[:, i]
                link(v.tensor_tensor(rt[:], bank[0][:, 0:40].rearrange("p (t n) -> p t n", t=2),
                                     bc(b_rt[:].unsqueeze(1), [P, TB, 20]), ALU.add))
                dve.sem_inc(sem("rt_e1"), 1)

                def first_max(vals, mx, eq, run, hot):
                    link(v.tensor_reduce(mx[:, :, 0], vals, AX, ALU.max))
                    link(v.tensor_tensor(eq, vals, bc(mx[:, :, 0:1], [P, TB, 4]), ALU.is_equal))
                    for tb in range(TB):
                        link(v.tensor_tensor_scan(out=run[:, tb, :], data0=ones4[:], data1=eq[:, tb, :], initial=0.0,
                                                  op0=ALU.mult, op1=ALU.add))
                    link(v.scalar_tensor_tensor(out=hot, in0=run, scalar=1.0, in1=eq, op0=ALU.is_equal, op1=ALU.mult))

                ones4 = scan_keep[:, 1:5]
                first_max(rt[:, :, 0:4], r_(0), r_(3), r_(4), r_(5))
                link(v.tensor_tensor(r_(1), rt[:, :, 0:4], bc(r_(0)[:, :, 0:1], [P, TB, 4]), ALU.subtract))
                for tb in range(TB):
                    link(v.tensor_tensor(rxx[:, tb], rt[:, tb, 4:20].rearrange("p (g e) -> p g e", g=4),
                                         bc(r_(5)[:, tb, :].unsqueeze(2), [P, 4, 4]), ALU.mult))
                link(v.tensor_tensor(rxx[:, :, 0:2, :], rxx[:, :, 0:2, :], rxx[:, :, 2:4, :], ALU.add))
                link(v.tensor_tensor(r_(8), rxx[:, :, 0, :], rxx[:, :, 1, :], ALU.add))
                first_max(r_(8), r_(0), r_(3), r_(4), r_(9))
                link(v.tensor_tensor(r_(6), r_(8), bc(r_(0)[:, :, 0:1], [P, TB, 4]), ALU.subtract))
                dve.sem_inc(sem("rt_x1"), 1)
                link(v.scalar_tensor_tensor(out=r_(8), in0=r_(9), scalar=NEG, in1=r_(8), op0=ALU.mult, op1=ALU.add))
                first_max(r_(8), r_(0), r_(3), r_(4), r_(10))
                q.need("rt_x2", 1)
                link(v.tensor_tensor(r_(9), r_(9), r_(10), ALU.add))
                link(v.tensor_tensor(r_(7), r_(7), r_(9), ALU.mult))
                link(v.tensor_reduce(r_(0)[:, :, 0], r_(7), AX, ALU.add))
                link(v.tensor_reduce(r_(0)[:, :, 1], r_(2), AX, ALU.add))
                link(v.tensor_tensor(r_(0)[:, :, 2], r_(0)[:, :, 0], r_(0)[:, :, 1], ALU.mult))
                link(v.reciprocal(r_(0)[:, :, 3], r_(0)[:, :, 2]))
                link(v.tensor_tensor(r_(7), r_(7), bc(r_(0)[:, :, 3:4], [P, TB, 4]), ALU.mult))
                for tb in range(TB):
                    link(v.tensor_tensor(comb[:, tb], bc(r_(5)[:, tb, :].unsqueeze(2), [P, 4, 4]),
                                         bc(r_(7)[:, tb, :].unsqueeze(1), [P, 4, 4]), ALU.mult))
                combf = comb[:].rearrange("p t g e -> p t (g e)")
                for tb in range(TB):
                    ins = v.tensor_tensor(sel[:, tb], bc(r_(5)[:, tb, :].unsqueeze(2), [P, 4, 4]),
                                          bc(r_(9)[:, tb, :].unsqueeze(1), [P, 4, 4]), ALU.mult)
                q.done(ins, "hs")
                dve.wait_ge(sem("g_loaded"), l * 16 + 16)
                for tb in range(TB):
                    q.done(v.tensor_tensor(h[:, tb, :], h[:, tb, :], g_bc[:], ALU.mult), "hs_f")
                q.need("rank_mm", 1)
                self_ = sel[:].rearrange("p t g e -> p t (g e)")
                link(v.tensor_reduce(most[:, 0:1], bank[0][:, 32:48], AX, ALU.max))
                v.tensor_scalar(flag[:], most[:, 0:1], float(P), None, ALU.is_gt).then_inc(sem("flag"), 1)
                link(v.tensor_tensor(place[:, :, 0, :], bank[0][:, 0:32].rearrange("p (t n) -> p t n", t=2), self_, ALU.mult))
                link(v.tensor_scalar(place[:, :, 0, :], place[:, :, 0, :], 1.0, None, ALU.subtract))
                link(v.tensor_scalar(place[:, :, 1, :], place[:, :, 0, :], float(P), None, ALU.subtract))
                for tb in range(TB):
                    q.need("hs_h", tb + 1)
                    ins = v.tensor_tensor(hs_lo[:, tb, :], h[:, tb, :], hs_hi[:, tb, :].bitcast(F32), ALU.subtract)
                link(ins)

                def choose(p, e):
                    for tb in range(TB):
                        at = place[:, tb, p, bass.ds(e, 1)] if not isinstance(e, int) else place[:, tb, p, e:e + 1]
                        ins = v.tensor_scalar(pick[:, tb, :], slot_no[:], at, None, ALU.is_equal)
                    ins.then_inc(sem("pick"), 1)

                def pieces(p, e, js):
                    for j in js:
                        for i in range(4):
                            n = 4 * j + i
                            q.need_turn("w_hi", p, e, n + 1)
                            v.tensor_tensor(w_lo[:, n % RP, :], ring[:, e_slot[j], i * PIECE:i * PIECE + PIECE],
                                            w_hi[:, n % RP, :].bitcast(F32), ALU.subtract).then_inc(sem("w_lo"), 1)
                        q.need_turn("w_lo", p, e, 4 * j + 4)
                        dve.sem_inc(sem("split"), 1)

                def gathered(p, e):
                    for b in range(2):
                        q.need_turn("ga_hi", p, e, b + 1)
                        v.tensor_tensor(ga_lo[:, 4 * b:4 * b + 4, :].rearrange("p a b -> p (a b)"), bank[b][:],
                                        ga_hi[:, 4 * b:4 * b + 4, :].rearrange("p a b -> p (a b)").bitcast(F32),
                                        ALU.subtract).then_inc(sem("ga_lo"), 1)

                def accumulate(p, e):
                    for n in range(4):
                        nh, tb = n // 2, n % 2
                        q.need_turn("sc_mm", p, e, n + 1)
                        xv = x[:, tb, nh * 512:nh * 512 + 512]
                        w = combf[:, tb, bass.ds(e, 1)] if not isinstance(e, int) else combf[:, tb, e:e + 1]
                        v.scalar_tensor_tensor(out=xv, in0=bank[SC_BANKS[n]][:], scalar=w, in1=xv,
                                               op0=ALU.mult, op1=ALU.add).then_inc(sem("x_acc"), 1)

                def turn(p, e, first=False, last=False):
                    pieces(p, e, (1,))
                    if not first:
                        accumulate(p, e - 1)
                    if not last:
                        q.need_turn("pickT_mm", p, e, 1)
                        choose(p, e + 1)
                    pieces(p, e, (2,))
                    q.need_turn("act_gate", p, e, 1)
                    v.tensor_tensor(hid[:, :], act_g[:, :], bank[3][:], ALU.mult).then_inc(sem("hid"), 1)
                    if not last:
                        gathered(p, e + 1)
                    q.need_turn("hidT_hi", p, e, 1)
                    v.tensor_tensor(hidT_lo[:].rearrange("p a b -> p (a b)"), bank[4][:],
                                    hidT_hi[:].rearrange("p a b -> p (a b)").bitcast(F32),
                                    ALU.subtract).then_inc(sem("hidT_lo"), 1)
                    if not last:
                        pieces(p, e + 1, (0,))
                    for nh in range(2):
                        c = slice(nh * 512, nh * 512 + 512)
                        q.need_turn("y_hi", p, e, nh + 1)
                        v.tensor_tensor(y_lo[:, c], bank[5 + nh][:], y_hi[:, c].bitcast(F32),
                                        ALU.subtract).then_inc(sem("y_lo"), 1)
                    if last:
                        accumulate(p, e)

                def one_pass(p):
                    choose(p, 0)
                    gathered(p, 0)
                    pieces(p, 0, (0,))
                    q.turns(p, turn)

                q.passes(one_pass, [(n, N_EXP * PER_TURN[n]) for n in
                                    ("split", "w_lo", "pick", "ga_lo", "hid", "hidT_lo", "y_lo", "x_acc")])
                dve.wait_ge(sem("x_acc"), l * (PASSES * N_EXP * 4) + PASSES * N_EXP * 4)
                dve.sem_inc(sem("ffn_done"), 1)
                q.leave()
            dve.wait_ge(sem("f_sumsq"), 2)
            v.tensor_scalar(st[:, 1, :], st[:, 0, :], 1.0 / D, EPS, ALU.mult, ALU.add).then_inc(sem("f_meansq"), 1)
            dve.wait_ge(sem("f_root"), 1)
            link(v.reciprocal(st[:, 3, :], st[:, 2, :]))
            dve.wait_ge(sem("go_loaded"), 16)
            for tb in range(TB):
                v.scalar_tensor_tensor(out=h[:, tb, :], in0=x[:, tb, :], scalar=st[:, 3, tb:tb + 1], in1=g_out,
                                       op0=ALU.mult, op1=ALU.mult).then_inc(sem("out_ready"), 1)

        for name, n in produced.items():
            if name in PER and PER[name] != n and name not in ("used",):
                print("semaphore", name, "produced", n, "said", PER[name])


N_PAR = 23
for _n, _k in dict(rank_mm=1, hs_f=2, hs_h=2, h_free=1, rt_x2=1, cpt_v=2, cpt_a=2, settled=0).items():
    PER[_n] = _k

_INS = ['x', 'mem', 'positions', 'norm_mix', 'w_in', 'conv_w', 'conv_b', 'gla_a_up', 'gla_a_b', 'gla_norm',
        's5_lambda_re', 's5_lambda_im', 's5_log_dt', 's5_b_re', 's5_b_im', 's5_c_re', 's5_c_im', 's5_d',
        's5_w_glu', 's5_b_glu', 'w_branch', 'w_out', 'norm_cross', 'w_cq', 'w_ckv', 'w_co', 'norm_ffn',
        'w_route_group', 'b_route_group', 'w_route_expert', 'b_route_expert', 'w_e_gate', 'w_e_up',
        'w_e_down', 'norm_mem', 'norm_final']


def kernel(**inputs):
    import concourse.bacc as _bacc
    from concourse.bass_utils import run_bass_kernel_spmd as _run

    nc = _bacc.Bacc("TRN2", target_bir_lowering=False, num_devices=1)
    arrays, T = {}, {}
    for name in _INS:
        a = np.ascontiguousarray(inputs[name])
        arrays["in_" + name] = a
        T[name] = nc.dram_tensor("in_" + name, a.shape, mybir.dt.from_np(a.dtype), kind="ExternalInput").ap()
    out = nc.dram_tensor("out", (1, S, D), F32, kind="ExternalOutput").ap()
    trunk(nc, T, out)
    r = _run(nc, [arrays], core_ids=[0])
    return r.results[0]["out"]
```

```python
from contextlib import ExitStack

import numpy as np
import concourse.bass as bass
from concourse import mybir

ALU = mybir.AluOpType
ACT = mybir.ActivationFunctionType
F32 = mybir.dt.float32
F32R = mybir.dt.float32r
I32 = mybir.dt.int32
AX = mybir.AxisListType.X

P = 128
D = 1024
S = 256
TB = S // P
KD = D // P
L = 2
EPS = 1e-6
W = 256
PI = float(np.pi)

C_H, C_B, C_C = 0, 256, 512
G_Q, G_K, G_V, G_R, G_A = 768, 1024, 1280, 1536, 1792
S_U, D_Q, D_K, D_V, I_Q, I_K, I_W, GATES = 1808, 2064, 2320, 2384, 2448, 2704, 2736, 2744

NS = 3
SLOT = KD * 512
N_EXP = 16
TOPK = 64
NEG = -1.0e30
TAKEN = -3.0e38

DENSE = ["m5", "m3", "m1", "m2", "m4", "m0", "g0", "g1", "g2", "g3", "ckv0", "br01",
         "g4", "g5", "g6", "g7", "br23", "wo0", "wo1", "ckv1", "cq", "co"]
MIX_COLS = {"m5": (D_K, GATES), "m3": (S_U, D_K), "m1": (C_C, G_K), "m2": (G_K, G_R),
            "m4": (G_R, S_U), "m0": (C_H, C_C)}
ND = len(DENSE)
NCH = ND + 3 * N_EXP

N_PAR = 17
N_RT = 5

PER = dict(
    sumsq=6, meansq=3, root=3, scale=3, h0_ready=3, h1_ready=3, tp_mm=16, tp_v=12, tp_a=12,
    dw_hi=20, dw_lo=20, dw_used=15,
    mix_mm=12, mix_ev=12, rope=1, sa_mm=3, sa_ev=3, la_mm=1, la_ev=1, ix_mm=8, ix_ev=8, ix_acc=8,
    ls_in=1, ls_ex=1, gla_cum=1, gla_exp=1, gla_qk=1, ketok_mm=1, ketok_ev=1, att_mm=2, att_ev=2,
    sp_in=1, sp2_in=1, sp2_out=1, bt_mm=1, ct_mm=1, bc_ev=2, b2_ready=1,
    u_mm=1, st_ready=1, dl_mm=3, dl_ev=3, mx=2, ex=2, p_ready=1, pt_mm=3, pt_ev=3,
    o_mm=2, o_sq=2, o_ms=1, o_rt=1, o_done=1, sr=1, od_mm=1, od_ev=1, ybt_mm=1, ybt_ev=1,
    e_in=1, e_tab=1, bu_mm=8, bu_ev=8, z_out=8, xs=8, yk=8, s5y=1, gelu=1, glu_mm=1, glu_ev=1, yc=1,
    u_conv=1, gate_mm=16, gate_ev=16, ckv_mm=4, ckv_ev=4, mg_mm=16, mg_ev=16, mg_add=16,
    wo_mm=4, wo_ev=4, cq_mm=2, cq_ev=2, cl_mm=4, cmx=1, cex=1, cp=1, cpt_mm=4,
    co_mm=2, co_ev=2, cy_mm=4, cy_ev=4, rt_mm=1, rt_e1=1, rt_x1=1, comb=1,
    hs=1, h_gained=2, flag=1, ffn_done=1, rank_mm=1, h_free=1, rt_x2=1, cpt_v=2, cpt_a=2,
)
SPLIT = ["g5", "g6", "g7", "wo0", "wo1"]
LAST_USE = {"m5": ("mix_mm", 2), "m3": ("mix_mm", 4), "m1": ("mix_mm", 6), "m2": ("mix_mm", 8), "m4": ("mix_mm", 10),
            "m0": ("mix_mm", 12), "ckv0": ("ckv_mm", 2), "ckv1": ("ckv_mm", 4), "br01": ("mg_mm", 8),
            "br23": ("mg_mm", 16), "wo0": ("wo_mm", 2), "wo1": ("wo_mm", 4), "cq": ("cq_mm", 2), "co": ("cy_mm", 4),
            **{f"g{i}": ("gate_mm", 2 * i + 2) for i in range(8)}}


def split_piece_used(n):
    return LAST_USE[SPLIT[n // 4]] if n % 4 == 3 else ("dw_used", 3 * (n // 4) + n % 4 + 1)


PER_TURN = dict(split=3, w_hi=12, w_lo=10, w_lo_p=2, w_used=12, pick=1, pickT_mm=1, pickT=1, ga_mm=1, ga_hi=1,
                ga_lo=1, gu_sb=2, guT_mm=2, act_gate=1, hid=1, hidT_hi=1, hidT_lo=1,
                y_mm=1, y_hi=2, y_lo=2, sc_mm=4, x_acc=4)
CAP = 64
PASSES = S // CAP
RP = 6
PIECE = SLOT // 4
DVE_PIECES = ((0, 1, 2, 3), (0, 1, 2), (0, 1, 2))
LO_UP_TO = (4, 7, 10)


def bc(ap, shape):
    return ap.broadcast_to(shape)


def trunk(nc, T, out):
    with ExitStack() as ctx:
        def sb(name, shape, dt=F32):
            return ctx.enter_context(nc.sbuf_tensor(name, shape, dt))

        sems = {}

        def sem(name):
            if name not in sems:
                sems[name] = ctx.enter_context(nc.semaphore(name))
            return sems[name]

        bank = [ctx.enter_context(nc.psum_tensor(f"bank{i}", [P, 512], F32)) for i in range(8)]

        ring = sb("ring", [P, NS, SLOT])
        x = sb("x", [P, TB, D])
        h = sb("h", [P, TB, D])
        hT = sb("hT", [P, KD, S])
        memT = sb("memT", [P, KD, S])
        ident = sb("ident", [P, P])
        gla_mask = sb("gla_mask", [P, P])
        cneg = sb("cneg", [P, P])
        scan_keep = sb("scan_keep", [P, S])
        tri = sb("tri", [P, P])
        ones = sb("ones", [P, P])
        slot_no = sb("slot_no", [P, 2, CAP])
        flag = sb("flag", [P, 1], I32)
        mask_b = sb("mask_b", [P, 2])
        mask_c = sb("mask_c", [P, 2])
        mc_i = sb("mc_i", [P, 1], I32)
        mc_j = sb("mc_j", [P, 1], I32)
        pos_i = sb("pos_i", [P, TB], I32)
        pos_f = sb("pos_f", [P, TB])
        invf = sb("invf", [P, 8])
        ang = sb("ang", [P, TB, 8])
        rr = sb("rr", [P, 4, 16])
        rope_cs = sb("rope_cs", [P, 2, TB, 8])
        junk = sb("junk", [P, 2])
        st = sb("st", [P, 4, TB])
        g_fm = sb("g_fm", [P, 4, KD])
        conv_w = sb("conv_w", [P, 3, 2])
        conv_b = sb("conv_b", [P, 2])
        a_up = sb("a_up", [16, W])
        a_b = sb("a_b", [P, 2])
        gla_g = sb("gla_g", [P, W])
        lam = sb("lam", [P, 3, 8])
        s5_b = sb("s5_b", [P, 2, 8, 16])
        s5_c = sb("s5_c", [P, 2, 2, 64])
        s5_d = sb("s5_d", [P, 2])
        b_glu = sb("b_glu", [P, 2])
        w_glu = sb("w_glu", [P, 2, W])
        b_rt = sb("b_rt", [P, 20])
        w_rt = sb("w_rt", [P, KD, 20])
        outer, branch_ctx = ctx, ExitStack()

        size = {"late": 0, "over": 0}

        def sb(name, shape, dt=F32):
            size["late"] += 4 * int(np.prod(shape[1:]))
            return branch_ctx.enter_context(nc.sbuf_tensor(name, shape, dt))

        gs = sb("gs", [P, TB, 2, D])
        kTx = sb("kTx", [P, 4, S])
        vx = sb("vx", [P, TB, 512])
        ydT = sb("ydT", [P, 2, S])
        en = sb("en", [P, 2, S])
        E = sb("E", [P, 2, 8, S])
        cst = sb("cst", [P, 3, TB, 4])
        late = size["late"]
        dt_ = sb("dtok", [P, TB, 424])
        dq = sb("dq", [P, TB, W])
        kk = sb("kk", [P, TB, 2, 64])
        ki4 = sb("ki4", [P, TB, 4, 32])
        rp = sb("rp", [P, 4, TB, 32])
        qTd = sb("qTd", [P, 2, S])
        kTd = sb("kTd", [P, 2, S])
        qiT = sb("qiT", [P, 2, S])
        rl = sb("rl", [P, 2, 512])
        state = rl[:].rearrange("p a b -> p (a b)")[:, 0:768].rearrange("p (n h e) -> p n h e", n=3, h=2)
        w16 = sb("w16", [P, TB, 8])
        isc = sb("isc", [P, 3, P])
        top8 = sb("top8", [P, 8])
        dl = sb("dl", [P, 3, 4 * P])
        dstat = sb("dstat", [P, 3, TB, 4])
        pT = sb("pT", [P, 3, 4, P])
        gq = sb("gq", [P, 2, S])
        gk = sb("gk", [P, 2, S])
        gv = sb("gv", [P, TB, W])
        gr = sb("gr", [P, TB, W])
        alow = sb("alow", [16, S])
        za = sb("za", [P, 2, S])
        zb = sb("zb", [P, 2, S])
        eb = sb("eb", [P, 2, S])
        ke = sb("ke", [P, 2, S])
        ketok = sb("ketok", [P, TB, W])
        attm = sb("attm", [P, TB, 4, P])
        ost = sb("ost", [P, 2, TB, 4])
        ybT = sb("ybT", [P, 2, S])
        cc = sb("cc", [P, 2, S])
        ch = sb("ch", [P, 2, S])
        cb = sb("cb", [P, 2, S])
        yaT = sb("yaT", [P, 2, S])
        uT = sb("uT", [P, 2, S])
        sp = sb("sp", [P, 20, 8])
        wpow = sb("wpow", [P, 2, 8])
        wtmp = sb("wtmp", [P, 4, 8])
        b2 = attm[:].rearrange("p a b c -> p (a b c)")[:, 0:512].rearrange("p (r t g c) -> p r t g c", r=2, t=8, g=2)
        c2 = attm[:].rearrange("p a b c -> p (a b c)")[:, 512:1024].rearrange("p (r h g s) -> p r h g s", r=2, h=2, g=2)
        bT = sb("bT", [P, 2, 2, P])
        cT = sb("cT", [P, 2, 2, P])
        gel = gk
        ycT = en
        hf = h[:].rearrange("p t n -> p (t n)")
        pq = hf[:, 0:1024].rearrange("p (q r s) -> p q r s", q=2, r=2)
        zi = hf[:, 1024:1536].rearrange("p (r s) -> p r s", r=2)
        zo = [flat.rearrange("p (r s) -> p r s", r=2) for flat in
              (dl[:].rearrange("p a b -> p (a b)")[:, 0:512], hf[:, 1536:2048])]
        xb = dl[:].rearrange("p a b -> p (a b)")[:, 512:1536].rearrange("p (q r s) -> p q r s", q=2, r=2)
        Ef = E[:].rearrange("p r t s -> p (r t s)")
        qTx = Ef[:, 0:1024].rearrange("p (h s) -> p h s", h=4)
        oTx = Ef[:, 1024:2048].rearrange("p (h s) -> p h s", h=4)
        px = Ef[:, 2048:4096].rearrange("p (t h m) -> p t h m", t=TB, h=4)
        pTx = gs[:].rearrange("p a b c -> p (a b c)")[:, 0:2048].rearrange("p (b h s) -> p b h s", b=2, h=4)

        branch_ctx.close()

        def sb(name, shape, dt=F32):
            size["over"] += 4 * int(np.prod(shape[1:]))
            return outer.enter_context(nc.sbuf_tensor(name, shape, dt))

        g_bc = sb("g_bc", [P, D])
        ga = sb("ga", [P, KD, 2, CAP], F32R)
        pick = sb("pick", [P, TB, 2, CAP])
        pickT = sb("pickT", [P, S], F32R)
        fold = sb("fold", [P, CAP])
        gu = sb("gu", [P, 2, 512])
        act_g = sb("act_g", [P, 4, CAP])
        hid = sb("hid", [P, 4, CAP])
        hidT = sb("hidT", [P, 4, 2, CAP], F32R)
        y_hi = sb("y_hi", [P, D], F32R)
        y_lo = sb("y_lo", [P, D], F32R)
        rt = sb("rt", [P, TB, 20])
        rx = sb("rx", [P, 12, TB, 4])
        rxx = sb("rxx", [P, TB, 4, 4])
        comb = sb("comb", [P, TB, 4, 4])
        sel = sb("sel", [P, TB, 4, 4])
        place = sb("place", [P, TB, PASSES * N_EXP])
        most = sb("most", [P, 2])
        sb("between", [P, (late - size["over"]) // 4 + 16])
        w_hi = sb("w_hi", [P, RP, PIECE], F32R)
        w_lo = sb("w_lo", [P, RP, PIECE], F32R)
        hT_hi = sb("hT_hi", [P, KD, S], F32R)
        hT_lo = sb("hT_lo", [P, KD, S], F32R)
        g_out = g_bc[:]

        class Order:

            def __init__(self, eng, name):
                self.e, self.name, self.n, self.base = eng, name, 0, 0
                self.own = sem(name + "_steps")

            def link(self, ins):
                ins.then_inc(self.own, 1)
                self.n += 1
                self.e.wait_ge(self.own, self.base + self.n)
                if self.name in ("pool", "pe"):
                    self.settle()

            def enter(self, l, stride):
                self.before, self.stride = self.n, stride
                self.base, self.n = l * stride + self.n, 0

            def leave(self):
                assert self.n < self.stride, (self.name, self.n)
                self.e.sem_inc(self.own, self.stride - self.n)
                self.base, self.n = L * self.stride + self.before, 0

            def turns(self, p, one):
                one(p, 0, first=True)
                self.settle()
                with self.e.Fori(1, N_EXP - 1) as e:
                    one(p, e)
                one(p, N_EXP - 1, last=True)

            def more_passes(self):
                self.settle()
                return self.e.value_load(flag[0:1, 0:1], min_val=0, max_val=1)

            def settle(self):
                self.e.sem_inc(sem("settled"), 1)

        SC_BANKS = (4, 7, 1, 0)
        ld = [sem(f"loaded{s}") for s in range(NS)]
        slot_of = [i % NS for i in range(NCH)]
        e_slot = slot_of[ND:ND + 3]
        dense_loads = [slot_of[:ND].count(s) for s in range(NS)]
        loads = [n + PASSES * N_EXP for n in dense_loads]
        nth = [slot_of[:i].count(slot_of[i]) + 1 for i in range(ND)]
        w_in = T["w_in"]

        def chunk_src(name, l):
            def k_tiles(ap):
                return ap.rearrange("o (p k) n -> p (o k) n", p=P)
            one = bass.ds(l, 1)
            if name in MIX_COLS:
                a, b = MIX_COLS[name]
                return k_tiles(w_in[one, :, a:b]), KD, b - a
            if name[0] == "g":
                a = GATES + int(name[1:]) * 512
                return k_tiles(w_in[one, :, a:a + 512]), KD, 512
            if name.startswith("ckv"):
                a = int(name[3]) * 512
                return k_tiles(T["w_ckv"][one, :, a:a + 512]), KD, 512
            if name.startswith("br"):
                i = int(name[2])
                return T["w_branch"][one, i:i + 2].rearrange("o i (j p) n -> p (o i j) n", p=P), 4, D
            if name.startswith("wo"):
                a = int(name[2]) * 512
                return k_tiles(T["w_out"][one, :, a:a + 512]), KD, 512
            if name == "cq":
                return k_tiles(T["w_cq"][one]), KD, 512
            if name == "co":
                return T["w_co"][one].rearrange("o (h p) n -> p (o h) n", p=P), 4, D

        def turns_before(name, l, p, e):
            return (l * PASSES + p) * (N_EXP * PER_TURN[name]) + e * PER_TURN[name]

        def skipped(name):
            return (PASSES - 1) * N_EXP * PER_TURN[name]

        def slot(s, k, n):
            return ring[:, s, 0:k * n].rearrange("p (k n) -> p k n", n=n)

        block = ctx.enter_context(nc.Block())

        @block.sync
        def _(sp_):
            q = Order(sp_, "sp")
            sp_.dma_start(h[:], T["mem"].rearrange("o (t p) n -> p (o t) n", p=P)).then_inc(sem("mem_loaded"), 16)
            sp_.dma_start(x[:], T["x"].rearrange("o (t p) n -> p (o t) n", p=P)).then_inc(sem("x_loaded"), 16)

            def freed_by(name):
                return ("dw_lo", 4 * SPLIT.index(name) + 4) if name in SPLIT else LAST_USE[name]

            with sp_.Fori(0, L) as l:
                for i, name in enumerate(DENSE):
                    if i < NS:
                        sp_.wait_ge(sem("split"), l * (PASSES * N_EXP * 3) + NS)
                        q.settle()
                    else:
                        mm_done, count = freed_by(DENSE[i - NS])
                        sp_.wait_ge(sem(mm_done), l * PER[mm_done] + count)
                        q.settle()
                    src, k, n = chunk_src(name, l)
                    sp_.dma_start(slot(slot_of[i], k, n), src).then_inc(ld[slot_of[i]], 16)

                def experts(p):
                    with sp_.Fori(0, N_EXP) as e:
                        for j, (wt, k, n) in enumerate((("w_e_gate", KD, 512), ("w_e_up", KD, 512), ("w_e_down", 4, D))):
                            if isinstance(p, int):
                                mm_done, count = freed_by(DENSE[ND + j - NS])
                                sp_.wait_ge(sem(mm_done), l * PER[mm_done] + count)
                                q.settle()
                            sp_.wait_ge(sem("split"), turns_before("split", l, p, e) + j + 1)
                            q.settle()
                            src = T[wt][bass.ds(l, 1), bass.ds(e, 1)].rearrange("o i (p k) n -> p (o i k) n", p=P)
                            sp_.dma_start(slot(e_slot[j], k, n), src).then_inc(ld[e_slot[j]], 16)

                experts(0)
                sp_.wait_ge(sem("flag"), l + 1)
                more = q.more_passes()
                with sp_.If(more):
                    with sp_.Fori(1, PASSES) as p:
                        experts(p)
                with sp_.Else():
                    sp_.wait_ge(sem("split"), turns_before("split", l, 1, 0) + NS)
                    for s in range(NS):
                        sp_.sem_inc(ld[s], (PASSES - 1) * N_EXP * 16)
            sp_.wait_ge(sem("out_ready"), 2)
            sp_.dma_start(out.rearrange("o (t p) n -> p (o t) n", p=P), h[:]).then_inc(sem("stored"), 16)
            sp_.wait_ge(sem("stored"), 16)

        @block.tensor
        def _(pe):
            q = Order(pe, "pe")
            mm = nc.tensor.matmul
            tr = nc.tensor.transpose

            def chunk(i):
                s = slot_of[i]
                pe.wait_ge(ld[s], l * (16 * loads[s]) + 16 * nth[i])
                return s

            def transposes():
                for j in range(4):
                    for k in (2 * j, 2 * j + 1):
                        for tb in range(TB):
                            ins = tr(bank[4 + j][:, (k % 2) * S + tb * P:(k % 2) * S + tb * P + P],
                                     h[:, tb, k::KD], ident[:])
                    ins.then_inc(sem("tp_mm"), 1)

            pe.wait_ge(sem("ident_ready"), 1)
            for tb in range(TB):
                pe.wait_ge(sem("m_h_ready"), tb + 1)
            for j in range(4):
                for k in (2 * j, 2 * j + 1):
                    for tb in range(TB):
                        ins = tr(bank[4 + j][:, (k % 2) * S + tb * P:(k % 2) * S + tb * P + P],
                                 h[:, tb, k::KD], ident[:])
                ins.then_inc(sem("m_tp_mm"), 1)
            pe.wait_ge(sem("m_tp_v"), 4)

            with pe.Fori(0, L) as l:
                q.enter(l, 64)
                pe.wait_ge(sem("h0_ready"), l * PER["h0_ready"] + 1)
                pe.wait_ge(sem("h1_ready"), l * PER["h1_ready"] + 1)
                transposes()
                pe.wait_ge(sem("tp_v"), l * PER["tp_v"] + 2)
                pe.wait_ge(sem("tp_a"), l * PER["tp_a"] + 2)

                def feature_major(dst, s, n, c0, m=P, src=hT):
                    w = slot(s, KD, n)
                    for k in range(KD):
                        ins = mm(dst, w[:, k, c0:c0 + m], src[:, k, :], start=(k == 0), stop=(k == KD - 1))
                    return ins

                def token_major(dst, s, n, c0, c1, tb, src=hT):
                    w = slot(s, KD, n)
                    for k in range(KD):
                        ins = mm(dst, src[:, k, tb * P:tb * P + P], w[:, k, c0:c1], start=(k == 0), stop=(k == KD - 1))
                    return ins

                s = chunk(0)
                for tb in range(TB):
                    token_major(bank[tb][:, 0:424], s, 424, 0, 424, tb).then_inc(sem("mix_mm"), 1)
                s = chunk(1)
                for j in range(2):
                    ins = feature_major(bank[2][:, j * S:j * S + S], s, 512, j * P)
                ins.then_inc(sem("mix_mm"), 1)
                for tb in range(TB):
                    ins = token_major(bank[3][:, tb * W:tb * W + W], s, 512, 256, 512, tb)
                ins.then_inc(sem("mix_mm"), 1)
                s = chunk(2)
                for b in range(2):
                    for j in range(2):
                        ins = feature_major(bank[4 + b][:, j * S:j * S + S], s, 512, (2 * b + j) * P)
                    ins.then_inc(sem("mix_mm"), 1)
                s = chunk(3)
                for j in range(2):
                    ins = feature_major(bank[6][:, j * S:j * S + S], s, 512, j * P)
                ins.then_inc(sem("mix_mm"), 1)
                for tb in range(TB):
                    ins = token_major(bank[7][:, tb * W:tb * W + W], s, 512, 256, 512, tb)
                ins.then_inc(sem("mix_mm"), 1)
                s = chunk(4)
                pe.wait_ge(sem("mix_ev"), l * PER["mix_ev"] + 1)
                for tb in range(TB):
                    ins = token_major(bank[0][:, tb * W:tb * W + W], s, 272, 0, 256, tb)
                ins.then_inc(sem("mix_mm"), 1)
                pe.wait_ge(sem("mix_ev"), l * PER["mix_ev"] + 2)
                feature_major(bank[1][0:16, 0:S], s, 272, 256, m=16).then_inc(sem("mix_mm"), 1)
                s = chunk(5)
                for b in range(2):
                    pe.wait_ge(sem("mix_ev"), l * PER["mix_ev"] + 3 + b)
                    for j in range(2):
                        ins = feature_major(bank[2 + b][:, j * S:j * S + S], s, 512, (2 * b + j) * P)
                    ins.then_inc(sem("mix_mm"), 1)

                def gates(g):
                    s = chunk(DENSE.index(f"g{g}"))
                    for tb in range(TB):
                        b = 2 * (g % 2) + tb
                        if g in (0, 1):
                            pe.wait_ge(sem("mix_ev"), l * PER["mix_ev"] + 9 + b)
                        elif g == 4:
                            pe.wait_ge(sem("mg_ev"), l * PER["mg_ev"] + 8)
                        elif g != 5:
                            pe.wait_ge(sem("gate_ev"), l * PER["gate_ev"] + 2 * (g - 2) + tb + 1)
                        token_major(bank[b][:], s, 512, 0, 512, tb).then_inc(sem("gate_mm"), 1)

                def split_products(name, b0, mm_done):
                    for i in range(4):
                        n = 4 * SPLIT.index(name) + i
                        pe.wait_ge(sem("dw_lo"), l * PER["dw_lo"] + n + 1)
                        for tb in range(TB):
                            for k in (2 * i, 2 * i + 1):
                                c = slice((k % 2) * 512, (k % 2) * 512 + 512)
                                t_hi, t_lo = hT_hi[:, k, tb * P:tb * P + P], hT_lo[:, k, tb * P:tb * P + P]
                                mm(bank[b0 + tb][:], t_hi, w_hi[:, n % RP, c], start=(k == 0), stop=False)
                                mm(bank[b0 + tb][:], t_hi, w_lo[:, n % RP, c], start=False, stop=False)
                                ins = mm(bank[b0 + tb][:], t_lo, w_hi[:, n % RP, c], start=False, stop=(k == KD - 1))
                            if i == 3:
                                ins.then_inc(sem(mm_done), 1)
                        if i < 3:
                            ins.then_inc(sem("dw_used"), 1)

                pe.wait_ge(sem("rope"), l * PER["rope"] + 1)
                pe.wait_ge(sem("mix_ev"), l * PER["mix_ev"] + 7)
                for hp in range(2):
                    for tb in range(TB):
                        ins = tr(bank[4][:, hp * S + tb * P:hp * S + tb * P + P], dq[:, tb, hp * P:hp * P + P], ident[:])
                ins.then_inc(sem("sa_mm"), 1)
                for tb in range(TB):
                    tr(bank[5][:, tb * P:tb * P + P], kk[:, tb].rearrange("p a b -> p (a b)"), ident[:])
                for tb in range(TB):
                    ins = tr(bank[5][:, S + tb * P:S + tb * P + P], ki4[:, tb].rearrange("p a b -> p (a b)"), ident[:])
                ins.then_inc(sem("sa_mm"), 1)
                for hp in range(2):
                    for tb in range(TB):
                        ins = tr(bank[6][:, hp * S + tb * P:hp * S + tb * P + P],
                                 dt_[:, tb, 128 + hp * P:128 + hp * P + P], ident[:])
                ins.then_inc(sem("sa_mm"), 1)
                pe.wait_ge(sem("mix_ev"), l * PER["mix_ev"] + 10)
                for j in range(2):
                    ins = mm(bank[7][:, j * S:j * S + S], a_up[:, j * P:j * P + P], alow[:, :], start=True, stop=True)
                ins.then_inc(sem("la_mm"), 1)
                gates(0)
                pe.wait_ge(sem("sa_ev"), l * PER["sa_ev"] + 3)
                pe.wait_ge(sem("la_ev"), l * PER["la_ev"] + 1)
                for hq in range(8):
                    r = 32 * (hq % 4)
                    ins = mm(bank[4 + hq % 4][:, (hq // 4) * S:(hq // 4) * S + S], qiT[r:r + 32, hq // 4, P:2 * P],
                             kTd[r:r + 32, 1, :], start=True, stop=True)
                    if hq >= 4:
                        ins.then_inc(sem("ix_mm"), 1)
                for hq in range(8):
                    r = 32 * (hq % 4)
                    if hq < 4:
                        pe.wait_ge(sem("ix_ev"), l * PER["ix_ev"] + 1 + hq)
                    ins = mm(bank[4 + hq % 4][:, (hq // 4) * P:(hq // 4) * P + P], qiT[r:r + 32, hq // 4, 0:P],
                             kTd[r:r + 32, 1, 0:P], start=True, stop=True)
                    if hq >= 4:
                        ins.then_inc(sem("ix_mm"), 1)
                gates(1)
                pe.wait_ge(sem("b2_ready"), l * PER["b2_ready"] + 1)
                pe.wait_ge(sem("ix_ev"), l * PER["ix_ev"] + 8)
                for ri in range(2):
                    for hf_ in range(2):
                        ins = tr(bank[7][:, (ri * 2 + hf_) * P:(ri * 2 + hf_) * P + P],
                                 b2[:, ri, 4 * hf_:4 * hf_ + 4].rearrange("p t g c -> p (t g c)"), ident[:])
                ins.then_inc(sem("bt_mm"), 1)
                for ri in range(2):
                    for hf_ in range(2):
                        ins = tr(bank[6][:, (ri * 2 + hf_) * P:(ri * 2 + hf_) * P + P],
                                 c2[:, ri, hf_].rearrange("p g s -> p (g s)"), ident[:])
                ins.then_inc(sem("ct_mm"), 1)
                pe.wait_ge(sem("gla_qk"), l * PER["gla_qk"] + 1)
                pe.wait_ge(sem("ix_ev"), l * PER["ix_ev"] + 8)
                for odd in range(2):
                    r = 64 * odd
                    for tb in range(TB):
                        c = slice(tb * P, tb * P + P)
                        for hd in (odd, odd + 2):
                            ins = mm(bank[4 + tb][:, hd * P:hd * P + P], en[r:r + 64, hd // 2, c],
                                     gq[r:r + 64, hd // 2, c], start=True, stop=True)
                        if odd:
                            ins.then_inc(sem("att_mm"), 1)
                    if not odd:
                        q.link(ins)
                gates(2)
                pe.wait_ge(sem("bc_ev"), l * PER["bc_ev"] + 2)
                for tb in range(TB):
                    for j in range(2):
                        ins = tr(bank[6][:, tb * W + j * P:tb * W + j * P + P], ke[:, j, tb * P:tb * P + P], ident[:])
                ins.then_inc(sem("ketok_mm"), 1)
                pe.wait_ge(sem("ketok_ev"), l * PER["ketok_ev"] + 1)
                pe.wait_ge(sem("att_ev"), l * PER["att_ev"] + 2)
                for odd in range(2):
                    r = 64 * odd
                    for hd in (odd, odd + 2):
                        ins = mm(bank[5][:, hd * P:hd * P + P], qTd[r:r + 64, hd // 2, 0:P], kTd[r:r + 64, 0, 0:P],
                                 start=True, stop=True)
                    if odd:
                        ins.then_inc(sem("dl_mm"), 1)
                    for hd in (odd, odd + 2):
                        ins = mm(bank[6 + hd // 2][:, odd * S:odd * S + S], qTd[r:r + 64, hd // 2, P:2 * P],
                                 kTd[r:r + 64, 0, :], start=True, stop=True)
                        if odd:
                            ins.then_inc(sem("dl_mm"), 1)
                    if not odd:
                        q.link(ins)
                for n in (0, 2, 1):
                    if n == 1:
                        q.link(ins)
                    r = 64 * (n % 2)
                    for hd in range(4):
                        ins = mm(bank[4][64 * (hd % 2):64 * (hd % 2) + 64, n * P + (hd // 2) * 64:n * P + (hd // 2) * 64 + 64],
                                 ketok[r:r + 64, n // 2, hd * 64:hd * 64 + 64], gv[r:r + 64, n // 2, hd * 64:hd * 64 + 64],
                                 start=True, stop=True)
                ins.then_inc(sem("u_mm"), 1)
                gates(3)
                pe.wait_ge(sem("st_ready"), l * PER["st_ready"] + 1)
                pe.wait_ge(sem("dl_ev"), l * PER["dl_ev"] + 1)
                for tb in range(TB):
                    for hd in range(4):
                        c = slice(hd * 64, hd * 64 + 64)
                        mm(bank[4 + tb][:, c], attm[:, tb, hd, :], gv[:, tb, c], start=(hd == 0), stop=False,
                           skip_group_check=True)
                    for half in range(2):
                        n = 2 * tb + half
                        if n == 0:
                            continue
                        for hp in range(2):
                            ins = mm(bank[4 + tb][64 * half:64 * half + 64, hp * P:hp * P + P],
                                     gq[:, hp, n * 64:n * 64 + 64], state[:, n - 1, hp, :],
                                     start=False, stop=(half == 1 and hp == 1), skip_group_check=True)
                    ins.then_inc(sem("o_mm"), 1)
                def cross_part(i):
                    b = i // 2
                    s = slot_of[DENSE.index("ckv0" if i < 4 else "ckv1")]
                    if i % 4 == 0:
                        chunk(DENSE.index("ckv0" if i < 4 else "ckv1"))
                    if i in (0, 2):
                        pe.wait_ge(sem("gate_ev"), l * PER["gate_ev"] + 5 + b)
                    elif i in (4, 6):
                        pe.wait_ge(sem("wo_ev"), l * PER["wo_ev"] + b + 1)
                    c = (i % 2) * 256
                    if i < 4:
                        ins = feature_major(bank[b][:, c:c + S], s, 512, i * P, src=memT)
                    else:
                        ins = token_major(bank[b][:, c:c + 256], s, 512, c, c + 256, b - 2, src=memT)
                    if i % 2:
                        ins.then_inc(sem("ckv_mm"), 1)

                pe.wait_ge(sem("p_ready"), l * PER["p_ready"] + 1)
                pe.wait_ge(sem("dl_ev"), l * PER["dl_ev"] + 3)
                for u, b in ((0, 6), (1, 7), (2, 4)):
                    if b == 4:
                        cross_part(0)
                        pe.wait_ge(sem("o_done"), l * PER["o_done"] + 1)
                    for hd in range(4):
                        src = dl[:, 0, hd * P:hd * P + P] if u == 0 else \
                            dl[:, 1:3].rearrange("p a (g s) -> p (a g) s", s=S)[:, hd, (u - 1) * P:u * P]
                        ins = tr(bank[b][:, hd * P:hd * P + P], src, ident[:])
                    ins.then_inc(sem("pt_mm"), 1)
                pe.wait_ge(sem("pt_ev"), l * PER["pt_ev"] + 3)
                for hd in range(4):
                    r = 64 * (hd % 2)
                    c = (hd // 2) * S
                    mm(bank[5][r:r + 64, c:c + P], dt_[:, 0, 64:128], pT[:, 0, hd, :], start=True, stop=True)
                    mm(bank[5][r:r + 64, c + P:c + S], dt_[:, 0, 64:128], pT[:, 1, hd, :], start=True, stop=False)
                    ins = mm(bank[5][r:r + 64, c + P:c + S], dt_[:, 1, 64:128], pT[:, 2, hd, :], start=False, stop=True)
                ins.then_inc(sem("od_mm"), 1)
                for j in range(2):
                    for tb in range(TB):
                        ins = tr(bank[6][:, j * S + tb * P:j * S + tb * P + P], za[:, tb, j * P:j * P + P], ident[:])
                ins.then_inc(sem("ybt_mm"), 1)

                def drive(t):
                    b = (4, 7)[t % 2]
                    r = 32 * (t % 4)
                    if t >= 2:
                        pe.wait_ge(sem("bu_ev"), l * PER["bu_ev"] + t - 1)
                    for ri in range(2):
                        ins = mm(bank[b][:, ri * S:ri * S + S], bT[r:r + 32, ri, t // 4, :], uT[r:r + 32, t // 4, :],
                                 start=True, stop=True)
                    ins.then_inc(sem("bu_mm"), 1)

                def read_out(t):
                    r = 32 * (t % 4)
                    pe.wait_ge(sem("xs"), l * PER["xs"] + t + 1)
                    if t == 0:
                        pe.wait_ge(sem("od_ev"), l * PER["od_ev"] + 1)
                    for ri in range(2):
                        ins = mm(bank[5][r:r + 32, (t // 4) * S:(t // 4) * S + S], cT[:, ri, t // 4, r:r + 32],
                                 xb[:, t % 2, ri, :], start=(ri == 0), stop=(ri == 1))
                    ins.then_inc(sem("yk"), 1)

                def merge(i, outputs=range(4)):
                    src = (yaT, ybT, ycT, ydT)[i]
                    s = slot_of[DENSE.index("br01" if i < 2 else "br23")]
                    w = slot(s, 4, D)
                    for tb in range(TB):
                        for nh in range(2):
                            if tb * 2 + nh not in outputs:
                                continue
                            n = i * 4 + tb * 2 + nh
                            if n < 2:
                                pe.wait_ge(sem("ckv_ev"), l * PER["ckv_ev"] + n + 1)
                            elif n < 4:
                                pe.wait_ge(sem("gate_ev"), l * PER["gate_ev"] + 5 + n)
                            elif i == 2:
                                pe.wait_ge(sem("gate_ev"), l * PER["gate_ev"] + 13 + tb * 2 + nh)
                            else:
                                pe.wait_ge(sem("mg_ev"), l * PER["mg_ev"] + n - 3)
                            for j in range(2):
                                ins = mm(bank[n % 4][:], src[:, j, tb * P:tb * P + P],
                                         w[:, (i % 2) * 2 + j, nh * 512:nh * 512 + 512], start=(j == 0), stop=(j == 1))
                            ins.then_inc(sem("mg_mm"), 1)

                drive(0)
                drive(1)
                for t in range(8):
                    if t < 3:
                        cross_part(t + 1)
                    elif t < 7:
                        if t == 3:
                            chunk(DENSE.index("br01"))
                            pe.wait_ge(sem("u_conv"), l * PER["u_conv"] + 1)
                        merge(0, (t - 3,))
                    else:
                        pe.wait_ge(sem("ybt_ev"), l * PER["ybt_ev"] + 1)
                        merge(1, (0, 1))
                    read_out(t)
                    if t + 2 < 8:
                        drive(t + 2)
                pe.wait_ge(sem("gelu"), l * PER["gelu"] + 1)
                for j in range(2):
                    for k in range(2):
                        ins = mm(bank[6][:, j * S:j * S + S], w_glu[:, k, j * P:j * P + P], gel[:, k, :],
                                 start=(k == 0), stop=(k == 1))
                ins.then_inc(sem("glu_mm"), 1)

                merge(1, (2, 3))
                gates(4)
                pe.wait_ge(sem("tp_v"), l * PER["tp_v"] + 4)
                split_products("g5", 2, "gate_mm")
                pe.wait_ge(sem("gate_ev"), l * PER["gate_ev"] + 10)
                split_products("g6", 0, "gate_mm")
                pe.wait_ge(sem("gate_ev"), l * PER["gate_ev"] + 12)
                split_products("g7", 2, "gate_mm")
                chunk(DENSE.index("br23"))
                pe.wait_ge(sem("yc"), l * PER["yc"] + 1)
                merge(2)
                merge(3)
                pe.wait_ge(sem("mg_add"), l * PER["mg_add"] + 16)
                transposes()
                pe.wait_ge(sem("tp_v"), l * PER["tp_v"] + 8)
                for nh in range(2):
                    pe.wait_ge(sem("mg_ev"), l * PER["mg_ev"] + 14 + 2 * nh)
                    split_products(f"wo{nh}", 2 * nh, "wo_mm")

                cross_part(4)
                cross_part(5)
                pe.wait_ge(sem("h0_ready"), l * PER["h0_ready"] + 2)
                pe.wait_ge(sem("h1_ready"), l * PER["h1_ready"] + 2)
                transposes()
                pe.wait_ge(sem("tp_v"), l * PER["tp_v"] + 10)
                pe.wait_ge(sem("tp_a"), l * PER["tp_a"] + 10)
                s = chunk(DENSE.index("cq"))
                for b in range(2):
                    for j in range(2):
                        ins = feature_major(bank[b][:, j * S:j * S + S], s, 512, (2 * b + j) * P)
                    ins.then_inc(sem("cq_mm"), 1)
                pe.wait_ge(sem("cq_ev"), l * PER["cq_ev"] + 2)
                for tb in range(TB):
                    for hd in range(4):
                        ins = mm(bank[4 + 2 * tb + hd // 2][:, (hd % 2) * S:(hd % 2) * S + S],
                                 qTx[:, hd, tb * P:tb * P + P], kTx[:, hd, :], start=True, stop=True)
                        if hd % 2:
                            ins.then_inc(sem("cl_mm"), 1)
                cross_part(6)
                cross_part(7)
                pe.wait_ge(sem("cp"), l * PER["cp"] + 1)
                pe.wait_ge(sem("ckv_ev"), l * PER["ckv_ev"] + 4)
                for mb in range(2):
                    for hp in range(2):
                        for hd in (2 * hp, 2 * hp + 1):
                            for tb in range(TB):
                                ins = tr(bank[mb * 2 + hp][:, (hd % 2) * S + tb * P:(hd % 2) * S + tb * P + P],
                                         px[:, tb, hd, mb * P:mb * P + P], ident[:])
                        ins.then_inc(sem("cpt_mm"), 1)
                pe.wait_ge(sem("cpt_v"), l * PER["cpt_v"] + 2)
                pe.wait_ge(sem("cpt_a"), l * PER["cpt_a"] + 2)
                for hp in range(2):
                    for hd in (2 * hp, 2 * hp + 1):
                        for mb in range(2):
                            ins = mm(bank[4 + hp][:, (hd % 2) * S:(hd % 2) * S + S], vx[:, mb, hd * P:hd * P + P],
                                     pTx[:, mb, hd, :], start=(mb == 0), stop=(mb == 1))
                    ins.then_inc(sem("co_mm"), 1)
                pe.wait_ge(sem("co_ev"), l * PER["co_ev"] + 2)
                s = chunk(DENSE.index("co"))
                w = slot(s, 4, D)
                for tb in range(TB):
                    for nh in range(2):
                        for hd in range(4):
                            ins = mm(bank[tb * 2 + nh][:], oTx[:, hd, tb * P:tb * P + P],
                                     w[:, hd, nh * 512:nh * 512 + 512], start=(hd == 0), stop=(hd == 3))
                        ins.then_inc(sem("cy_mm"), 1)

                pe.wait_ge(sem("h0_ready"), l * PER["h0_ready"] + 3)
                pe.wait_ge(sem("h1_ready"), l * PER["h1_ready"] + 3)
                transposes()
                pe.wait_ge(sem("tp_v"), l * PER["tp_v"] + 12)
                pe.wait_ge(sem("tp_a"), l * PER["tp_a"] + 12)
                for tb in range(TB):
                    for k in range(KD):
                        ins = mm(bank[0][:, tb * 20:tb * 20 + 20], hT[:, k, tb * P:tb * P + P], w_rt[:, k, :],
                                 start=(k == 0), stop=(k == KD - 1))
                ins.then_inc(sem("rt_mm"), 1)
                pe.wait_ge(sem("rt_e1"), l * PER["rt_e1"] + 1)
                q.settle()
                pe.wait_ge(sem("hs"), l * PER["hs"] + 1)
                sel_ = lambda tb: sel[:, tb].rearrange("p g e -> p (g e)")
                mm(bank[0][:, 0:16], tri[:], sel_(0), start=True, stop=True)
                mm(bank[0][:, 16:32], tri[:], sel_(1), start=True, stop=False)
                mm(bank[0][:, 16:32], ones[:], sel_(0), start=False, stop=True)
                mm(bank[0][:, 32:48], ones[:], sel_(0), start=True, stop=False)
                mm(bank[0][:, 32:48], ones[:], sel_(1), start=False, stop=True).then_inc(sem("rank_mm"), 1)

                def gather(p, e, k0):
                    for k in range(k0, k0 + 4):
                        dst = bank[0][:, k * CAP:k * CAP + CAP]
                        for tb in range(TB):
                            ins = mm(dst, h[:, tb, k::KD], pick[:, tb, 0, :], start=(tb == 0), stop=(tb == TB - 1))
                    return ins

                def scatter(p, e):
                    for nh in range(2):
                        c = slice(nh * 512, nh * 512 + 512)
                        pe.wait_ge(sem("y_lo"), turns_before("y_lo", l, p, e) + nh + 1)
                        for tb in range(TB):
                            b = SC_BANKS[nh * 2 + tb]
                            mm(bank[b][:], pickT[:, tb * P:tb * P + P], y_hi[:, c], start=True, stop=False)
                            mm(bank[b][:], pickT[:, tb * P:tb * P + P], y_lo[:, c], start=False,
                               stop=True).then_inc(sem("sc_mm"), 1)

                def piece_ready(p, e, n):
                    j, i = n // 4, n % 4
                    if i in DVE_PIECES[j]:
                        pe.wait_ge(sem("w_lo"), turns_before("w_lo", l, p, e) + LO_UP_TO[j] - len(DVE_PIECES[j]) + i + 1)
                    else:
                        pe.wait_ge(sem("w_lo_p"), turns_before("w_lo_p", l, p, e) + j)

                def widen(p, e, j, i):
                    n = 4 * j + i
                    piece_ready(p, e, n)
                    for k in (2 * i, 2 * i + 1):
                        c = slice((k % 2) * 512, (k % 2) * 512 + 512)
                        tile = ga[:, k].rearrange("p a b -> p (a b)")
                        mm(bank[2 + j][:], tile, w_hi[:, n % RP, c], start=(k == 0), stop=False)
                        ins = mm(bank[2 + j][:], tile, w_lo[:, n % RP, c], start=False, stop=(k == KD - 1))
                    ins.then_inc(sem("w_used"), 1)

                def folded(dst, j):
                    for t in range(4):
                        ins = mm(dst[:, t * CAP:t * CAP + CAP], gu[:, j, t::4], fold[:], start=True, stop=True)
                    ins.then_inc(sem("guT_mm"), 1)

                def turn(p, e, first=False, last=False):
                    pe.wait_ge(sem("ga_lo"), turns_before("ga_lo", l, p, e) + 1)
                    for i in range(4):
                        widen(p, e, 0, i)
                    if not first:
                        scatter(p, e - 1)
                    for tb in range(TB):
                        ins = tr(bank[5][:, tb * P:tb * P + P],
                                 pick[:, tb].rearrange("p a b -> p (a b)"), ident[:])
                    ins.then_inc(sem("pickT_mm"), 1)
                    for i in range(2):
                        widen(p, e, 1, i)
                    pe.wait_ge(sem("gu_sb"), turns_before("gu_sb", l, p, e) + 1)
                    if not first:
                        pe.wait_ge(sem("x_acc"), turns_before("x_acc", l, p, e) - 3)
                    folded(bank[4], 0)
                    for i in range(2, 4):
                        widen(p, e, 1, i)
                    if not last:
                        pe.wait_ge(sem("pick"), turns_before("pick", l, p, e + 1) + 1)
                        if not first:
                            pe.wait_ge(sem("x_acc"), turns_before("x_acc", l, p, e))
                        gather(p, e + 1, 0)
                    pe.wait_ge(sem("gu_sb"), turns_before("gu_sb", l, p, e) + 2)
                    folded(bank[2], 1)
                    if not last:
                        gather(p, e + 1, 4).then_inc(sem("ga_mm"), 1)
                    pe.wait_ge(sem("hidT_lo"), turns_before("hidT_lo", l, p, e) + 1)
                    pe.wait_ge(sem("pickT"), turns_before("pickT", l, p, e) + 1)
                    for t in range(4):
                        n = 8 + t
                        piece_ready(p, e, n)
                        tile = hidT[:, t].rearrange("p a b -> p (a b)")
                        for nh in range(2):
                            c = slice(nh * 512, nh * 512 + 512)
                            mm(bank[5 + nh][:], tile, w_hi[:, n % RP, c], start=(t == 0), stop=False)
                            ins = mm(bank[5 + nh][:], tile, w_lo[:, n % RP, c], start=False, stop=(t == 3))
                            if t == 3 and nh == 0:
                                ins.then_inc(sem("y_mm"), 1)
                        ins.then_inc(sem("w_used"), 1)
                    if last:
                        pe.wait_ge(sem("x_acc"), turns_before("x_acc", l, p, e))
                        scatter(p, e)

                def one_pass(p):
                    if not isinstance(p, int):
                        pe.wait_ge(sem("x_acc"), (l * PASSES + p) * (4 * N_EXP))
                    pe.wait_ge(sem("h_gained"), l * PER["h_gained"] + 2)
                    pe.wait_ge(sem("pick"), turns_before("pick", l, p, 0) + 1)
                    gather(p, 0, 0)
                    gather(p, 0, 4).then_inc(sem("ga_mm"), 1)
                    q.turns(p, turn)

                one_pass(0)
                pe.wait_ge(sem("flag"), l + 1)
                more = q.more_passes()
                with pe.If(more):
                    with pe.Fori(1, PASSES) as p:
                        one_pass(p)
                with pe.Else():
                    pe.wait_ge(sem("ga_mm"), turns_before("ga_mm", l, 1, 0))
                    pe.sem_inc(sem("ga_mm"), skipped("ga_mm"))
                    pe.wait_ge(sem("guT_mm"), turns_before("guT_mm", l, 1, 0))
                    pe.sem_inc(sem("guT_mm"), skipped("guT_mm"))
                    pe.wait_ge(sem("pickT_mm"), turns_before("pickT_mm", l, 1, 0))
                    pe.sem_inc(sem("pickT_mm"), skipped("pickT_mm"))
                    pe.wait_ge(sem("y_mm"), turns_before("y_mm", l, 1, 0))
                    pe.sem_inc(sem("y_mm"), skipped("y_mm"))
                    pe.wait_ge(sem("w_used"), turns_before("w_used", l, 1, 0) + RP)
                    pe.sem_inc(sem("w_used"), skipped("w_used"))
                    pe.wait_ge(sem("sc_mm"), turns_before("sc_mm", l, 1, 0))
                    pe.sem_inc(sem("sc_mm"), skipped("sc_mm"))
                q.leave()

        @block.scalar
        def _(act):
            q = Order(act, "act")
            A = nc.scalar.activation

            def copy(dst, src, **kw):
                return A(dst, src, ACT.Copy, **kw)

            act.wait_ge(sem("mem_loaded"), 16)
            for tb in range(TB):
                A(kTx[:].rearrange("p a b -> p (a b)"), h[:, tb, :], ACT.Square,
                  accum_out=st[:, 0, tb:tb + 1]).then_inc(sem("ends_sumsq"), 1)
                act.wait_ge(sem("ends_sumsq"), tb + 1)
            act.wait_ge(sem("ends_meansq"), 1)
            A(st[:, 2, :], st[:, 1, :], ACT.Sqrt).then_inc(sem("ends_root"), 1)
            act.wait_ge(sem("ang_ready"), 1)
            A(rope_cs[:, 1].rearrange("p t f -> p (t f)"), rr[:, 0, :], ACT.Sin).then_inc(sem("rope_ready"), 1)
            A(rope_cs[:, 0].rearrange("p t f -> p (t f)"), rr[:, 1, :], ACT.Sin).then_inc(sem("rope_ready"), 1)
            act.wait_ge(sem("x_loaded"), 16)
            act.wait_ge(sem("m_tp_v"), 4)

            def norm_stats(u):
                for tb in range(TB):
                    A(h[:, 1, :], x[:, tb, :], ACT.Square, accum_out=st[:, 0, tb:tb + 1]).then_inc(sem("sumsq"), 1)
                    act.wait_ge(sem("sumsq"), l * PER["sumsq"] + 2 * u + tb + 1)
                act.wait_ge(sem("meansq"), l * PER["meansq"] + u + 1)
                A(st[:, 2, :], st[:, 1, :], ACT.Sqrt).then_inc(sem("root"), 1)
                act.wait_ge(sem("scale"), l * PER["scale"] + u + 1)
                A(h[:, 1, :], x[:, 1, :], ACT.Copy, scale=st[:, 3, 1:2]).then_inc(sem("h1_ready"), 1)

            def norm_evacuate(u, g):
                for j in (1, 3):
                    act.wait_ge(sem("tp_mm"), l * PER["tp_mm"] + 4 * u + j + 1)
                    for i in range(2):
                        k = 2 * j + i
                        ins = A(hT[:, k, :], bank[4 + j][:, i * S:i * S + S], ACT.Copy, scale=g_fm[:, g, k:k + 1])
                    ins.then_inc(sem("tp_a"), 1)

            with act.Fori(0, L) as l:
                q.enter(l, 256)
                norm_stats(0)
                act.wait_ge(sem("g_mix_loaded"), l * 16 + 16)
                norm_evacuate(0, 0)
                act.wait_ge(sem("par_loaded"), l * N_PAR * 16 + N_PAR * 16)
                q.link(A(sp[:, 0, :], lam[:, 2, :], ACT.Exp))
                A(junk[:, 1:2], junk[:, 0:1], ACT.Copy).then_inc(sem("sp_in"), 1)
                act.wait_ge(sem("sp2_in"), l * PER["sp2_in"] + 1)
                A(sp[:, 2, :], sp[:, 1, :], ACT.Exp)
                A(sp[:, 8, :], sp[:, 6, :], ACT.Sin)
                A(sp[:, 9, :], sp[:, 7, :], ACT.Sin).then_inc(sem("sp2_out"), 1)
                flat = lambda t: t[:].rearrange("p a b -> p (a b)")
                act.wait_ge(sem("mix_mm"), l * PER["mix_mm"] + 1)
                copy(dt_[:, 0, :], bank[0][:, 0:424]).then_inc(sem("mix_ev"), 1)
                act.wait_ge(sem("mix_mm"), l * PER["mix_mm"] + 2)
                copy(dt_[:, 1, :], bank[1][:, 0:424]).then_inc(sem("mix_ev"), 1)
                for n, (dst, b) in enumerate(((uT, 2), (dq, 3), (cc, 4), (gq, 5), (gk, 6), (gv, 7), (gr, 0))):
                    act.wait_ge(sem("mix_mm"), l * PER["mix_mm"] + n + 3)
                    copy(flat(dst), bank[b][:]).then_inc(sem("mix_ev"), 1)
                act.wait_ge(sem("mix_mm"), l * PER["mix_mm"] + 10)
                copy(alow[:, :], bank[1][0:16, 0:S]).then_inc(sem("mix_ev"), 1)
                for n, (dst, b) in enumerate(((ch, 2), (cb, 3))):
                    act.wait_ge(sem("mix_mm"), l * PER["mix_mm"] + n + 11)
                    copy(flat(dst), bank[b][:]).then_inc(sem("mix_ev"), 1)
                for n, (dst, b) in enumerate(((qTd, 4), (kTd, 5), (qiT, 6))):
                    act.wait_ge(sem("sa_mm"), l * PER["sa_mm"] + n + 1)
                    copy(flat(dst), bank[b][:]).then_inc(sem("sa_ev"), 1)

                def gate(g):
                    i = (g // 2) % 2
                    for tb in range(TB):
                        act.wait_ge(sem("gate_mm"), l * PER["gate_mm"] + 2 * g + tb + 1)
                        if g == 4 and tb == 0:
                            act.wait_ge(sem("mg_add"), l * PER["mg_add"] + 8)
                        A(gs[:, tb, i, (g % 2) * 512:(g % 2) * 512 + 512], bank[2 * (g % 2) + tb][:], ACT.Sigmoid).then_inc(sem("gate_ev"), 1)

                act.wait_ge(sem("mix_ev"), l * PER["mix_ev"] + 9)
                A(flat(gr), flat(gr), ACT.Silu).then_inc(sem("sr"), 1)
                act.wait_ge(sem("ls_in"), l * PER["ls_in"] + 1)
                q.link(A(flat(zb), flat(za), ACT.Abs))
                q.link(A(flat(zb), flat(zb), ACT.Exp, scale=-1.0))
                A(flat(zb), flat(zb), ACT.Ln, bias=1.0).then_inc(sem("ls_ex"), 1)
                act.wait_ge(sem("gla_cum"), l * PER["gla_cum"] + 1)
                A(flat(eb), flat(za), ACT.Exp, scale=1.0 / 16)
                A(flat(en), flat(za), ACT.Exp, scale=-1.0 / 16)
                A(flat(ke), flat(zb), ACT.Exp, scale=1.0 / 16).then_inc(sem("gla_exp"), 1)
                gate(0)
                for n in range(8):
                    act.wait_ge(sem("ix_mm"), l * PER["ix_mm"] + n + 1)
                    if n >= 2:
                        act.wait_ge(sem("ix_acc"), l * PER["ix_acc"] + n - 1)
                    c = slice(0, 2 * S if n < 4 else 2 * P)
                    A(rl[:, n % 2, c], bank[4 + n % 4][:, c], ACT.Relu).then_inc(sem("ix_ev"), 1)
                gate(1)
                act.wait_ge(sem("bt_mm"), l * PER["bt_mm"] + 1)
                copy(bT[:].rearrange("p a b c -> p (a b c)"), bank[7][:]).then_inc(sem("bc_ev"), 1)
                act.wait_ge(sem("ct_mm"), l * PER["ct_mm"] + 1)
                copy(cT[:].rearrange("p a b c -> p (a b c)"), bank[6][:]).then_inc(sem("bc_ev"), 1)
                gate(2)
                act.wait_ge(sem("ketok_mm"), l * PER["ketok_mm"] + 1)
                copy(flat(ketok), bank[6][:]).then_inc(sem("ketok_ev"), 1)
                for tb in range(TB):
                    act.wait_ge(sem("mx"), l * PER["mx"] + tb + 1)
                    for hd in range(4):
                        v = dl[:, 0, hd * P:hd * P + P] if tb == 0 else \
                            dl[:, 1:3].rearrange("p a (g s) -> p (a g) s", s=S)[:, hd, :]
                        ins = A(v, v, ACT.Exp, bias=dstat[:, 0, tb, hd:hd + 1], accum_out=dstat[:, 1, tb, hd:hd + 1])
                    ins.then_inc(sem("ex"), 1)
                gate(3)
                for tb in range(TB):
                    act.wait_ge(sem("o_mm"), l * PER["o_mm"] + tb + 1)
                    A(zb[:, tb, :], bank[4 + tb][:, 0:W], ACT.Square).then_inc(sem("o_sq"), 1)
                act.wait_ge(sem("o_ms"), l * PER["o_ms"] + 1)
                A(ost[:, 1].rearrange("p a b -> p (a b)"), ost[:, 0].rearrange("p a b -> p (a b)"), ACT.Sqrt).then_inc(sem("o_rt"), 1)
                for u, b in ((0, 6), (1, 7), (2, 4)):
                    act.wait_ge(sem("pt_mm"), l * PER["pt_mm"] + u + 1)
                    copy(pT[:, u].rearrange("p a b -> p (a b)"), bank[b][:]).then_inc(sem("pt_ev"), 1)
                act.wait_ge(sem("od_mm"), l * PER["od_mm"] + 1)
                copy(flat(ydT), bank[5][:]).then_inc(sem("od_ev"), 1)
                act.wait_ge(sem("ybt_mm"), l * PER["ybt_mm"] + 1)
                copy(flat(ybT), bank[6][:]).then_inc(sem("ybt_ev"), 1)
                for b in range(2):
                    act.wait_ge(sem("ckv_mm"), l * PER["ckv_mm"] + b + 1)
                    copy(kTx[:, 2 * b:2 * b + 2, :].rearrange("p a b -> p (a b)"), bank[b][:]).then_inc(sem("ckv_ev"), 1)
                act.wait_ge(sem("s5y"), l * PER["s5y"] + 1)
                A(flat(gel), flat(gel), ACT.Gelu_apprx_tanh).then_inc(sem("gelu"), 1)
                act.wait_ge(sem("glu_mm"), l * PER["glu_mm"] + 1)
                for j in range(2):
                    ins = A(ycT[:, j, :], bank[6][:, j * S:j * S + S], ACT.Sigmoid, bias=b_glu[:, j:j + 1])
                ins.then_inc(sem("glu_ev"), 1)

                def split_pieces(name, which=range(4)):
                    i = DENSE.index(name)
                    s_ = slot_of[i]
                    act.wait_ge(ld[s_], l * (16 * loads[s_]) + 16 * nth[i])
                    for i in which:
                        n = 4 * SPLIT.index(name) + i
                        if n >= RP:
                            used, count = split_piece_used(n - RP)
                            act.wait_ge(sem(used), l * PER[used] + count)
                        copy(w_hi[:, n % RP, :], ring[:, s_, i * PIECE:i * PIECE + PIECE]).then_inc(sem("dw_hi"), 1)

                act.wait_ge(sem("mg_mm"), l * PER["mg_mm"] + 8)
                act.wait_ge(sem("yc"), l * PER["yc"] + 1)
                for j in range(2):
                    copy(hT_hi[:, 4 * j:4 * j + 4, :].rearrange("p a b -> p (a b)"),
                         hT[:, 4 * j:4 * j + 4, :].rearrange("p a b -> p (a b)")).then_inc(sem("tp_a"), 1)
                split_pieces("g5")
                gate(4)
                split_pieces("g6")
                gate(5)
                split_pieces("g7")
                gate(6)
                split_pieces("wo0")
                gate(7)
                split_pieces("wo1", (0, 1))
                for j in range(4):
                    act.wait_ge(sem("tp_mm"), l * PER["tp_mm"] + 4 + j + 1)
                    copy(hT_hi[:, 2 * j:2 * j + 2, :].rearrange("p a b -> p (a b)"), bank[4 + j][:]).then_inc(sem("tp_a"), 1)
                split_pieces("wo1", (2, 3))
                A(junk[:, 1:2], junk[:, 0:1], ACT.Sqrt)
                act.wait_ge(sem("wo_ev"), l * PER["wo_ev"] + 4)
                norm_stats(1)
                norm_evacuate(2, 1)
                act.wait_ge(sem("ckv_mm"), l * PER["ckv_mm"] + 3)
                copy(vx[:, 0, :], bank[2][:]).then_inc(sem("ckv_ev"), 1)
                for b in range(2):
                    act.wait_ge(sem("cq_mm"), l * PER["cq_mm"] + b + 1)
                    copy(qTx[:, 2 * b:2 * b + 2, :].rearrange("p a b -> p (a b)"), bank[b][:]).then_inc(sem("cq_ev"), 1)
                A(junk[:, 1:2], junk[:, 0:1], ACT.Exp)
                act.wait_ge(sem("cmx"), l * PER["cmx"] + 1)
                for tb in range(TB):
                    for hd in range(4):
                        ins = A(px[:, tb, hd, :], bank[4 + 2 * tb + hd // 2][:, (hd % 2) * S:(hd % 2) * S + S], ACT.Exp,
                                bias=cst[:, 0, tb, hd:hd + 1], scale=128 ** -0.5, accum_out=cst[:, 1, tb, hd:hd + 1])
                ins.then_inc(sem("cex"), 1)
                act.wait_ge(sem("ckv_mm"), l * PER["ckv_mm"] + 4)
                copy(vx[:, 1, :], bank[3][:]).then_inc(sem("ckv_ev"), 1)
                for n in (1, 3):
                    act.wait_ge(sem("cpt_mm"), l * PER["cpt_mm"] + n + 1)
                    copy(pTx[:, n // 2, 2:4, :].rearrange("p a b -> p (a b)"), bank[n][:]).then_inc(sem("cpt_a"), 1)
                for hp in range(2):
                    act.wait_ge(sem("co_mm"), l * PER["co_mm"] + hp + 1)
                    copy(oTx[:, 2 * hp:2 * hp + 2, :].rearrange("p a b -> p (a b)"), bank[4 + hp][:]).then_inc(sem("co_ev"), 1)
                A(junk[:, 1:2], junk[:, 0:1], ACT.Sqrt)
                act.wait_ge(sem("cy_ev"), l * PER["cy_ev"] + 4)
                norm_stats(2)
                act.wait_ge(sem("rt_loaded"), l * N_RT * 16 + N_RT * 16)
                norm_evacuate(3, 2)
                act.wait_ge(sem("rt_x1"), l * PER["rt_x1"] + 1)
                A(rx[:, 2].rearrange("p a b -> p (a b)"), rx[:, 1].rearrange("p a b -> p (a b)"), ACT.Exp)
                A(rx[:, 7].rearrange("p a b -> p (a b)"), rx[:, 6].rearrange("p a b -> p (a b)"), ACT.Exp).then_inc(sem("rt_x2"), 1)
                def pieces(p, e, j, which):
                    s_ = e_slot[j]
                    act.wait_ge(ld[s_], l * (16 * loads[s_]) + 16 * (dense_loads[s_] + 1) + p * (16 * N_EXP) + e * 16)
                    for i in which:
                        n = 4 * j + i
                        act.wait_ge(sem("w_used"), turns_before("w_used", l, p, e) + n + 1)
                        copy(w_hi[:, n % RP, :], ring[:, s_, i * PIECE:i * PIECE + PIECE]).then_inc(sem("w_hi"), 1)

                def gathered(p, e):
                    act.wait_ge(sem("ga_mm"), turns_before("ga_mm", l, p, e) + 1)
                    copy(ga[:, :, 0, :], bank[0][:].rearrange("p (k c) -> p k c", c=CAP)).then_inc(sem("ga_hi"), 1)

                def turn(p, e, first=False, last=False):
                    pieces(p, e, 1, (0, 1))
                    act.wait_ge(sem("w_used"), turns_before("w_used", l, p, e) + RP + 4)
                    copy(gu[:, 0, :], bank[2][:]).then_inc(sem("gu_sb"), 1)
                    pieces(p, e, 1, (2, 3))
                    act.wait_ge(sem("pickT_mm"), turns_before("pickT_mm", l, p, e) + 1)
                    copy(pickT[:, :], bank[5][:, 0:S]).then_inc(sem("pickT"), 1)
                    pieces(p, e, 2, (0, 1))
                    act.wait_ge(sem("guT_mm"), turns_before("guT_mm", l, p, e) + 1)
                    A(act_g[:].rearrange("p a b -> p (a b)"), bank[4][:, 0:4 * CAP], ACT.Silu).then_inc(sem("act_gate"), 1)
                    act.wait_ge(sem("w_used"), turns_before("w_used", l, p, e) + RP + 8)
                    copy(gu[:, 1, :], bank[3][:]).then_inc(sem("gu_sb"), 1)
                    pieces(p, e, 2, (2, 3))
                    act.wait_ge(sem("hid"), turns_before("hid", l, p, e) + 1)
                    copy(hidT[:, :, 0, :], hid[:]).then_inc(sem("hidT_hi"), 1)
                    if not last:
                        gathered(p, e + 1)
                        pieces(p, e + 1, 0, range(4))
                    for nh in range(2):
                        if nh == 0:
                            act.wait_ge(sem("y_mm"), turns_before("y_mm", l, p, e) + 1)
                        else:
                            act.wait_ge(sem("w_used"), turns_before("w_used", l, p, e) + RP + 12)
                        copy(y_hi[:, nh * 512:nh * 512 + 512], bank[5 + nh][:]).then_inc(sem("y_hi"), 1)

                def one_pass(p):
                    pieces(p, 0, 0, range(4))
                    gathered(p, 0)
                    q.turns(p, turn)

                one_pass(0)
                act.wait_ge(sem("flag"), l + 1)
                more = q.more_passes()
                with act.If(more):
                    with act.Fori(1, PASSES) as p:
                        one_pass(p)
                with act.Else():
                    act.wait_ge(sem("w_hi"), turns_before("w_hi", l, 1, 0))
                    act.sem_inc(sem("w_hi"), skipped("w_hi"))
                    act.wait_ge(sem("ga_hi"), turns_before("ga_hi", l, 1, 0))
                    act.sem_inc(sem("ga_hi"), skipped("ga_hi"))
                    act.wait_ge(sem("gu_sb"), turns_before("gu_sb", l, 1, 0))
                    act.sem_inc(sem("gu_sb"), skipped("gu_sb"))
                    act.wait_ge(sem("pickT"), turns_before("pickT", l, 1, 0))
                    act.sem_inc(sem("pickT"), skipped("pickT"))
                    act.wait_ge(sem("act_gate"), turns_before("act_gate", l, 1, 0))
                    act.sem_inc(sem("act_gate"), skipped("act_gate"))
                    act.wait_ge(sem("hidT_hi"), turns_before("hidT_hi", l, 1, 0))
                    act.sem_inc(sem("hidT_hi"), skipped("hidT_hi"))
                    act.wait_ge(sem("y_hi"), turns_before("y_hi", l, 1, 0))
                    act.sem_inc(sem("y_hi"), skipped("y_hi"))
                A(junk[:, 1:2], junk[:, 0:1], ACT.Sqrt)
                act.wait_ge(sem("x_acc"), l * (PASSES * N_EXP * 4) + PASSES * N_EXP * 4)
                q.leave()
            for tb in range(TB):
                A(h[:, tb, :], x[:, tb, :], ACT.Square, accum_out=st[:, 0, tb:tb + 1]).then_inc(sem("ends_sumsq"), 1)
            act.wait_ge(sem("ends_meansq"), 2)
            A(st[:, 2, :], st[:, 1, :], ACT.Sqrt).then_inc(sem("ends_root"), 1)

        @block.gpsimd
        def _(pool):
            q = Order(pool, "pool")
            g = nc.gpsimd

            def load(dst, src, name):
                pool.dma_start(dst, src, allow_slow_non_contiguous=True).then_inc(sem(name), 16)

            load(pos_i[:], T["positions"].rearrange("o (t p) -> p (o t)", p=P), "pos_loaded")
            load(g_fm[:, 3, :], T["norm_mem"].rearrange("(p k) -> p k", p=P), "gm_loaded")
            q.link(g.memset(ident[:], 0.0))
            g.affine_select(out=ident[:], in_=ident[:], compare_op=ALU.not_equal, fill=1.0, base=0,
                            pattern=[[-1, P]], channel_multiplier=1).then_inc(sem("ident_ready"), 1)
            q.link(g.memset(gla_mask[:], 1.0))
            q.link(g.memset(ones[:], 1.0))
            q.link(g.affine_select(out=tri[:], in_=ones[:], compare_op=ALU.is_ge, fill=0.0, base=0,
                                   pattern=[[1, P]], channel_multiplier=-1))
            q.link(g.iota(slot_no[:], pattern=[[0, 2], [1, CAP]], base=0, channel_multiplier=0,
                          allow_small_or_imprecise_dtypes=True))
            q.link(g.affine_select(out=gla_mask[:], in_=gla_mask[:], compare_op=ALU.is_ge, fill=0.0, base=0,
                                   pattern=[[1, P]], channel_multiplier=-1))
            q.link(g.affine_select(out=gla_mask[:, 64:128], in_=gla_mask[:, 64:128], compare_op=ALU.is_ge, fill=0.0,
                                   base=-64, pattern=[[0, 64]], channel_multiplier=1))
            q.link(g.memset(cneg[:], 0.0))
            q.link(g.affine_select(out=cneg[:], in_=cneg[:], compare_op=ALU.is_ge, fill=NEG, base=0,
                                   pattern=[[-1, P]], channel_multiplier=1))
            q.link(g.memset(scan_keep[:], 1.0))
            q.link(g.memset(scan_keep[:].rearrange("p (c j) -> p c j", j=64)[:, :, 0], 0.0))
            q.link(g.memset(mask_b[0:64, 0:1], 1.0))
            q.link(g.memset(mask_b[64:128, 0:1], 0.0))
            q.link(g.memset(mask_b[0:64, 1:2], 0.0))
            q.link(g.memset(mask_b[64:128, 1:2], 1.0))
            g.memset(junk[:], 0.0)
            g.iota(mc_i[:], pattern=[[0, 1]], base=0, channel_multiplier=1).then_inc(sem("masks_ready"), 1)

            def layer_parameters(one):
                fm = lambda t: t[one].rearrange("o (p k) -> p (o k)", p=P)
                jp = lambda t: t[one].rearrange("o (j p) -> p (o j)", p=P)

                def par(dst, src):
                    load(dst, src, "par_loaded")

                load(g_fm[:, 0, :], fm(T["norm_mix"]), "g_mix_loaded")
                for i, n in enumerate(("s5_lambda_re", "s5_lambda_im")):
                    par(lam[:, i, :], T[n][one].rearrange("o (t g) s -> (g s) (o t)", g=2))
                for g2 in range(2):
                    par(lam[64 * g2:64 * g2 + 64, 2, :],
                        T["s5_log_dt"][one].rearrange("o (t g) -> g (o t)", g=2)[g2:g2 + 1].broadcast_to([64, 8]))
                for i, n in enumerate(("s5_b_re", "s5_b_im")):
                    par(s5_b[:, i], T[n][one].rearrange("o (t g) s c -> (g s) (o t) c", g=2))
                for i, n in enumerate(("s5_c_re", "s5_c_im")):
                    par(s5_c[:, i], T[n][one].rearrange("o (a g) c s -> (g c) (o a) s", a=2))
                par(g_fm[:, 1, :], fm(T["norm_cross"]))
                par(conv_w[:], T["conv_w"][one].rearrange("o k (j p) -> p (o k) j", p=P))
                par(conv_b[:], jp(T["conv_b"]))
                par(a_up[:], T["gla_a_up"][one].rearrange("o r n -> r (o n)"))
                par(a_b[:], jp(T["gla_a_b"]))
                par(gla_g[:], T["gla_norm"][one].broadcast_to([P, W]))
                par(s5_d[:], jp(T["s5_d"]))
                par(b_glu[:], jp(T["s5_b_glu"]))
                par(w_glu[:], T["s5_w_glu"][one].rearrange("o (k p) n -> p (o k) n", p=P))

            layer_parameters(slice(0, 1))

            with pool.Fori(0, L) as l:
                q.enter(l, 256)
                pool.wait_ge(sem("ffn_done"), l * PER["ffn_done"] + 1)
                q.settle()
                one = bass.ds(l, 1)
                load(g_fm[:, 2, :], T["norm_ffn"][one].rearrange("o (p k) -> p (o k)", p=P), "rt_loaded")
                load(b_rt[:, 0:4], T["b_route_group"][one].broadcast_to([P, 4]), "rt_loaded")
                load(b_rt[:, 4:20], T["b_route_expert"][one].broadcast_to([P, 16]), "rt_loaded")
                load(w_rt[:, :, 0:4], T["w_route_group"][one].rearrange("o (p k) n -> p (o k) n", p=P), "rt_loaded")
                load(w_rt[:, :, 4:20], T["w_route_expert"][one].rearrange("o (p k) n -> p (o k) n", p=P), "rt_loaded")

                pool.wait_ge(sem("e_in"), l * PER["e_in"] + 1)
                q.settle()
                q.link(g.memset(E[:, 0, :, 0:1], 1.0))
                q.link(g.memset(E[:, 1, :, 0:1], 0.0))
                m = 1
                tA, tB = h[:, 0, :], h[:, 1, :]
                pool.wait_ge(sem("h_free"), l * PER["h_free"] + 1)
                q.settle()
                while m < S:
                    wre, wim = (bc(wpow[:, r, :].unsqueeze(2), [P, 8, m]) for r in range(2))
                    ta, tb_ = (t[:, 0:8 * m].rearrange("p (t s) -> p t s", t=8) for t in (tA, tB))
                    g.tensor_tensor(ta, E[:, 0, :, 0:m], wre, ALU.mult)
                    q.link(g.tensor_tensor(tb_, E[:, 1, :, 0:m], wim, ALU.mult))
                    q.link(g.tensor_tensor(E[:, 0, :, m:2 * m], ta, tb_, ALU.subtract))
                    g.tensor_tensor(ta, E[:, 0, :, 0:m], wim, ALU.mult)
                    q.link(g.tensor_tensor(tb_, E[:, 1, :, 0:m], wre, ALU.mult))
                    q.link(g.tensor_tensor(E[:, 1, :, m:2 * m], ta, tb_, ALU.add))
                    g.tensor_tensor(wtmp[:, 0, :], wpow[:, 0, :], wpow[:, 0, :], ALU.mult)
                    g.tensor_tensor(wtmp[:, 1, :], wpow[:, 1, :], wpow[:, 1, :], ALU.mult)
                    q.link(g.tensor_tensor(wtmp[:, 2, :], wpow[:, 0, :], wpow[:, 1, :], ALU.mult))
                    g.tensor_tensor(wpow[:, 0, :], wtmp[:, 0, :], wtmp[:, 1, :], ALU.subtract)
                    q.link(g.tensor_tensor(wpow[:, 1, :], wtmp[:, 2, :], wtmp[:, 2, :], ALU.add))
                    m *= 2
                g.memset(junk[:], 0.0).then_inc(sem("e_tab"), 1)
                pool.wait_ge(sem("mix_ev"), l * PER["mix_ev"] + 12)
                q.settle()
                q.link(g.tensor_tensor(ch[:], ch[:], cc[:], ALU.mult))
                for j in range(2):
                    u, y = ch[:, j, :], yaT[:, j, :]
                    t = cc[:, j, :]
                    q.link(g.tensor_scalar(y, u, conv_w[:, 2, j:j + 1], conv_b[:, j:j + 1], ALU.mult, ALU.add))
                    for d in (1, 2):
                        q.link(g.tensor_scalar(t[:, 0:S - d], u[:, 0:S - d], conv_w[:, 2 - d, j:j + 1], None, ALU.mult))
                        q.link(g.tensor_tensor(y[:, d:S], y[:, d:S], t[:, 0:S - d], ALU.add))
                g.tensor_tensor(yaT[:], yaT[:], cb[:], ALU.mult).then_inc(sem("u_conv"), 1)
                for t in range(8):
                    pool.wait_ge(sem("z_out"), l * PER["z_out"] + t + 1)
                    q.settle()
                    if t >= 2:
                        pool.wait_ge(sem("yk"), l * PER["yk"] + t - 1)
                        q.settle()
                    g.tensor_tensor(gel[:], zo[t % 2], bc(E[:, 0:1, t, :], [P, 2, S]), ALU.mult)
                    q.link(g.tensor_tensor(ycT[:], zo[t % 2], bc(E[:, 1:2, t, :], [P, 2, S]), ALU.mult))
                    q.link(g.tensor_tensor(xb[:, t % 2, 0, :], gel[:, 0, :], ycT[:, 1, :], ALU.subtract))
                    g.tensor_tensor(xb[:, t % 2, 1, :], gel[:, 1, :], ycT[:, 0, :], ALU.add).then_inc(sem("xs"), 1)
                    pool.wait_ge(sem("xs"), l * PER["xs"] + t + 1)
                    q.settle()
                for n in range(16):
                    i, tb, nh = n // 4, (n // 2) % 2, n % 2
                    pool.wait_ge(sem("mg_ev"), l * PER["mg_ev"] + n + 1)
                    q.settle()
                    src = gs[:, tb, i % 2, nh * 512:nh * 512 + 512]
                    dst_ = h[:, tb, nh * 512:nh * 512 + 512]
                    if i == 0:
                        g.tensor_copy(dst_, src).then_inc(sem("mg_add"), 1)
                    else:
                        pool.wait_ge(sem("mg_add"), l * PER["mg_add"] + n - 3)
                        q.settle()
                        g.tensor_tensor(dst_, dst_, src, ALU.add).then_inc(sem("mg_add"), 1)
                pool.wait_ge(sem("cy_ev"), l * PER["cy_ev"] + 4)
                q.settle()
                load(g_bc[:], T["norm_ffn"][one].broadcast_to([P, D]), "g_loaded")
                pool.wait_ge(sem("tp_mm"), l * PER["tp_mm"] + 16)
                q.settle()
                pool.wait_ge(sem("g_loaded"), l * 16 + 16)
                q.settle()
                for tb in range(TB):
                    g.tensor_tensor(h[:, tb, :], h[:, tb, :], g_bc[:], ALU.mult).then_inc(sem("h_gained"), 1)
                layer_parameters(bass.ds((L - 1) - l, 1))

                def piece(p, e, j):
                    n = 4 * j + 3
                    if j > 0:
                        pool.wait_ge(sem("w_hi"), turns_before("w_hi", l, p, e) + n + 1)
                        q.settle()
                        g.tensor_tensor(w_lo[:, n % RP, :], ring[:, e_slot[j], 3 * PIECE:4 * PIECE],
                                        w_hi[:, n % RP, :].bitcast(F32), ALU.subtract).then_inc(sem("w_lo_p"), 1)
                        pool.wait_ge(sem("w_lo_p"), turns_before("w_lo_p", l, p, e) + j)
                        q.settle()
                    pool.wait_ge(sem("w_lo"), turns_before("w_lo", l, p, e) + LO_UP_TO[j])
                    q.settle()
                    pool.sem_inc(sem("split"), 1)

                def turn(p, e, first=False, last=False):
                    piece(p, e, 1)
                    piece(p, e, 2)
                    if not last:
                        piece(p, e + 1, 0)

                def one_pass(p):
                    piece(p, 0, 0)
                    q.turns(p, turn)

                one_pass(0)
                pool.wait_ge(sem("flag"), l + 1)
                more = q.more_passes()
                with pool.If(more):
                    with pool.Fori(1, PASSES) as p:
                        one_pass(p)
                with pool.Else():
                    pool.wait_ge(sem("w_lo_p"), turns_before("w_lo_p", l, 1, 0))
                    pool.sem_inc(sem("w_lo_p"), skipped("w_lo_p"))
                    pool.wait_ge(sem("split"), turns_before("split", l, 1, 0) + NS)
                    pool.sem_inc(sem("split"), skipped("split"))
                q.leave()
            pool.wait_ge(sem("par_loaded"), (L + 1) * N_PAR * 16)
            pool.wait_ge(sem("g_mix_loaded"), (L + 1) * 16)
            pool.wait_ge(sem("ffn_done"), L + 1)
            load(g_out, T["norm_final"].rearrange("(o n) -> o n", o=1).broadcast_to([P, D]), "go_loaded")

        @block.vector
        def _(dve):
            q = Order(dve, "dve")
            v = nc.vector
            flat = lambda t: t[:].rearrange("p a b -> p (a b)")
            flat3 = lambda t: t[:].rearrange("p a b c -> p (a b c)")
            link = q.link

            dve.sem_inc(sem("ffn_done"), 1)
            dve.sem_inc(sem("split"), NS)
            dve.sem_inc(sem("w_used"), RP)
            dve.wait_ge(sem("ends_sumsq"), 2)
            v.tensor_scalar(st[:, 1, :], st[:, 0, :], 1.0 / D, EPS, ALU.mult, ALU.add).then_inc(sem("ends_meansq"), 1)
            inv = (500000.0 ** (-np.arange(8) * 0.125)).astype(np.float32)
            for i in range(8):
                v.memset(invf[:, i:i + 1], float(inv[i]))
            dve.wait_ge(sem("pos_loaded"), 16)
            link(v.tensor_copy(pos_f[:], pos_i[:]))
            link(v.tensor_tensor(ang[:], bc(pos_f[:].unsqueeze(2), [P, TB, 8]),
                                 bc(invf[:].unsqueeze(1), [P, TB, 8]), ALU.mult))

            def reduce_angle(a, r_sin, r_cos, t0, t1):
                magic = 1.5 * 2.0 ** 23
                c1 = 6.28125
                c2 = 0.0019350051879882812
                c3 = float(2 * np.pi - c1 - c2)
                link(v.tensor_scalar(t0, a, 1.0 / (2 * PI), magic, ALU.mult, ALU.add))
                link(v.tensor_scalar(t0, t0, magic, None, ALU.subtract))
                link(v.scalar_tensor_tensor(out=t1, in0=t0, scalar=-c1, in1=a, op0=ALU.mult, op1=ALU.add))
                link(v.scalar_tensor_tensor(out=t1, in0=t0, scalar=-c2, in1=t1, op0=ALU.mult, op1=ALU.add))
                link(v.scalar_tensor_tensor(out=t1, in0=t0, scalar=-c3, in1=t1, op0=ALU.mult, op1=ALU.add))
                link(v.tensor_scalar(r_sin, t1, 3.1415925, -3.1415925, ALU.min, ALU.max))
                link(v.scalar_tensor_tensor(out=t0, in0=t1, scalar=-1.0, in1=t1, op0=ALU.mult, op1=ALU.max))
                link(v.tensor_scalar(r_cos, t0, -1.0, PI / 2, ALU.mult, ALU.add))

            reduce_angle(ang[:].rearrange("p t f -> p (t f)"), rr[:, 0, :], rr[:, 1, :], rr[:, 2, :], rr[:, 3, :])
            dve.sem_inc(sem("ang_ready"), 1)
            dve.wait_ge(sem("masks_ready"), 1)
            link(v.tensor_scalar(mc_j[:], mc_i[:], 4, 1, ALU.logical_shift_right, ALU.bitwise_and))
            link(v.tensor_copy(mask_c[:, 1:2], mc_j[:]))
            link(v.tensor_scalar(mask_c[:, 0:1], mask_c[:, 1:2], -1.0, 1.0, ALU.mult, ALU.add))
            dve.wait_ge(sem("ends_root"), 1)
            link(v.reciprocal(st[:, 3, :], st[:, 2, :]))
            for tb in range(TB):
                v.tensor_scalar(h[:, tb, :], h[:, tb, :], st[:, 3, tb:tb + 1], None, ALU.mult).then_inc(sem("m_h_ready"), 1)
            dve.wait_ge(sem("gm_loaded"), 16)
            for j in range(4):
                dve.wait_ge(sem("m_tp_mm"), j + 1)
                v.tensor_tensor(memT[:, 2 * j:2 * j + 2, :], bank[4 + j][:].rearrange("p (k s) -> p k s", k=2),
                                bc(g_fm[:, 3, 2 * j:2 * j + 2].unsqueeze(2), [P, 2, S]), ALU.mult).then_inc(sem("m_tp_v"), 1)
            dve.wait_ge(sem("rope_ready"), 2)

            def norm_h(u):
                dve.wait_ge(sem("sumsq"), l * PER["sumsq"] + 2 * u + 2)
                v.tensor_scalar(st[:, 1, :], st[:, 0, :], 1.0 / D, EPS, ALU.mult, ALU.add).then_inc(sem("meansq"), 1)
                dve.wait_ge(sem("root"), l * PER["root"] + u + 1)
                v.reciprocal(st[:, 3, :], st[:, 2, :]).then_inc(sem("scale"), 1)
                dve.wait_ge(sem("scale"), l * PER["scale"] + u + 1)
                v.tensor_scalar(h[:, 0, :], x[:, 0, :], st[:, 3, 0:1], None, ALU.mult).then_inc(sem("h0_ready"), 1)

            def norm_evacuate(u, g):
                for j in (0, 2):
                    dve.wait_ge(sem("tp_mm"), l * PER["tp_mm"] + 4 * u + j + 1)
                    v.tensor_tensor(hT[:, 2 * j:2 * j + 2, :], bank[4 + j][:].rearrange("p (k s) -> p k s", k=2),
                                           bc(g_fm[:, g, 2 * j:2 * j + 2].unsqueeze(2), [P, 2, S]), ALU.mult).then_inc(sem("tp_v"), 1)

            def top_k(w):
                for i in range(TOPK // 8):
                    q.settle()
                    link(v.max(top8[:], w))
                    q.settle()
                    link(v.match_replace(w, top8[:], w, TAKEN))

            def rope(t, half, step, n):
                a, b = t[:, :, :, 0:half], t[:, :, :, half:2 * half]
                cos = bc(rope_cs[:, 0, :, ::step].unsqueeze(2), [P, TB, n, half])
                sin = bc(rope_cs[:, 1, :, ::step].unsqueeze(2), [P, TB, n, half])
                r = [rp[:, i, :, 0:n * half].rearrange("p t (n f) -> p t n f", n=n) for i in range(4)]
                v.tensor_tensor(r[0], a, cos, ALU.mult)
                v.tensor_tensor(r[1], b, sin, ALU.mult)
                v.tensor_tensor(r[2], b, cos, ALU.mult)
                link(v.tensor_tensor(r[3], a, sin, ALU.mult))
                v.tensor_tensor(a, r[0], r[1], ALU.subtract)
                link(v.tensor_tensor(b, r[2], r[3], ALU.add))

            with dve.Fori(0, L) as l:
                q.enter(l, 512)
                norm_h(0)
                dve.wait_ge(sem("g_mix_loaded"), l * 16 + 16)
                norm_evacuate(0, 0)
                dve.wait_ge(sem("par_loaded"), l * N_PAR * 16 + N_PAR * 16)
                dve.wait_ge(sem("sp_in"), l * PER["sp_in"] + 1)
                s_ = lambda i: sp[:, i, :]
                link(v.tensor_tensor(s_(1), lam[:, 0, :], s_(0), ALU.mult))
                link(v.tensor_tensor(s_(3), lam[:, 1, :], s_(0), ALU.mult))
                reduce_angle(s_(3), s_(6), s_(7), s_(4), s_(5))
                v.memset(s_(19), 0.0).then_inc(sem("sp2_in"), 1)
                dve.wait_ge(sem("sp2_out"), l * PER["sp2_out"] + 1)
                v.tensor_copy(wpow[:, 0, :], s_(9))
                v.tensor_copy(wpow[:, 1, :], s_(8)).then_inc(sem("e_in"), 1)
                dve.wait_ge(sem("tp_mm"), l * PER["tp_mm"] + 4)
                dve.sem_inc(sem("h_free"), 1)
                link(v.tensor_tensor(s_(10), s_(2), s_(9), ALU.mult))
                link(v.tensor_tensor(s_(11), s_(2), s_(8), ALU.mult))
                link(v.tensor_scalar(s_(10), s_(10), 1.0, None, ALU.subtract))
                link(v.tensor_tensor(s_(12), lam[:, 0, :], lam[:, 0, :], ALU.mult))
                link(v.tensor_tensor(s_(13), lam[:, 1, :], lam[:, 1, :], ALU.mult))
                link(v.tensor_tensor(s_(12), s_(12), s_(13), ALU.add))
                link(v.reciprocal(s_(12), s_(12)))
                link(v.tensor_tensor(s_(13), s_(10), lam[:, 0, :], ALU.mult))
                link(v.tensor_tensor(s_(14), s_(11), lam[:, 1, :], ALU.mult))
                link(v.tensor_tensor(s_(13), s_(13), s_(14), ALU.add))
                link(v.tensor_tensor(s_(13), s_(13), s_(12), ALU.mult))
                link(v.tensor_tensor(s_(14), s_(11), lam[:, 0, :], ALU.mult))
                link(v.tensor_tensor(s_(15), s_(10), lam[:, 1, :], ALU.mult))
                link(v.tensor_tensor(s_(14), s_(14), s_(15), ALU.subtract))
                link(v.tensor_tensor(s_(14), s_(14), s_(12), ALU.mult))
                fr = bc(s_(13).unsqueeze(2), [P, 8, 16])
                fi = bc(s_(14).unsqueeze(2), [P, 8, 16])
                t4 = [rl[:, 0, i * 128:i * 128 + 128].rearrange("p (t c) -> p t c", t=8) for i in range(4)]
                v.tensor_tensor(t4[0], s5_b[:, 0], fr, ALU.mult)
                v.tensor_tensor(t4[1], s5_b[:, 1], fi, ALU.mult)
                v.tensor_tensor(t4[2], s5_b[:, 1], fr, ALU.mult)
                link(v.tensor_tensor(t4[3], s5_b[:, 0], fi, ALU.mult))
                link(v.tensor_tensor(t4[0], t4[0], t4[1], ALU.subtract))
                link(v.tensor_tensor(t4[2], t4[2], t4[3], ALU.add))
                for ri in range(2):
                    for g2 in range(2):
                        v.tensor_scalar(b2[:, ri, :, g2, :], t4[2 * ri], mask_b[:, g2:g2 + 1], None, ALU.mult)
                        v.tensor_scalar(c2[:, ri, :, g2, :], s5_c[:, ri], mask_c[:, g2:g2 + 1], 1.0 - 2.0 * ri,
                                        ALU.mult, ALU.mult)
                v.memset(s_(19), 0.0).then_inc(sem("b2_ready"), 1)
                dve.wait_ge(sem("mix_ev"), l * PER["mix_ev"] + 4)
                rope(dq[:].rearrange("p t (n d) -> p t n d", n=4), 8, 1, 4)
                rope(dt_[:, :, 0:64].unsqueeze(2), 8, 1, 1)
                rope(dt_[:, :, 128:384].rearrange("p t (n d) -> p t n d", n=8), 4, 2, 8)
                rope(dt_[:, :, 384:416].unsqueeze(2), 4, 2, 1)
                v.tensor_copy(kk[:], bc(dt_[:, :, 0:64].unsqueeze(2), [P, TB, 2, 64]))
                v.tensor_scalar(w16[:], dt_[:, :, 416:424], 0.0625, None, ALU.mult)
                v.tensor_copy(ki4[:], bc(dt_[:, :, 384:416].unsqueeze(2), [P, TB, 4, 32])).then_inc(sem("rope"), 1)
                dve.wait_ge(sem("la_mm"), l * PER["la_mm"] + 1)
                for j in range(2):
                    ins = v.tensor_scalar(za[:, j, :], bank[7][:, j * S:j * S + S], a_b[:, j:j + 1], None, ALU.add)
                q.link(ins)
                v.memset(s_(19), 0.0).then_inc(sem("la_ev"), 1)
                dve.sem_inc(sem("ls_in"), 1)
                dve.wait_ge(sem("ls_ex"), l * PER["ls_ex"] + 1)
                link(v.scalar_tensor_tensor(out=zb[:], in0=za[:], scalar=0.0, in1=zb[:], op0=ALU.min, op1=ALU.subtract))
                for j in range(2):
                    ins = v.tensor_tensor_scan(out=za[:, j, :], data0=scan_keep[:], data1=zb[:, j, :], initial=0.0,
                                               op0=ALU.mult, op1=ALU.add)
                link(ins)
                zc = za[:].rearrange("p a (c j) -> p (a c) j", j=64)
                v.tensor_tensor(zb[:].rearrange("p a (c j) -> p (a c) j", j=64),
                                       bc(zc[:, :, 63:64], [P, 8, 64]), zc, ALU.subtract).then_inc(sem("gla_cum"), 1)
                for n in range(8):
                    dve.wait_ge(sem("ix_ev"), l * PER["ix_ev"] + n + 1)
                    blk = 1 if n < 4 else 0
                    wide = S if n < 4 else P
                    acc = isc[:, 1:3, :].rearrange("p a s -> p (a s)") if n < 4 else isc[:, 0, :]
                    for i in range(2):
                        hd = n % 4 + 4 * i
                        src = rl[:, n % 2, i * wide:i * wide + wide]
                        if hd == 0:
                            link(v.tensor_scalar(acc, src, w16[:, blk, 0:1], None, ALU.mult))
                        else:
                            ins = v.scalar_tensor_tensor(out=acc, in0=src, scalar=w16[:, blk, hd:hd + 1], in1=acc,
                                                         op0=ALU.mult, op1=ALU.add)
                            if i == 0:
                                link(ins)
                    ins.then_inc(sem("ix_acc"), 1)
                    dve.wait_ge(sem("ix_acc"), l * PER["ix_acc"] + n + 1)
                dve.wait_ge(sem("gla_exp"), l * PER["gla_exp"] + 1)
                dve.wait_ge(sem("mix_ev"), l * PER["mix_ev"] + 8)
                link(v.scalar_tensor_tensor(out=gq[:], in0=gq[:], scalar=0.125, in1=eb[:], op0=ALU.mult, op1=ALU.mult))
                link(v.tensor_tensor(en[:], en[:], gk[:], ALU.mult))
                v.tensor_tensor(ke[:], ke[:], gk[:], ALU.mult).then_inc(sem("gla_qk"), 1)
                for blk in range(2):
                    d_ = isc[:, 2 * blk, :]
                    link(v.tensor_tensor(d_, d_, cneg[:], ALU.add))
                    w_ = isc[:, 0, :] if blk == 0 else isc[:, 1:3, :].rearrange("p a s -> p (a s)")
                    top_k(w_)
                    link(v.tensor_scalar(w_, w_, TAKEN, NEG, ALU.not_equal, ALU.mult))
                    link(v.tensor_tensor(d_, d_, cneg[:], ALU.add))
                for tb in range(TB):
                    dve.wait_ge(sem("att_mm"), l * PER["att_mm"] + tb + 1)
                    if tb == 0:
                        dve.wait_ge(sem("bc_ev"), l * PER["bc_ev"] + 2)
                    v.tensor_tensor(attm[:, tb], bank[4 + tb][:].rearrange("p (h s) -> p h s", h=4),
                                           bc(gla_mask[:].unsqueeze(1), [P, 4, P]), ALU.mult).then_inc(sem("att_ev"), 1)
                for u in range(3):
                    dve.wait_ge(sem("dl_mm"), l * PER["dl_mm"] + u + 1)
                    n, wide = (4, P) if u == 0 else (2, S)
                    bias = isc[:, 0, :] if u == 0 else isc[:, 1:3, :].rearrange("p a s -> p (a s)")
                    v.scalar_tensor_tensor(out=dl[:, u].rearrange("p (h s) -> p h s", h=n),
                                                  in0=bank[5 + u][:].rearrange("p (h s) -> p h s", h=n), scalar=0.125,
                                                  in1=bc(bias.unsqueeze(1), [P, n, wide]), op0=ALU.mult, op1=ALU.add).then_inc(sem("dl_ev"), 1)
                dve.wait_ge(sem("dl_ev"), l * PER["dl_ev"] + 3)
                v.tensor_reduce(dstat[:, 0, 0, :], dl[:, 0].rearrange("p (h s) -> p h s", h=4), AX, ALU.max,
                                       negate=True).then_inc(sem("mx"), 1)
                v.tensor_reduce(dstat[:, 0, 1, :], dl[:, 1:3].rearrange("p a (g s) -> p (a g) s", s=S), AX, ALU.max,
                                       negate=True).then_inc(sem("mx"), 1)
                dve.wait_ge(sem("u_mm"), l * PER["u_mm"] + 1)
                link(v.memset(rl[:], 0.0))
                for n in range(3):
                    for i in range(2):
                        r = slice(64 * i, 64 * i + 64)
                        if n == 0:
                            v.tensor_copy(state[r, 0, :, r], bank[4][r, 0:P].rearrange("p (h e) -> p h e", h=2))
                            continue
                        for hp in range(2):
                            ins = v.scalar_tensor_tensor(out=state[r, n, hp, r], in0=state[r, n - 1, hp, r],
                                                         scalar=eb[r, hp, 64 * n + 63:64 * n + 64],
                                                         in1=bank[4][r, n * P + hp * 64:n * P + hp * 64 + 64],
                                                         op0=ALU.mult, op1=ALU.add)
                    if n:
                        link(ins)
                    else:
                        link(v.memset(s_(19), 0.0))
                v.memset(s_(19), 0.0).then_inc(sem("st_ready"), 1)
                dve.wait_ge(sem("ex"), l * PER["ex"] + 2)
                link(v.reciprocal(dstat[:, 2].rearrange("p a b -> p (a b)"), dstat[:, 1].rearrange("p a b -> p (a b)")))
                vv = dl[:, 0].rearrange("p (h s) -> p h s", h=4)
                link(v.tensor_tensor(vv, vv, bc(dstat[:, 2, 0, :].unsqueeze(2), [P, 4, P]), ALU.mult))
                vv = dl[:, 1:3].rearrange("p a (g s) -> p (a g) s", s=S)
                v.tensor_tensor(vv, vv, bc(dstat[:, 2, 1, :].unsqueeze(2), [P, 4, S]), ALU.mult).then_inc(sem("p_ready"), 1)
                dve.wait_ge(sem("o_sq"), l * PER["o_sq"] + 2)
                link(v.tensor_reduce(ost[:, 0].rearrange("p a b -> p (a b)"),
                                     zb[:].rearrange("p t (h d) -> p (t h) d", h=4), AX, ALU.add))
                q.link(v.tensor_scalar(ost[:, 0], ost[:, 0], 1.0 / 64, EPS, ALU.mult, ALU.add))
                v.memset(s_(19), 0.0).then_inc(sem("o_ms"), 1)
                dve.wait_ge(sem("sr"), l * PER["sr"] + 1)
                link(v.tensor_tensor(gr[:], gr[:], bc(gla_g[:].unsqueeze(1), [P, TB, W]), ALU.mult))
                dve.wait_ge(sem("o_rt"), l * PER["o_rt"] + 1)
                link(v.reciprocal(ost[:, 0].rearrange("p a b -> p (a b)"), ost[:, 1].rearrange("p a b -> p (a b)")))
                for tb in range(TB):
                    ins = v.tensor_tensor(za[:, tb, :].rearrange("p (h d) -> p h d", h=4),
                                          bank[4 + tb][:, 0:W].rearrange("p (h d) -> p h d", h=4),
                                          bc(ost[:, 0, tb, :].unsqueeze(2), [P, 4, 64]), ALU.mult)
                link(ins)
                v.tensor_tensor(za[:], za[:], gr[:], ALU.mult).then_inc(sem("o_done"), 1)
                dve.wait_ge(sem("e_tab"), l * PER["e_tab"] + 1)
                dve.wait_ge(sem("pt_mm"), l * PER["pt_mm"] + 3)
                for t in range(8):
                    dve.wait_ge(sem("bu_mm"), l * PER["bu_mm"] + t + 1)
                    bu = bank[(4, 7)[t % 2]][:].rearrange("p (r s) -> p r s", r=2)
                    v.tensor_tensor(pq[:, 0], bu, bc(E[:, 0:1, t, :], [P, 2, S]), ALU.mult)
                    link(v.tensor_tensor(pq[:, 1], bu, bc(E[:, 1:2, t, :], [P, 2, S]), ALU.mult))
                    dve.sem_inc(sem("bu_ev"), 1)
                    if t >= 1:
                        dve.wait_ge(sem("z_out"), l * PER["z_out"] + t)
                    v.tensor_tensor(zi[:, 0, :], pq[:, 0, 0, :], pq[:, 1, 1, :], ALU.add)
                    link(v.tensor_tensor(zi[:, 1, :], pq[:, 0, 1, :], pq[:, 1, 0, :], ALU.subtract))
                    if t >= 2:
                        dve.wait_ge(sem("xs"), l * PER["xs"] + t - 1)
                    for ri in range(2):
                        ins = v.tensor_tensor_scan(out=zo[t % 2][:, ri, :], data0=bc(sp[:, 2, t:t + 1], [P, S]), data1=zi[:, ri, :],
                                                   initial=0.0, op0=ALU.mult, op1=ALU.add)
                    ins.then_inc(sem("z_out"), 1)
                def merge(n):
                    i, tb, nh = n // 4, (n // 2) % 2, n % 2
                    dve.wait_ge(sem("mg_mm"), l * PER["mg_mm"] + n + 1)
                    dve.wait_ge(sem("gate_ev"), l * PER["gate_ev"] + 4 * i + 4)
                    gsv = gs[:, tb, i % 2, nh * 512:nh * 512 + 512]
                    v.tensor_tensor(gsv, bank[n % 4][:], gsv, ALU.mult).then_inc(sem("mg_ev"), 1)

                for n in range(4):
                    merge(n)
                dve.wait_ge(sem("yk"), l * PER["yk"] + 8)
                for j in range(2):
                    ins = v.scalar_tensor_tensor(out=gel[:, j, :], in0=uT[:, j, :], scalar=s5_d[:, j:j + 1],
                                                 in1=bank[5][:, j * S:j * S + S], op0=ALU.mult, op1=ALU.add)
                ins.then_inc(sem("s5y"), 1)
                dve.wait_ge(sem("glu_ev"), l * PER["glu_ev"] + 1)
                v.tensor_tensor(ycT[:], ycT[:], gel[:], ALU.mult).then_inc(sem("yc"), 1)
                def split_pieces(name, which=range(4)):
                    s_ = slot_of[DENSE.index(name)]
                    for i in which:
                        n = 4 * SPLIT.index(name) + i
                        dve.wait_ge(sem("dw_hi"), l * PER["dw_hi"] + n + 1)
                        v.tensor_tensor(w_lo[:, n % RP, :], ring[:, s_, i * PIECE:i * PIECE + PIECE],
                                        w_hi[:, n % RP, :].bitcast(F32), ALU.subtract).then_inc(sem("dw_lo"), 1)

                for n in range(4, 8):
                    merge(n)
                for j in range(2):
                    dve.wait_ge(sem("tp_a"), l * PER["tp_a"] + 2 + j + 1)
                    v.tensor_tensor(hT_lo[:, 4 * j:4 * j + 4, :], hT[:, 4 * j:4 * j + 4, :],
                                    hT_hi[:, 4 * j:4 * j + 4, :].bitcast(F32), ALU.subtract).then_inc(sem("tp_v"), 1)
                for name in SPLIT[:4]:
                    split_pieces(name)
                split_pieces("wo1", (0, 1))
                for n in range(8, 16):
                    merge(n)
                for j in range(4):
                    dve.wait_ge(sem("tp_a"), l * PER["tp_a"] + 4 + j + 1)
                    v.tensor_tensor(hT_lo[:, 2 * j:2 * j + 2, :].rearrange("p a b -> p (a b)"), bank[4 + j][:],
                                    hT_hi[:, 2 * j:2 * j + 2, :].rearrange("p a b -> p (a b)").bitcast(F32),
                                    ALU.subtract).then_inc(sem("tp_v"), 1)
                split_pieces("wo1", (2, 3))
                for n in range(4):
                    nh, tb = n // 2, n % 2
                    dve.wait_ge(sem("wo_mm"), l * PER["wo_mm"] + n + 1)
                    xv = x[:, tb, nh * 512:nh * 512 + 512]
                    v.tensor_tensor(xv, xv, bank[n][:], ALU.add).then_inc(sem("wo_ev"), 1)
                norm_h(1)
                norm_evacuate(2, 1)
                for n in range(4):
                    dve.wait_ge(sem("cl_mm"), l * PER["cl_mm"] + n + 1)
                    link(v.tensor_reduce(cst[:, 2, n // 2, 2 * (n % 2):2 * (n % 2) + 2],
                                         bank[4 + n][:].rearrange("p (h s) -> p h s", h=2), AX, ALU.max))
                v.tensor_scalar(cst[:, 0], cst[:, 2], -(128 ** -0.5), None, ALU.mult).then_inc(sem("cmx"), 1)
                dve.wait_ge(sem("cex"), l * PER["cex"] + 1)
                link(v.reciprocal(cst[:, 2].rearrange("p a b -> p (a b)"), cst[:, 1].rearrange("p a b -> p (a b)")))
                for tb in range(TB):
                    ins = v.tensor_tensor(px[:, tb], px[:, tb], bc(cst[:, 2, tb, :].unsqueeze(2), [P, 4, S]), ALU.mult)
                ins.then_inc(sem("cp"), 1)
                for n in (0, 2):
                    dve.wait_ge(sem("cpt_mm"), l * PER["cpt_mm"] + n + 1)
                    ins = v.tensor_copy(pTx[:, n // 2, 0:2, :].rearrange("p a b -> p (a b)"), bank[n][:])
                    ins.then_inc(sem("cpt_v"), 1)
                for n in range(4):
                    tb, nh = n // 2, n % 2
                    dve.wait_ge(sem("cy_mm"), l * PER["cy_mm"] + n + 1)
                    xv = x[:, tb, nh * 512:nh * 512 + 512]
                    v.tensor_tensor(xv, xv, bank[n][:], ALU.add).then_inc(sem("cy_ev"), 1)
                norm_h(2)
                dve.wait_ge(sem("rt_loaded"), l * N_RT * 16 + N_RT * 16)
                norm_evacuate(3, 2)
                dve.wait_ge(sem("rt_mm"), l * PER["rt_mm"] + 1)
                r_ = lambda i: rx[:, i]
                link(v.tensor_tensor(rt[:], bank[0][:, 0:40].rearrange("p (t n) -> p t n", t=2),
                                     bc(b_rt[:].unsqueeze(1), [P, TB, 20]), ALU.add))
                dve.sem_inc(sem("rt_e1"), 1)

                def first_max(vals, mx, eq, run, hot):
                    link(v.tensor_reduce(mx[:, :, 0], vals, AX, ALU.max))
                    link(v.tensor_tensor(eq, vals, bc(mx[:, :, 0:1], [P, TB, 4]), ALU.is_equal))
                    for tb in range(TB):
                        link(v.tensor_tensor_scan(out=run[:, tb, :], data0=ones4[:], data1=eq[:, tb, :], initial=0.0,
                                                  op0=ALU.mult, op1=ALU.add))
                    link(v.scalar_tensor_tensor(out=hot, in0=run, scalar=1.0, in1=eq, op0=ALU.is_equal, op1=ALU.mult))

                ones4 = scan_keep[:, 1:5]
                first_max(rt[:, :, 0:4], r_(0), r_(3), r_(4), r_(5))
                link(v.tensor_tensor(r_(1), rt[:, :, 0:4], bc(r_(0)[:, :, 0:1], [P, TB, 4]), ALU.subtract))
                for tb in range(TB):
                    link(v.tensor_tensor(rxx[:, tb], rt[:, tb, 4:20].rearrange("p (g e) -> p g e", g=4),
                                         bc(r_(5)[:, tb, :].unsqueeze(2), [P, 4, 4]), ALU.mult))
                link(v.tensor_tensor(rxx[:, :, 0:2, :], rxx[:, :, 0:2, :], rxx[:, :, 2:4, :], ALU.add))
                link(v.tensor_tensor(r_(8), rxx[:, :, 0, :], rxx[:, :, 1, :], ALU.add))
                first_max(r_(8), r_(0), r_(3), r_(4), r_(9))
                link(v.tensor_tensor(r_(6), r_(8), bc(r_(0)[:, :, 0:1], [P, TB, 4]), ALU.subtract))
                dve.sem_inc(sem("rt_x1"), 1)
                link(v.scalar_tensor_tensor(out=r_(8), in0=r_(9), scalar=NEG, in1=r_(8), op0=ALU.mult, op1=ALU.add))
                first_max(r_(8), r_(0), r_(3), r_(4), r_(10))
                dve.wait_ge(sem("rt_x2"), l * PER["rt_x2"] + 1)
                link(v.tensor_tensor(r_(9), r_(9), r_(10), ALU.add))
                link(v.tensor_tensor(r_(7), r_(7), r_(9), ALU.mult))
                link(v.tensor_reduce(r_(0)[:, :, 0], r_(7), AX, ALU.add))
                link(v.tensor_reduce(r_(0)[:, :, 1], r_(2), AX, ALU.add))
                link(v.tensor_tensor(r_(0)[:, :, 2], r_(0)[:, :, 0], r_(0)[:, :, 1], ALU.mult))
                link(v.reciprocal(r_(0)[:, :, 3], r_(0)[:, :, 2]))
                link(v.tensor_tensor(r_(7), r_(7), bc(r_(0)[:, :, 3:4], [P, TB, 4]), ALU.mult))
                for tb in range(TB):
                    link(v.tensor_tensor(comb[:, tb], bc(r_(5)[:, tb, :].unsqueeze(2), [P, 4, 4]),
                                         bc(r_(7)[:, tb, :].unsqueeze(1), [P, 4, 4]), ALU.mult))
                combf = comb[:].rearrange("p t g e -> p t (g e)")
                for tb in range(TB):
                    ins = v.tensor_tensor(sel[:, tb], bc(r_(5)[:, tb, :].unsqueeze(2), [P, 4, 4]),
                                          bc(r_(9)[:, tb, :].unsqueeze(1), [P, 4, 4]), ALU.mult)
                ins.then_inc(sem("hs"), 1)
                dve.wait_ge(sem("rank_mm"), l * PER["rank_mm"] + 1)
                self_ = sel[:].rearrange("p t g e -> p t (g e)")
                link(v.tensor_reduce(most[:, 0:1], bank[0][:, 32:48], AX, ALU.max))
                v.tensor_scalar(flag[:], most[:, 0:1], float(CAP), None, ALU.is_gt).then_inc(sem("flag"), 1)
                first_pass = place[:, :, 0:N_EXP]
                link(v.tensor_tensor(first_pass, bank[0][:, 0:32].rearrange("p (t n) -> p t n", t=2), self_, ALU.mult))
                link(v.tensor_scalar(first_pass, first_pass, 1.0, None, ALU.subtract))
                for p in range(1, PASSES):
                    v.tensor_scalar(place[:, :, p * N_EXP:p * N_EXP + N_EXP], first_pass, float(p * CAP), None, ALU.subtract)
                link(v.tensor_tensor(fold[:], ident[:, 0:CAP], ident[:, CAP:2 * CAP], ALU.add))

                def choose(p, e):
                    i = p * N_EXP + e
                    for tb in range(TB):
                        at = place[:, tb, i:i + 1] if isinstance(i, int) else place[:, tb, bass.ds(i, 1)]
                        ins = v.tensor_scalar(pick[:, tb], slot_no[:], at, None, ALU.is_equal)
                    ins.then_inc(sem("pick"), 1)

                def pieces(p, e, j):
                    for i in DVE_PIECES[j]:
                        n = 4 * j + i
                        dve.wait_ge(sem("w_hi"), turns_before("w_hi", l, p, e) + n + 1)
                        v.tensor_tensor(w_lo[:, n % RP, :], ring[:, e_slot[j], i * PIECE:i * PIECE + PIECE],
                                        w_hi[:, n % RP, :].bitcast(F32), ALU.subtract).then_inc(sem("w_lo"), 1)

                def gathered(p, e):
                    dve.wait_ge(sem("ga_hi"), turns_before("ga_hi", l, p, e) + 1)
                    v.tensor_tensor(ga[:, :, 1, :], bank[0][:].rearrange("p (k c) -> p k c", c=CAP),
                                    ga[:, :, 0, :].bitcast(F32), ALU.subtract).then_inc(sem("ga_lo"), 1)

                def accumulate(p, e):
                    for n in range(4):
                        nh, tb = n // 2, n % 2
                        dve.wait_ge(sem("sc_mm"), turns_before("sc_mm", l, p, e) + n + 1)
                        xv = x[:, tb, nh * 512:nh * 512 + 512]
                        w = combf[:, tb, bass.ds(e, 1)] if not isinstance(e, int) else combf[:, tb, e:e + 1]
                        v.scalar_tensor_tensor(out=xv, in0=bank[SC_BANKS[n]][:], scalar=w, in1=xv,
                                               op0=ALU.mult, op1=ALU.add).then_inc(sem("x_acc"), 1)

                def turn(p, e, first=False, last=False):
                    pieces(p, e, 1)
                    if not first:
                        accumulate(p, e - 1)
                    if not last:
                        dve.wait_ge(sem("pickT_mm"), turns_before("pickT_mm", l, p, e) + 1)
                        choose(p, e + 1)
                    pieces(p, e, 2)
                    dve.wait_ge(sem("act_gate"), turns_before("act_gate", l, p, e) + 1)
                    dve.wait_ge(sem("guT_mm"), turns_before("guT_mm", l, p, e) + 2)
                    v.tensor_tensor(hid[:].rearrange("p a b -> p (a b)"), act_g[:].rearrange("p a b -> p (a b)"),
                                    bank[2][:, 0:4 * CAP], ALU.mult).then_inc(sem("hid"), 1)
                    dve.wait_ge(sem("hidT_hi"), turns_before("hidT_hi", l, p, e) + 1)
                    v.tensor_tensor(hidT[:, :, 1, :], hid[:], hidT[:, :, 0, :].bitcast(F32),
                                    ALU.subtract).then_inc(sem("hidT_lo"), 1)
                    if not last:
                        gathered(p, e + 1)
                        pieces(p, e + 1, 0)
                    for nh in range(2):
                        c = slice(nh * 512, nh * 512 + 512)
                        dve.wait_ge(sem("y_hi"), turns_before("y_hi", l, p, e) + nh + 1)
                        v.tensor_tensor(y_lo[:, c], bank[5 + nh][:], y_hi[:, c].bitcast(F32),
                                        ALU.subtract).then_inc(sem("y_lo"), 1)
                    if last:
                        accumulate(p, e)

                def one_pass(p):
                    choose(p, 0)
                    pieces(p, 0, 0)
                    gathered(p, 0)
                    q.turns(p, turn)

                one_pass(0)
                dve.wait_ge(sem("flag"), l + 1)
                more = q.more_passes()
                with dve.If(more):
                    with dve.Fori(1, PASSES) as p:
                        one_pass(p)
                with dve.Else():
                    dve.wait_ge(sem("w_lo"), turns_before("w_lo", l, 1, 0))
                    dve.sem_inc(sem("w_lo"), skipped("w_lo"))
                    dve.wait_ge(sem("pick"), turns_before("pick", l, 1, 0))
                    dve.sem_inc(sem("pick"), skipped("pick"))
                    dve.wait_ge(sem("ga_lo"), turns_before("ga_lo", l, 1, 0))
                    dve.sem_inc(sem("ga_lo"), skipped("ga_lo"))
                    dve.wait_ge(sem("hid"), turns_before("hid", l, 1, 0))
                    dve.sem_inc(sem("hid"), skipped("hid"))
                    dve.wait_ge(sem("hidT_lo"), turns_before("hidT_lo", l, 1, 0))
                    dve.sem_inc(sem("hidT_lo"), skipped("hidT_lo"))
                    dve.wait_ge(sem("y_lo"), turns_before("y_lo", l, 1, 0))
                    dve.sem_inc(sem("y_lo"), skipped("y_lo"))
                    dve.wait_ge(sem("x_acc"), turns_before("x_acc", l, 1, 0))
                    dve.sem_inc(sem("x_acc"), skipped("x_acc"))
                dve.wait_ge(sem("x_acc"), l * (PASSES * N_EXP * 4) + PASSES * N_EXP * 4)
                dve.sem_inc(sem("ffn_done"), 1)
                q.leave()
            dve.wait_ge(sem("ends_sumsq"), 4)
            v.tensor_scalar(st[:, 1, :], st[:, 0, :], 1.0 / D, EPS, ALU.mult, ALU.add).then_inc(sem("ends_meansq"), 1)
            dve.wait_ge(sem("ends_root"), 2)
            link(v.reciprocal(st[:, 3, :], st[:, 2, :]))
            dve.wait_ge(sem("go_loaded"), 16)
            for tb in range(TB):
                v.scalar_tensor_tensor(out=h[:, tb, :], in0=x[:, tb, :], scalar=st[:, 3, tb:tb + 1], in1=g_out,
                                       op0=ALU.mult, op1=ALU.mult).then_inc(sem("out_ready"), 1)


_INS = ['x', 'mem', 'positions', 'norm_mix', 'w_in', 'conv_w', 'conv_b', 'gla_a_up', 'gla_a_b', 'gla_norm',
        's5_lambda_re', 's5_lambda_im', 's5_log_dt', 's5_b_re', 's5_b_im', 's5_c_re', 's5_c_im', 's5_d',
        's5_w_glu', 's5_b_glu', 'w_branch', 'w_out', 'norm_cross', 'w_cq', 'w_ckv', 'w_co', 'norm_ffn',
        'w_route_group', 'b_route_group', 'w_route_expert', 'b_route_expert', 'w_e_gate', 'w_e_up',
        'w_e_down', 'norm_mem', 'norm_final']


def kernel(**inputs):
    import concourse.bacc as _bacc
    from concourse.bass_utils import run_bass_kernel_spmd as _run

    nc = _bacc.Bacc("TRN2", target_bir_lowering=False, num_devices=1)
    arrays, T = {}, {}
    for name in _INS:
        a = np.ascontiguousarray(inputs[name])
        arrays["in_" + name] = a
        T[name] = nc.dram_tensor("in_" + name, a.shape, mybir.dt.from_np(a.dtype), kind="ExternalInput").ap()
    out = nc.dram_tensor("out", (1, S, D), F32, kind="ExternalOutput").ap()
    trunk(nc, T, out)
    r = _run(nc, [arrays], core_ids=[0])
    return r.results[0]["out"]
```
